# Optimizing a Trainium2 kernel written in Bass

```python
import jax
import jax.numpy as jnp
from jax import lax
import numpy as np
import jax, jax.numpy as jnp

D_MODEL = 1024
BATCH = 1
SEQ = 256
DEPTH = 1

GRID_W = 64
CTX_LEN = 256
EPS = 1e-6
MLA_HEADS = 8
MLA_NOPE = 64
MLA_ROPE = 32
MLA_V_HEAD = 64
MLA_Q_LORA = 384
MLA_KV_LORA = 256
MLA_WIDTH = MLA_HEADS * MLA_V_HEAD
MLA_SCALE = (MLA_NOPE + MLA_ROPE) ** -0.5
ROPE_AXIS_DIM = MLA_ROPE // 2
ROPE_THETA = 10000.0
Q_BLOCK = 128
GLA_HEADS = 4
GLA_HEAD_K = 128
GLA_HEAD_V = 128
GLA_KEY = GLA_HEADS * GLA_HEAD_K
GLA_VALUE = GLA_HEADS * GLA_HEAD_V
GLA_QSCALE = GLA_HEAD_K ** -0.5
GATE_RANK = 16
GATE_NORM = 16.0
GLA_CHUNK = 64
D_FF = 2816
CONV_W = 3
IN_SPLITS = (MLA_Q_LORA, MLA_KV_LORA, MLA_ROPE, GLA_KEY, GLA_KEY, GLA_VALUE, GLA_VALUE, 2 * GATE_RANK, 2 * D_MODEL)
IN_COLS = sum(IN_SPLITS)


def rms_norm(x, g):
    xf = x.astype(jnp.float32)
    y = xf * lax.rsqrt(jnp.mean(xf * xf, axis=-1, keepdims=True) + EPS)
    return (y * g.astype(jnp.float32)).astype(x.dtype)

def modulate(h, shift, scale):
    return h * (1 + scale) + shift

def split_columns(z):
    offsets = [int(o) for o in np.cumsum(IN_SPLITS)[:-1]]
    return jnp.split(z, offsets, axis=-1)

def heads(z, n_heads):
    return z.reshape(z.shape[:-1] + (n_heads, z.shape[-1] // n_heads))

def axial_angles(length):
    t = jnp.arange(length, dtype=jnp.int32)
    row = (t // GRID_W).astype(jnp.float32)
    col = (t % GRID_W).astype(jnp.float32)
    inv_freq = ROPE_THETA ** (-jnp.arange(0, ROPE_AXIS_DIM, 2, dtype=jnp.float32) / ROPE_AXIS_DIM)
    return row[:, None] * inv_freq, col[:, None] * inv_freq

def rotate_axis(x, ang):
    x1, x2 = jnp.split(x, 2, axis=-1)
    cos, sin = jnp.cos(ang), jnp.sin(ang)
    return jnp.concatenate([x1 * cos - x2 * sin, x2 * cos + x1 * sin], axis=-1)

def rope_2d(x, ang_row, ang_col):
    xf = x.astype(jnp.float32)
    xr, xc = xf[..., :ROPE_AXIS_DIM], xf[..., ROPE_AXIS_DIM:]
    return jnp.concatenate([rotate_axis(xr, ang_row), rotate_axis(xc, ang_col)], axis=-1).astype(x.dtype)

def mla_queries(q_c, q_norm_g, w_uq):
    q = heads(rms_norm(q_c, q_norm_g) @ w_uq, MLA_HEADS)
    return q[..., :MLA_NOPE], q[..., MLA_NOPE:]

def mla_keys_values(kv_c, kv_norm_g, w_ukv):
    kv = heads(rms_norm(kv_c, kv_norm_g) @ w_ukv, MLA_HEADS)
    return kv[..., :MLA_NOPE], kv[..., MLA_NOPE:]

def attention(q_nope, q_rope, k_nope, k_rope, v):
    b, lq = q_nope.shape[:2]
    nb = lq // Q_BLOCK

    def blocks(z):
        return jnp.moveaxis(z.reshape((b, nb, Q_BLOCK) + z.shape[2:]), 1, 0)

    def one_block(qs):
        qn, qr = qs
        s = jnp.einsum('bqhd,bkhd->bhqk', qn, k_nope) + jnp.einsum('bqhr,bkr->bhqk', qr, k_rope)
        p = jax.nn.softmax(s.astype(jnp.float32) * MLA_SCALE, axis=-1).astype(v.dtype)
        return jnp.einsum('bhqk,bkhd->bqhd', p, v)

    o = lax.map(one_block, (blocks(q_nope), blocks(q_rope)))
    return jnp.moveaxis(o, 0, 1).reshape(b, lq, MLA_WIDTH)

def to_chunks(z):
    b, l, h, d = z.shape
    return z.reshape(b, l // GLA_CHUNK, GLA_CHUNK, h, d).transpose(0, 3, 1, 2, 4)

def from_chunks(z):
    b, h, n, c, d = z.shape
    return z.transpose(0, 2, 3, 1, 4).reshape(b, n * c, h, d)

def chunk_state_terms(kc, vc, b_cum):
    b_last = b_cum[..., -1:, :]
    u = jnp.einsum('bhncd,bhncv->bhndv', kc * jnp.exp(b_last - b_cum), vc)
    decay = jnp.exp(b_last[..., 0, :])
    return decay, u

def scan_states(decay, u, s0):
    def step(s, inp):
        d, du = inp
        return d[..., None] * s + du, s

    s_final, s_in = lax.scan(step, s0, (jnp.moveaxis(decay, 2, 0), jnp.moveaxis(u, 2, 0)))
    return s_final, jnp.moveaxis(s_in, 0, 2)

def gla_direction(q, k, v, g, s0):
    qc, kc, vc = (to_chunks(z.astype(jnp.float32)) for z in (q, k, v))
    b_cum = jnp.cumsum(to_chunks(g), axis=3)
    decay, u = chunk_state_terms(kc, vc, b_cum)
    s_final, s_in = scan_states(decay, u, s0)
    qe = qc * jnp.exp(b_cum)
    mask = jnp.tril(jnp.ones((GLA_CHUNK, GLA_CHUNK), jnp.float32))
    a = jnp.einsum('bhncd,bhnsd->bhncs', qe, kc * jnp.exp(-b_cum)) * mask
    o = jnp.einsum('bhncs,bhnsv->bhncv', a, vc) + jnp.einsum('bhncd,bhndv->bhncv', qe, s_in)
    return from_chunks(o), s_final

def gla_final_state(k, v, g, s0):
    kc, vc = to_chunks(k.astype(jnp.float32)), to_chunks(v.astype(jnp.float32))
    decay, u = chunk_state_terms(kc, vc, jnp.cumsum(to_chunks(g), axis=3))
    s_final, _ = scan_states(decay, u, s0)
    return s_final

def flip(z):
    return jnp.flip(z, axis=1)

def gla_bidirectional(q, k, v, g_f, g_b, s_f, s_b):
    o_f, s_f_out = gla_direction(q, k, v, g_f, s_f)
    o_b, s_b_out = gla_direction(flip(q), flip(k), flip(v), flip(g_b), s_b)
    return o_f + flip(o_b), s_f_out, s_b_out

def gla_inputs(gq, gk, gv, glow, w_decay, b_decay):
    lf, lb = glow[..., :GATE_RANK], glow[..., GATE_RANK:]
    g_f = jax.nn.log_sigmoid((lf @ w_decay[0] + b_decay[0]).astype(jnp.float32)) / GATE_NORM
    g_b = jax.nn.log_sigmoid((lb @ w_decay[1] + b_decay[1]).astype(jnp.float32)) / GATE_NORM
    return (heads(gq, GLA_HEADS) * GLA_QSCALE, heads(gk, GLA_HEADS), heads(gv, GLA_HEADS),
            heads(g_f, GLA_HEADS), heads(g_b, GLA_HEADS))

def gla_branch(o, r, norm_g, w_br):
    y = rms_norm(o, norm_g).reshape(o.shape[0], o.shape[1], GLA_VALUE).astype(r.dtype) * jax.nn.silu(r)
    return y @ w_br

def merge_branches(br_mla, br_gla, gate_logits, w_out):
    g = jax.nn.sigmoid(gate_logits.astype(jnp.float32)).astype(br_mla.dtype)
    g_mla, g_gla = jnp.split(g, 2, axis=-1)
    return (g_mla * br_mla + g_gla * br_gla) @ w_out

def token_mixer(h, hc, w_in, q_norm_g, w_uq, kv_norm_g, w_ukv, w_decay, b_decay, gla_norm_g,
                w_br_mla, w_br_gla, w_out, ang_row, ang_col, update_ctx):
    q_c, kv_c, k_rope, gq, gk, gv, gr, glow, gate_logits = split_columns(h @ w_in)
    q_cc, kv_cc, k_rope_c, gq_c, gk_c, gv_c, gr_c, glow_c, gate_logits_c = split_columns(hc @ w_in)

    k_nope_c, v_c = mla_keys_values(kv_cc, kv_norm_g, w_ukv)
    k_nope, v = mla_keys_values(kv_c, kv_norm_g, w_ukv)
    q_nope, q_rope = mla_queries(q_c, q_norm_g, w_uq)
    q_rope = rope_2d(q_rope, ang_row[:, None, :], ang_col[:, None, :])
    k_rope = rope_2d(k_rope, ang_row, ang_col)
    o_mla = attention(q_nope, q_rope,
                      jnp.concatenate([k_nope, k_nope_c], axis=1),
                      jnp.concatenate([k_rope, k_rope_c], axis=1),
                      jnp.concatenate([v, v_c], axis=1))

    b = h.shape[0]
    s0 = jnp.zeros((b, GLA_HEADS, GLA_HEAD_K, GLA_HEAD_V), jnp.float32)
    qg_c, kg_c, vg_c, gf_c, gb_c = gla_inputs(gq_c, gk_c, gv_c, glow_c, w_decay, b_decay)
    qg, kg, vg, gf, gb = gla_inputs(gq, gk, gv, glow, w_decay, b_decay)
    if update_ctx:
        o_gla_c, s_f, s_b = gla_bidirectional(qg_c, kg_c, vg_c, gf_c, gb_c, s0, s0)
    else:
        s_f = gla_final_state(kg_c, vg_c, gf_c, s0)
        s_b = gla_final_state(flip(kg_c), flip(vg_c), flip(gb_c), s0)
    o_gla, _, _ = gla_bidirectional(qg, kg, vg, gf, gb, s_f, s_b)

    out_lat = merge_branches(o_mla @ w_br_mla, gla_branch(o_gla, gr, gla_norm_g, w_br_gla), gate_logits, w_out)
    out_ctx = None
    if update_ctx:
        q_nope_c, q_rope_c = mla_queries(q_cc, q_norm_g, w_uq)
        o_mla_c = attention(q_nope_c, q_rope_c, k_nope_c, k_rope_c, v_c)
        out_ctx = merge_branches(o_mla_c @ w_br_mla, gla_branch(o_gla_c, gr_c, gla_norm_g, w_br_gla),
                                 gate_logits_c, w_out)
    return out_lat, out_ctx

def depthwise_conv_grid(u, w, bias, rows, cols):
    b, l, ch = u.shape
    grid = u.reshape(b, rows, cols, ch)
    y = lax.conv_general_dilated(grid, w[:, :, None, :].astype(u.dtype), (1, 1), 'SAME',
                                 dimension_numbers=('NHWC', 'HWIO', 'NHWC'), feature_group_count=ch)
    return y.reshape(b, l, ch) + bias

def conv_ffn(h, w_up, conv_w, conv_b, w_down, rows, cols):
    val, gate = jnp.split(h @ w_up, 2, axis=-1)
    gate = depthwise_conv_grid(gate, conv_w, conv_b, rows, cols)
    return (jax.nn.gelu(gate, approximate=False) * val) @ w_down

def first_inputs(seed: int = 0) -> dict:
    key = jax.random.key(seed)
    ks = jax.random.split(key, 24)
    f32 = jnp.float32

    def normal(k, shape, s=1.0):
        return s * jax.random.normal(k, shape, f32)

    def dense(k, shape, fan_in, gain=1.0):
        return normal(k, shape, gain * fan_in ** -0.5)

    def norm_gain(k, shape):
        return 1.0 + normal(k, shape, 0.05)

    return {
        "x": normal(ks[0], (BATCH, SEQ, D_MODEL)),
        "c": normal(ks[1], (BATCH, D_MODEL)),
        "ctx": normal(ks[2], (BATCH, CTX_LEN, D_MODEL)),
        "c_ctx": normal(ks[3], (D_MODEL,)),
        "w_ada": dense(ks[4], (DEPTH, D_MODEL, 6 * D_MODEL), D_MODEL, 0.5),
        "b_ada": normal(ks[5], (DEPTH, 6 * D_MODEL), 0.01),
        "norm1_g": norm_gain(ks[6], (DEPTH, D_MODEL)),
        "w_in": dense(ks[7], (DEPTH, D_MODEL, IN_COLS), D_MODEL),
        "q_norm_g": norm_gain(ks[8], (DEPTH, MLA_Q_LORA)),
        "w_uq": dense(ks[9], (DEPTH, MLA_Q_LORA, MLA_HEADS * (MLA_NOPE + MLA_ROPE)), MLA_Q_LORA),
        "kv_norm_g": norm_gain(ks[10], (DEPTH, MLA_KV_LORA)),
        "w_ukv": dense(ks[11], (DEPTH, MLA_KV_LORA, MLA_HEADS * (MLA_NOPE + MLA_V_HEAD)), MLA_KV_LORA),
        "gla_w_decay": dense(ks[12], (DEPTH, 2, GATE_RANK, GLA_KEY), GATE_RANK),
        "gla_b_decay": normal(ks[13], (DEPTH, 2, GLA_KEY), 0.1),
        "gla_norm_g": norm_gain(ks[14], (DEPTH, GLA_HEAD_V)),
        "w_br_mla": dense(ks[15], (DEPTH, MLA_WIDTH, D_MODEL), MLA_WIDTH),
        "w_br_gla": dense(ks[16], (DEPTH, GLA_VALUE, D_MODEL), GLA_VALUE),
        "w_out": dense(ks[17], (DEPTH, D_MODEL, D_MODEL), D_MODEL),
        "norm2_g": norm_gain(ks[18], (DEPTH, D_MODEL)),
        "w_up": dense(ks[19], (DEPTH, D_MODEL, 2 * D_FF), D_MODEL),
        "conv_w": dense(ks[20], (DEPTH, CONV_W, CONV_W, D_FF), CONV_W * CONV_W),
        "conv_b": normal(ks[21], (DEPTH, D_FF), 0.01),
        "w_down": dense(ks[22], (DEPTH, D_FF, D_MODEL), D_FF),
        "final_g": norm_gain(ks[23], (D_MODEL,)),
    }

def first_block(x, c, ctx, c_ctx, w_ada, b_ada, norm1_g, w_in, q_norm_g, w_uq, kv_norm_g, w_ukv,
              gla_w_decay, gla_b_decay, gla_norm_g, w_br_mla, w_br_gla, w_out, norm2_g, w_up,
              conv_w, conv_b, w_down, final_g):
    length = x.shape[1]
    rows = length // GRID_W
    ang_row, ang_col = axial_angles(length)
    x_lat, x_ctx = x, ctx
    for layer in range(DEPTH):
        update_ctx = layer + 1 < DEPTH
        mod = jax.nn.silu(c) @ w_ada[layer] + b_ada[layer]
        mod_c = jax.nn.silu(c_ctx) @ w_ada[layer] + b_ada[layer]
        sh1, sc1, gt1, sh2, sc2, gt2 = jnp.split(mod[:, None, :], 6, axis=-1)
        sh1c, sc1c, gt1c, sh2c, sc2c, gt2c = jnp.split(mod_c, 6, axis=-1)

        h = modulate(rms_norm(x_lat, norm1_g[layer]), sh1, sc1)
        hc = modulate(rms_norm(x_ctx, norm1_g[layer]), sh1c, sc1c)
        mix, mix_c = token_mixer(h, hc, w_in[layer], q_norm_g[layer], w_uq[layer], kv_norm_g[layer],
                                 w_ukv[layer], gla_w_decay[layer], gla_b_decay[layer], gla_norm_g[layer],
                                 w_br_mla[layer], w_br_gla[layer], w_out[layer], ang_row, ang_col, update_ctx)
        x_lat = x_lat + gt1 * mix
        h = modulate(rms_norm(x_lat, norm2_g[layer]), sh2, sc2)
        x_lat = x_lat + gt2 * conv_ffn(h, w_up[layer], conv_w[layer], conv_b[layer], w_down[layer], rows, GRID_W)
        if update_ctx:
            x_ctx = x_ctx + gt1c * mix_c
            hc = modulate(rms_norm(x_ctx, norm2_g[layer]), sh2c, sc2c)
            x_ctx = x_ctx + gt2c * conv_ffn(hc, w_up[layer], conv_w[layer], conv_b[layer], w_down[layer],
                                            1, x_ctx.shape[1])
    return rms_norm(x_lat, final_g)


DEPTH_2 = 2

A_HEADS = 8
A_KV_HEADS = 2
A_HEAD_DIM = 64
B_HEADS = 4
B_HEAD_DIM = 128
B_CHUNK = 128
B_CONV = 3
POOL_WINDOWS = (2, 4, 8, 16)
POOL_GROUP = D_MODEL // 4
N_EXPERTS = 16
EC_FACTOR = 2
D_EXPERT = 1024
NORM_EPS = 1e-6

A_Q = A_HEADS * A_HEAD_DIM
A_KV = A_KV_HEADS * A_HEAD_DIM
B_W = B_HEADS * B_HEAD_DIM
N_GATES = 2 * 2 * B_HEADS
EVEN_IN = A_Q + 2 * A_KV + 4 * B_W + N_GATES
MIX_W = A_Q + B_W
EVEN_SPLITS = (A_Q, A_Q + A_KV, A_Q + 2 * A_KV, A_Q + 2 * A_KV + B_W, A_Q + 2 * A_KV + 2 * B_W,
               A_Q + 2 * A_KV + 3 * B_W, A_Q + 2 * A_KV + 4 * B_W)
N_EVEN = (DEPTH_2 + 1) // 2
N_ODD = DEPTH_2 // 2


def rmsnorm(x, g):
    xf = x.astype(jnp.float32)
    y = xf * lax.rsqrt(jnp.mean(xf * xf, axis=-1, keepdims=True) + NORM_EPS)
    return (y * g.astype(jnp.float32)).astype(x.dtype)

def adaln(cond, w, b):
    m = jax.nn.silu(cond) @ w + b
    return m.reshape(cond.shape[:-1] + (1, 6, D_MODEL))

def modulate_2(x, g, shift, scale):
    return rmsnorm(x, g) * (1 + scale) + shift

def axial_rope(n_tokens):
    rows = n_tokens // GRID_W
    row_ids = jnp.repeat(jnp.arange(rows, dtype=jnp.float32), GRID_W)
    col_ids = jnp.tile(jnp.arange(GRID_W, dtype=jnp.float32), rows)
    half = A_HEAD_DIM // 2
    inv = ROPE_THETA ** (-jnp.arange(0, half, 2, dtype=jnp.float32) / half)
    ang = jnp.stack([row_ids[:, None] * inv, col_ids[:, None] * inv], axis=1)
    return jnp.cos(ang), jnp.sin(ang)

def apply_rope(x, cos, sin):
    Bn, n, H, d = x.shape
    xr = x.reshape(Bn, n, H, 2, 2, d // 4)
    x1, x2 = xr[..., 0, :], xr[..., 1, :]
    c = cos[None, :, None].astype(x.dtype)
    s = sin[None, :, None].astype(x.dtype)
    return jnp.stack([x1 * c - x2 * s, x2 * c + x1 * s], axis=-2).reshape(x.shape)

def attend_blocks(q, k, v):
    Bn, Lq, _, d = q.shape
    G = A_HEADS // A_KV_HEADS
    nb = Lq // Q_BLOCK
    qb = q.reshape(Bn, nb, Q_BLOCK, A_KV_HEADS, G, d).transpose(1, 0, 3, 4, 2, 5)
    kt = jnp.swapaxes(k, 1, 2)
    vt = jnp.swapaxes(v, 1, 2)
    scale = d ** -0.5

    def one_block(qblk):
        s = jnp.einsum('bhgtd,bhsd->bhgts', qblk, kt).astype(jnp.float32) * scale
        p = jax.nn.softmax(s, axis=-1).astype(vt.dtype)
        return jnp.einsum('bhgts,bhsd->bhgtd', p, vt)

    o = lax.map(one_block, qb)
    return o.transpose(1, 0, 4, 2, 3, 5).reshape(Bn, Lq, A_HEADS * d)

def short_conv(x, w):
    n = x.shape[1]
    pad = B_CONV // 2
    xp = jnp.pad(x, ((0, 0), (pad, B_CONV - 1 - pad), (0, 0)))
    return sum(xp[:, j:j + n] * w[j] for j in range(B_CONV))

def mlstm_zero_state(Bn):
    return (jnp.zeros((Bn, B_HEADS, B_HEAD_DIM, B_HEAD_DIM), jnp.float32),
            jnp.zeros((Bn, B_HEADS, B_HEAD_DIM), jnp.float32),
            jnp.full((Bn, B_HEADS), -1e30, jnp.float32))

def mlstm_scan(q, k, v, ig, lf, state):
    Bn, H, L, d = q.shape
    nc = L // B_CHUNK
    k = k * (d ** -0.5)

    def to_chunks(a):
        a = a.reshape(a.shape[:2] + (nc, B_CHUNK) + a.shape[3:])
        return jnp.moveaxis(a, 2, 0)

    tril = jnp.tril(jnp.ones((B_CHUNK, B_CHUNK), dtype=bool))

    def step(carry, inp):
        C, n, m = carry
        qc, kc, vc, ic, fc = inp
        b = jnp.cumsum(fc, axis=-1)
        log_d = jnp.where(tril, b[..., :, None] - b[..., None, :] + ic[..., None, :], -jnp.inf)
        log_inter = m[..., None] + b
        m_t = jnp.maximum(log_inter, jnp.max(log_d, axis=-1))
        w_intra = jnp.exp(log_d - m_t[..., None]) * jnp.einsum('bhtd,bhsd->bhts', qc, kc)
        w_inter = jnp.exp(log_inter - m_t)
        num = (w_inter[..., None] * jnp.einsum('bhed,bhtd->bhte', C, qc)
               + jnp.einsum('bhts,bhse->bhte', w_intra, vc))
        den = w_inter * jnp.einsum('bhd,bhtd->bht', n, qc) + jnp.sum(w_intra, axis=-1)
        h = num / jnp.maximum(jnp.abs(den), jnp.exp(-m_t))[..., None]
        b_end = b[..., -1]
        log_w = b_end[..., None] - b + ic
        m_new = jnp.maximum(m + b_end, jnp.max(log_w, axis=-1))
        w_s = jnp.exp(log_w - m_new[..., None])
        decay = jnp.exp(m + b_end - m_new)
        C = decay[..., None, None] * C + jnp.einsum('bhs,bhse,bhsd->bhed', w_s, vc, kc)
        n = decay[..., None] * n + jnp.einsum('bhs,bhsd->bhd', w_s, kc)
        return (C, n, m_new), h

    state, h = lax.scan(step, state, tuple(to_chunks(a) for a in (q, k, v, ig, lf)))
    h = jnp.moveaxis(h, 0, 2).reshape(Bn, H, L, d)
    return h, state

def mlstm_bidir(q, k, v, ig, lf, states):
    h_f, s_f = mlstm_scan(q, k, v, ig[0], lf[0], states[0])
    flip = lambda a: jnp.flip(a, axis=2)
    h_b, s_b = mlstm_scan(flip(q), flip(k), flip(v), flip(ig[1]), flip(lf[1]), states[1])
    return h_f + flip(h_b), (s_f, s_b)

def even_mixer(h_lat, h_ctx, ctx_out, w_in, w_out, g_qn, g_kn, w_conv, b_gate, g_hn):
    Bn, L, _ = h_lat.shape

    def project(h):
        n = h.shape[1]
        qa, ka, va, qb, kb, vb, ob, gt = jnp.split(h @ w_in, EVEN_SPLITS, axis=-1)
        qa = rmsnorm(qa.reshape(Bn, n, A_HEADS, A_HEAD_DIM), g_qn)
        ka = rmsnorm(ka.reshape(Bn, n, A_KV_HEADS, A_HEAD_DIM), g_kn)
        va = va.reshape(Bn, n, A_KV_HEADS, A_HEAD_DIM)
        qk = jax.nn.silu(short_conv(jnp.concatenate([qb, kb], axis=-1), w_conv))
        to_heads = lambda a: a.reshape(Bn, n, B_HEADS, B_HEAD_DIM).transpose(0, 2, 1, 3).astype(jnp.float32)
        qm, km, vm = to_heads(qk[..., :B_W]), to_heads(qk[..., B_W:]), to_heads(vb)
        g = (gt + b_gate).astype(jnp.float32).reshape(Bn, n, 2, 2, B_HEADS).transpose(2, 3, 0, 4, 1)
        ig = g[:, 0]
        lf = jax.nn.log_sigmoid(g[:, 1])
        return (qa, ka, va), (qm, km, vm, ig, lf), ob

    def mlstm_out(hm, ob):
        n = hm.shape[2]
        hm = rmsnorm(jnp.swapaxes(hm, 1, 2), g_hn.reshape(B_HEADS, B_HEAD_DIM))
        return hm.reshape(Bn, n, B_W).astype(ob.dtype) * jax.nn.sigmoid(ob)

    (qa_c, ka_c, va_c), mc, ob_c = project(h_ctx)
    (qa_l, ka_l, va_l), ml, ob_l = project(h_lat)
    cos, sin = axial_rope(L)
    qa_l = apply_rope(qa_l, cos, sin)
    ka_l = apply_rope(ka_l, cos, sin)
    o_a = attend_blocks(qa_l, jnp.concatenate([ka_c, ka_l], axis=1), jnp.concatenate([va_c, va_l], axis=1))
    st0 = mlstm_zero_state(Bn)
    h_c, ctx_states = mlstm_bidir(*mc, (st0, st0))
    h_l, _ = mlstm_bidir(*ml, ctx_states)
    y = jnp.concatenate([o_a, mlstm_out(h_l, ob_l)], axis=-1) @ w_out
    yc = None
    if ctx_out:
        yc = jnp.concatenate([attend_blocks(qa_c, ka_c, va_c), mlstm_out(h_c, ob_c)], axis=-1) @ w_out
    return y, yc

def pool_mixer(h, w_in, w_grp, s_pool):
    Bn, n, _ = h.shape
    u = h @ w_in
    uf = u.astype(jnp.float32)
    S = jnp.pad(jnp.cumsum(uf, axis=1), ((0, 0), (1, 0), (0, 0)))
    t = jnp.arange(n)
    outs = []
    for gi, w in enumerate(POOL_WINDOWS):
        lo = w // 2
        hi = w - 1 - lo
        a = jnp.clip(t - lo, 0, n - 1)
        e = jnp.clip(t + hi, 0, n - 1)
        Sg = S[:, :, gi * POOL_GROUP:(gi + 1) * POOL_GROUP]
        cnt = (e - a + 1).astype(jnp.float32)[None, :, None]
        outs.append((Sg[:, e + 1] - Sg[:, a]) / cnt - uf[:, :, gi * POOL_GROUP:(gi + 1) * POOL_GROUP])
    p = jnp.stack(outs, axis=2).astype(u.dtype)
    y = jnp.einsum('bngc,gce->bnge', p, w_grp).reshape(Bn, n, D_MODEL)
    return y * s_pool

def ec_moe(h, w_router, w_gate, w_up, w_down):
    Bn, n, Dm = h.shape
    cap = max(1, EC_FACTOR * n // N_EXPERTS)
    aff = jax.nn.softmax(jnp.einsum('bnd,de->bne', h, w_router).astype(jnp.float32), axis=-1)
    gate, idx = lax.top_k(jnp.swapaxes(aff, 1, 2), cap)
    xs = jax.vmap(lambda hb, ib: hb[ib])(h, idx)
    a = jax.nn.silu(jnp.einsum('becd,edf->becf', xs, w_gate)) * jnp.einsum('becd,edf->becf', xs, w_up)
    out = jnp.einsum('becf,efd->becd', a, w_down) * gate[..., None].astype(h.dtype)
    return jax.vmap(lambda ob, ib: jnp.zeros((n, Dm), ob.dtype).at[ib.reshape(-1)].add(ob.reshape(-1, Dm)))(out, idx)

def second_inputs(seed: int = 0) -> dict:
    key = jax.random.key(seed)
    ks = jax.random.split(key, 23)
    nrm = lambda k, shape, s: s * jax.random.normal(k, shape, jnp.float32)
    fb = jnp.linspace(3.0, 6.0, B_HEADS)
    gate_base = jnp.concatenate([jnp.zeros((B_HEADS,)), fb, jnp.zeros((B_HEADS,)), fb])
    return {
        "x": nrm(ks[0], (BATCH, SEQ, D_MODEL), 1.0),
        "c": nrm(ks[1], (BATCH, D_MODEL), 1.0),
        "ctx": nrm(ks[2], (BATCH, CTX_LEN, D_MODEL), 1.0),
        "c_ctx": nrm(ks[3], (D_MODEL,), 1.0),
        "w_mod": nrm(ks[4], (DEPTH_2, D_MODEL, 6 * D_MODEL), 0.5 * D_MODEL ** -0.5),
        "b_mod": nrm(ks[5], (DEPTH_2, 6 * D_MODEL), 0.02),
        "g_norm1": 1.0 + nrm(ks[6], (DEPTH_2, D_MODEL), 0.02),
        "g_norm2": 1.0 + nrm(ks[7], (DEPTH_2, D_MODEL), 0.02),
        "w_in_even": nrm(ks[8], (N_EVEN, D_MODEL, EVEN_IN), D_MODEL ** -0.5),
        "w_out_even": nrm(ks[9], (N_EVEN, MIX_W, D_MODEL), MIX_W ** -0.5),
        "g_qnorm": 1.0 + nrm(ks[10], (N_EVEN, A_HEAD_DIM), 0.02),
        "g_knorm": 1.0 + nrm(ks[11], (N_EVEN, A_HEAD_DIM), 0.02),
        "w_conv": nrm(ks[12], (N_EVEN, B_CONV, 2 * B_W), B_CONV ** -0.5),
        "b_gate": gate_base[None] + nrm(ks[13], (N_EVEN, N_GATES), 0.1),
        "g_hnorm": 1.0 + nrm(ks[14], (N_EVEN, B_W), 0.02),
        "w_in_odd": nrm(ks[15], (N_ODD, D_MODEL, D_MODEL), D_MODEL ** -0.5),
        "w_pool_grp": nrm(ks[16], (N_ODD, 4, POOL_GROUP, POOL_GROUP), POOL_GROUP ** -0.5),
        "s_pool": 1.0 + nrm(ks[17], (N_ODD, D_MODEL), 0.1),
        "w_router": nrm(ks[18], (DEPTH_2, D_MODEL, N_EXPERTS), D_MODEL ** -0.5),
        "w_exp_gate": nrm(ks[19], (DEPTH_2, N_EXPERTS, D_MODEL, D_EXPERT), D_MODEL ** -0.5),
        "w_exp_up": nrm(ks[20], (DEPTH_2, N_EXPERTS, D_MODEL, D_EXPERT), D_MODEL ** -0.5),
        "w_exp_down": nrm(ks[21], (DEPTH_2, N_EXPERTS, D_EXPERT, D_MODEL), D_EXPERT ** -0.5),
        "g_final": 1.0 + nrm(ks[22], (D_MODEL,), 0.02),
    }

def second_block(x, c, ctx, c_ctx, w_mod, b_mod, g_norm1, g_norm2, w_in_even, w_out_even, g_qnorm, g_knorm,
              w_conv, b_gate, g_hnorm, w_in_odd, w_pool_grp, s_pool, w_router, w_exp_gate, w_exp_up,
              w_exp_down, g_final):
    xc = ctx
    for i in range(DEPTH_2):
        ctx_next = any(j % 2 == 0 for j in range(i + 1, DEPTH_2))
        ctx_used = (i % 2 == 0) or ctx_next
        m_lat = adaln(c, w_mod[i], b_mod[i])
        h = modulate_2(x, g_norm1[i], m_lat[..., 0, :], m_lat[..., 1, :])
        yc = None
        if ctx_used:
            m_ctx = adaln(c_ctx, w_mod[i], b_mod[i])
            hc = modulate_2(xc, g_norm1[i], m_ctx[..., 0, :], m_ctx[..., 1, :])
        if i % 2 == 0:
            e = i // 2
            y, yc = even_mixer(h, hc, ctx_next, w_in_even[e], w_out_even[e], g_qnorm[e], g_knorm[e],
                               w_conv[e], b_gate[e], g_hnorm[e])
        else:
            o = i // 2
            y = pool_mixer(h, w_in_odd[o], w_pool_grp[o], s_pool[o])
            if ctx_next:
                yc = pool_mixer(hc, w_in_odd[o], w_pool_grp[o], s_pool[o])
        x = x + m_lat[..., 2, :] * y
        h = modulate_2(x, g_norm2[i], m_lat[..., 3, :], m_lat[..., 4, :])
        x = x + m_lat[..., 5, :] * ec_moe(h, w_router[i], w_exp_gate[i], w_exp_up[i], w_exp_down[i])
        if ctx_next:
            xc = xc + m_ctx[..., 2, :] * yc
            hc = modulate_2(xc, g_norm2[i], m_ctx[..., 3, :], m_ctx[..., 4, :])
            xc = xc + m_ctx[..., 5, :] * ec_moe(hc, w_router[i], w_exp_gate[i], w_exp_up[i], w_exp_down[i])
    return rmsnorm(x, g_final)


def setup_inputs(seed=0):
    out = dict(first_inputs(seed))
    for name, value in second_inputs(seed + 1).items():
        if name != "x":
            out[name + "_2"] = value
    return out


def reference(
    x, c, ctx, c_ctx, w_ada, b_ada, norm1_g, w_in, q_norm_g, w_uq, kv_norm_g, w_ukv,
    gla_w_decay, gla_b_decay, gla_norm_g, w_br_mla, w_br_gla, w_out, norm2_g, w_up, conv_w,
    conv_b, w_down, final_g, c_2, ctx_2, c_ctx_2, w_mod_2, b_mod_2, g_norm1_2, g_norm2_2,
    w_in_even_2, w_out_even_2, g_qnorm_2, g_knorm_2, w_conv_2, b_gate_2, g_hnorm_2, w_in_odd_2,
    w_pool_grp_2, s_pool_2, w_router_2, w_exp_gate_2, w_exp_up_2, w_exp_down_2, g_final_2,
):
    x = first_block(
        x, c, ctx, c_ctx, w_ada, b_ada, norm1_g, w_in, q_norm_g, w_uq, kv_norm_g, w_ukv,
        gla_w_decay, gla_b_decay, gla_norm_g, w_br_mla, w_br_gla, w_out, norm2_g, w_up, conv_w,
        conv_b, w_down, final_g,
    )
    return second_block(
        x, c_2, ctx_2, c_ctx_2, w_mod_2, b_mod_2, g_norm1_2, g_norm2_2, w_in_even_2,
        w_out_even_2, g_qnorm_2, g_knorm_2, w_conv_2, b_gate_2, g_hnorm_2, w_in_odd_2,
        w_pool_grp_2, s_pool_2, w_router_2, w_exp_gate_2, w_exp_up_2, w_exp_down_2, g_final_2,
    )


_drawn_inputs = setup_inputs


def setup_inputs(seed=0):
    import zlib

    import numpy as np

    out = dict(_drawn_inputs(seed))
    spreads = {}
    factors = {'b_ada': 4.678,
     'norm1_g': 4.34,
     'q_norm_g': 8.0,
     'w_uq': 3.431,
     'kv_norm_g': 8.0,
     'gla_w_decay': 3.027,
     'gla_b_decay': 7.829,
     'gla_norm_g': 8.0,
     'norm2_g': 3.23,
     'conv_b': 8.0,
     'g_norm1_2': 8.0,
     'g_norm2_2': 6.338,
     'g_qnorm_2': 8.0,
     'g_knorm_2': 8.0,
     'g_hnorm_2': 8.0,
     'g_final_2': 2.963}
    for name, (base, spread) in spreads.items():
        noise = np.random.default_rng([zlib.crc32(name.encode()), seed]).standard_normal(out[name].shape)
        drawn = base * np.exp(spread * noise) if base else spread * noise
        out[name] = jnp.asarray(drawn.astype(out[name].dtype))
    for name, factor in factors.items():
        out[name] = (out[name] * factor).astype(out[name].dtype)
    return out
```

```python
from contextlib import ExitStack

import numpy as np

import concourse.bass as bass
from concourse import mybir

F32 = mybir.dt.float32
ACT = mybir.ActivationFunctionType
ALU = mybir.AluOpType
AX = mybir.AxisListType

D = 1024
KD = D // 128
T = 256
TB = T // 128
GRID_W = 64
ROWS = T // GRID_W
EPS = 1e-6
Q_LORA, KV_LORA, ROPE = 384, 256, 32
MLA_H, NOPE, VH = 8, 64, 64
QH = NOPE + ROPE
GH = 4
GCH = 64
D_FF = 2816
KF = D_FF // 128
A_H, A_KV, A_D = 8, 2, 64
B_H = 4
N_EXP, CAP = 16, 32

IN_KV, IN_GQ, IN_GK, IN_GV, IN_GR, IN_LOW, IN_GATE = 384, 672, 1184, 1696, 2208, 2720, 2752
EV_KA, EV_QB, EV_VB, EV_OB, EV_GT = 512, 768, 1792, 2304, 2816

SLOTS = 6
SLOT = 4096
RING = 4


def shape_tables():
    s, t = np.arange(128)[:, None], np.arange(128)[None, :]
    same = (s // GCH) == (t // GCH)
    parts, at = [], {}

    def add(name, a):
        a = np.asarray(a, np.float32).reshape(128, -1)
        at[name] = (sum(p.shape[1] for p in parts), a.shape[1])
        parts.append(a)

    add("ident", s == t)
    add("ones", np.ones((128, 128)))
    add("upto64", same & (s <= t))
    add("from64", same & (s >= t))
    add("sum_upto64", (same & (s <= t)) / 16.0)
    add("sum_from64", (same & (s >= t)) / 16.0)
    add("sum_after64", (same & (s > t)) / 16.0)
    add("sum_before64", (same & (s < t)) / 16.0)
    add("upto128", s <= t)
    add("from128", s >= t)
    add("bar_later", np.where(t > s, -1e30, 0.0))
    add("bar_earlier", np.where(t < s, -1e30, 0.0))
    pick = np.zeros((128, 2, 4, 32), np.float32)
    for d in range(2):
        for tb in range(4):
            for c in range(2):
                pick[c * 64:(c + 1) * 64, d, tb, d * 8 + tb * 2 + c] = 1 / 16.0
    add("chunk_pick", pick)
    add("slot_numbers", np.broadcast_to(np.arange(CAP, dtype=np.float32), (128, CAP)))
    tok = np.arange(T).reshape(TB, 128)
    for name, dim in (("rope32", ROPE), ("rope64", A_D)):
        half = dim // 2
        inv = np.float32(10000.0) ** (-np.arange(0, half, 2, dtype=np.float32) / np.float32(half))
        ang = np.stack([(tok // GRID_W)[..., None] * inv, (tok % GRID_W)[..., None] * inv], 2).astype(np.float32)
        both = np.stack([np.cos(ang), np.sin(ang)], 1)
        add(name, both.transpose(2, 0, 1, 3, 4))
    return np.concatenate(parts, 1), at


def pool_table():
    m = np.zeros((T, 4, T), np.float32)
    for g, w in enumerate((2, 4, 8, 16)):
        lo, hi = w // 2, w - 1 - w // 2
        for t in range(T):
            a, e = max(t - lo, 0), min(t + hi, T - 1)
            m[a:e + 1, g, t] = 1.0 / (e - a + 1)
            m[t, g, t] -= 1.0
    return m.reshape(TB, 128, 4 * T)


class Groups:

    def __init__(self, banks, done, freed):
        self.banks, self.done, self.freed = banks, done, freed
        self.count, self.turns, self.number, self.bank, self.use, self.last_user = 0, [0, 0], {}, {}, {}, {}

    def open(self, pe, name, second=False):
        turn = self.turns[second]
        b, use = turn % RING + RING * second, turn // RING
        self.turns[second] += 1
        if use:
            pe.wait_ge(self.freed[b], use)
        self.bank[name], self.use[name] = b, use
        return self.banks[b]

    def close(self, ins, name):
        ins.then_inc(self.done, 1)
        self.count += 1
        self.number[name] = self.count

    def over(self, *items):
        for item in items:
            self.last_user[item] = self.count

    def take(self, eng, name):
        eng.wait_ge(self.done, self.number[name])
        return self.banks[self.bank[name]] if name in self.bank else None

    def drain(self, eng, b):
        uses = (self.turns[0] - b + RING - 1) // RING
        eng.wait_ge(self.freed[b], uses)

    def read(self, eng, name):
        eng.wait_ge(self.freed[self.bank[name]], self.use[name] + 1)

    def give(self, ins, name):
        ins.then_inc(self.freed[self.bank[name]], 1)


def weight_items(w):
    items = []

    def cols(key, a, c0, n, k=KD):
        items.append((key, [((0, k * n), k, a[0:k * 128, c0:c0 + n].rearrange("(k p) n -> p k n", p=128))]))

    def rows(key, a, r0, k, n=D):
        items.append((key, [((0, k * n), k, a[r0:r0 + k * 128, :].rearrange("(k p) n -> p k n", p=128))]))

    def mod(i):
        src = w["w_ada"][0] if i < 12 else w["w_mod_2"][0] if i < 24 else w["w_mod_2"][1]
        cols(("mod", i), src, (i % 12) * 512, 512)

    mods = iter(range(36))
    for _ in range(4):
        mod(next(mods))
    w_in = w["w_in"][0]
    cols("kvr", w_in, IN_KV, IN_GQ - IN_KV)
    cols("w_ukv", w["w_ukv"][0], 0, 1024, 2)
    cols("qc", w_in, 0, Q_LORA)
    cols("w_uq", w["w_uq"][0], 0, MLA_H * QH, 3)
    for j in range(MLA_H):
        mod(next(mods))
    for key, c0 in (("gk", IN_GK), ("gv", IN_GV), ("gq", IN_GQ), ("gr", IN_GR)):
        cols(key, w_in, c0, 512)
        mod(next(mods))
    cols("low", w_in, IN_LOW, 32)
    rows("w_br_mla", w["w_br_mla"][0], 0, 4)
    rows("w_br_gla", w["w_br_gla"][0], 0, 4)
    for g in range(2):
        cols(("gate_mla", g), w_in, IN_GATE + 512 * g, 512)
        cols(("gate_gla", g), w_in, IN_GATE + D + 512 * g, 512)
    for g in range(2):
        rows(("w_out", g), w["w_out"][0], 512 * g, 4)
    for g in range(6):
        n = min(512, D_FF - 512 * g)
        cols(("up_gate", g), w["w_up"][0], D_FF + 512 * g, n)
        cols(("up_val", g), w["w_up"][0], 512 * g, n)
        mod(next(mods))
    for g in range(6):
        rows(("down", g), w["w_down"][0], 512 * g, min(4, KF - 4 * g))
    even = w["w_in_even_2"][0]
    cols("e_k", even, EV_QB + 512, 512)
    cols("e_q", even, EV_QB, 512)
    cols("e_kv", even, EV_KA, 256)
    cols("e_gt", even, EV_GT, 16)
    cols("e_qa", even, 0, 512)
    cols("e_ob", even, EV_OB, 512)
    for j in range(A_H):
        mod(next(mods))
    cols("e_vb", even, EV_VB, 512)
    for i in mods:
        mod(i)
    for g in range(2):
        rows(("e_out", g), w["w_out_even_2"][0], 512 * g, 4)
    cols(("router", 0), w["w_router_2"][0], 0, N_EXP)
    between = []
    mine, items = items, between
    for g in range(2):
        cols(("o_in", g), w["w_in_odd_2"][0], 512 * g, 512)
    items.append(("pool", [((0, TB * 4 * T), TB, w["pool"].rearrange("b p n -> p b n"))]))
    groups = w["w_pool_grp_2"][0].rearrange("g c e -> (g c) e")
    cols("w_grp", groups, 0, 256)
    cols(("router", 1), w["w_router_2"][1], 0, N_EXP)
    return mine, between


def build(nc, w, consts, out):
    table, at = consts
    before, between = weight_items(w)
    ctx = ExitStack()
    with ctx:
        def sb(name, shape):
            return ctx.enter_context(nc.sbuf_tensor(name, shape, F32))[:]

        sems = {}

        def sem(name):
            if name not in sems:
                sems[name] = ctx.enter_context(nc.semaphore(name))
            return sems[name]

        ring = sb("ring", [128, SLOTS * SLOT])
        cst = sb("cst", [128, table.shape[1]])
        vcol = sb("vcol", [128, 512])
        modc = sb("modc", [128, 3 * 96])
        cond = sb("cond", [128, 2, KD, 32])
        mrow = sb("mrow", [128, 512])
        gain = sb("gain", [128, 8 * KD])
        rs = sb("rs", [128, T])
        xT = sb("xT", [128, KD, T])
        hT = sb("hT", [128, KD, 2 * T])
        small = sb("small", [128, 768])
        AR = 17536
        arena = sb("arena", [128, AR])
        bank = [ctx.enter_context(nc.psum_tensor(f"bank{i}", [128, 512], F32))[:, :] for i in range(8)]
        acc = bank[RING:]

        def c_(name, lo=0, n=None):
            a, k = at[name]
            return cst[:, a + lo:a + lo + (n or k)]

        ident, ones = c_("ident"), c_("ones")

        def ar(off, *shape):
            n = int(np.prod(shape))
            assert off + n <= AR, (off, shape)
            v = arena[:, off:off + n]
            if len(shape) == 2:
                v = v.rearrange("p (a b) -> p a b", a=shape[0])
            if len(shape) == 3:
                v = v.rearrange("p (a b c) -> p a b c", a=shape[0], b=shape[1])
            return v

        vat, tiles = {}, [0, 0, 0, 0]
        vparts = [[], [], [], []]
        for t, name, a in (
            (0, "b_ada", w["b_ada"][0]), (0, "n1", w["norm1_g"][0]), (0, "n2", w["norm2_g"][0]),
            (0, "qn", w["q_norm_g"][0]), (0, "kvn", w["kv_norm_g"][0]), (0, "glan", w["gla_norm_g"][0]),
            (0, "conv_b", w["conv_b"][0]), (0, "c", w["c"][0]), (0, "cc", w["c_ctx"]),
            (0, "s_pool", w["s_pool_2"][0]), (0, "hn", w["g_hnorm_2"][0]),
            (1, "b_mod", w["b_mod_2"]), (1, "c2", w["c_2"][0]), (1, "cc2", w["c_ctx_2"]), (1, "n1_2", w["g_norm1_2"]),
            (3, "w_conv", w["w_conv_2"][0]), (3, "n2_2", w["g_norm2_2"]), (3, "fin", w["final_g"]),
            (3, "fin2", w["g_final_2"]),
        ):
            flat = a if len(a.shape) == 1 else a.rearrange("a b -> (a b)")
            n = flat.shape[0] // 128
            if t == 3 and not tiles[3]:
                tiles[3] = 9 * KF - 128
            vat[name] = (t, tiles[t], n)
            vparts[t].append((tiles[t], flat.rearrange("(r c) -> r c", c=128)))
            tiles[t] += n
        taps = w["conv_w"][0].rearrange("a b (r c) -> (a b r) c", c=128)
        vparts[2].append((0, taps[0:128, :]))
        vparts[3].append((0, taps[128:9 * KF, :]))
        tiles[2] = 128
        n_vdma = sum(len(p) for p in vparts)

        def vc(name, lo=0, n=1):
            t, r, _ = vat[name]
            return vcol[:, 128 * t + r + lo:128 * t + r + lo + n]

        def tap(i, j):
            r = i * KF + j
            return vcol[:, 256 + r:257 + r]

        def mc(which, part, r=0, lo=0, n=KD):
            v = modc[:, 96 * which:96 * which + 96].rearrange("p (j r) -> p j r", r=2)
            return v[:, KD * part + lo:KD * part + lo + n, r]

        def gains(i):
            return gain[:, KD * i:KD * i + KD]

        x_tm = ar(0, 4, D)
        xcT = ar(4096, KD, T)
        vrow = ar(6144, 512)
        sq = ar(AR - 2048, KD, T)
        kvr = ar(0, 4, 288)
        qc = ar(1152, 2, Q_LORA)
        qcT = ar(1920, 3, T)
        kvT = ar(2688, 2, 512)
        q_tm = ar(3712, TB, MLA_H * QH)
        v_tm = ar(5248, 4, MLA_H * VH)
        kcat = ar(7296, 4, MLA_H * QH)
        qT = ar(10368, MLA_H, T)
        kT = ar(12416, MLA_H, 512)
        prob = ar(3712, 2, 512)
        probT = ar(7296, 2, 4 * T)
        o_mla = ar(16512, 4, T)
        gk = ar(0, 4, 512)
        gv = ar(2048, 4, 512)
        gq = ar(4096, 2, 512)
        grT = ar(5120, 4, T)
        gg = ar(6144, 4, 1024)
        gex = ar(10240, 2, 512)
        wdec = ar(11264, 1024)
        qeT = ar(11264, 2, 4 * T)
        keT = ar(13312, 2, 4 * T)
        low = ar(15360, 512)
        dtm = ar(15872, 512)
        st = [ar(15360, 2, 512), ar(10240, 2, 512)]
        atT = ar(0, 8, 128)
        atM = ar(1024, 2, 256)
        o_gla = ar(4096, 4, T)
        sqg = ar(11264, 2, 512)
        rtg = ar(13312, 2, 512)
        merged = ar(8192, KD, T)
        sig = ar(10240, 4, T)
        part = ar(11264, 2, T)
        ff = ar(0, KF, T)
        pad = ar(5632, 3, 6 * 66)
        gel = ar(7168, 3, T)
        e_oT = ar(0, 4, T)
        e_mT = ar(1024, 4, T)
        e_qa = ar(2048, TB, 512)
        e_kv = ar(3072, 4, 256)
        e_qT = ar(4096, A_H, T)
        e_kT = ar(6144, A_KV, 512)
        e_prob = ar(7168, 2, 512)
        e_probT = ar(8192, 2, 4 * T)
        raw = ar(10240, 3, 2 * 258)
        qk = ar(11840, KD, 512)
        e_ob = ar(15936, 4, T)
        v1 = ar(2048, 4, 4 * 130)
        cn = [ar(4128, 4, 258), ar(5160, 4, 258)]
        kw = ar(6192, 8, 128)
        ktm = ar(7216, 4, 512)
        dm = ar(9264, 8, 128)
        wm = ar(10288, 8, 128)
        h_e = ar(11312, 4, 128)
        h_tm = ar(0, TB, D)
        xsel = ar(2048, KD, 512)
        hot = ar(6144, TB, 512)
        gates = ar(7168, N_EXP, T)
        hotg = ar(11264, TB, 4 * 512)
        gu = ar(11264, 512)
        act_t = ar(11776, 8, CAP)
        sil = ar(12032, 8, CAP)
        dsb = ar(12288, 2, 512)
        xe = ar(15360, 2, KD * CAP)
        gsm = ar(16960, 576)
        xc2 = ar(8192, TB, D)
        xc2T = ar(10240, KD, T)
        u_tm = ar(0, TB, D)
        pT = ar(2048, KD, T)

        eps, one = small[:, 0:1], small[:, 1:2]
        junk = small[:, 384:768]
        nul = small[:, 2:4]
        m_gt = gsm[:, 0:64].rearrange("p (b c) -> p b c", b=4)
        m_lf, m_b, m_r, m_end, m_top, m_ln = (
            gsm[:, 64 + 32 * i:96 + 32 * i].rearrange("p (b c) -> p b c", b=4) for i in range(6))
        m_m = gsm[:, 256:288].rearrange("p (j c) -> p j c", j=4)
        m_mx = gsm[:, 288:296]
        m_x = gsm[:, 296:344].rearrange("p (i c) -> p i c", i=6)
        m_M, m_in, m_em, m_sum, m_nq, m_wr, m_den = (gsm[:, 344 + 8 * i:352 + 8 * i] for i in range(7))
        m_ss = gsm[:, 400:408]
        dmx = [hT[:, 2 * i:2 * i + 2, :].rearrange("p a b -> p (a b)").rearrange("p (c s) -> p c s", c=8)
               for i in range(2)]
        aff = small[:, 128:160].rearrange("p (b e) -> p b e", b=TB)
        mask_t = small[:, 160:192].rearrange("p (b e) -> p b e", b=TB)
        top8 = small[0:N_EXP, 192:200]
        turn_of = small[:, 200:232].rearrange("p (b e) -> p b e", b=TB)
        work, mask_e = ar(13824, T), ar(14080, T)
        gates_flat = ar(7168, N_EXP * T)
        moe_base = {}
        BLOCKS = ((2, 3, 0, 1), (3, 2, 1, 0))

        done, freed = sem("matmuls_done"), [sem(f"bank_read_{b}") for b in range(8)]
        G = Groups(bank, done, freed)
        slot_full = [sem(f"slot_full_{i}") for i in range(SLOTS)]
        place, sent, items_of = {}, [0] * SLOTS, {}

        def queue(items, first):
            for i, (key, pieces) in enumerate(items):
                sl = (first + i) % SLOTS
                sent[sl] += 16
                place[key] = (sl, sent[sl])
            return (first + len(items)) % SLOTS

        moe_first = [queue(before, 0), 0]
        moe_sent = [list(sent), None]
        per_expert = [32 if (s - moe_first[0]) % SLOTS < 4 else 16 for s in range(SLOTS)]
        for s in range(SLOTS):
            sent[s] += N_EXP * per_expert[s]
        moe_first[1] = queue(between, moe_first[0])
        moe_sent[1] = list(sent)

        def weights(pe, key):
            sl, count = place[key]
            pe.wait_ge(slot_full[sl], count)
            return ring[:, sl * SLOT:(sl + 1) * SLOT]

        def w3(v, k, n):
            return v[:, 0:k * n].rearrange("p (k n) -> p k n", k=k)

        block = ctx.enter_context(nc.Block())

        @block.tensor
        def _(pe):
            def chain(name, b, lhs, rhs, n):
                for k in range(n):
                    ins = pe.matmul(b, lhs(k), rhs(k), start=(k == 0), stop=(k == n - 1))
                G.close(ins, name)

            def turn(name, b, srcs):
                for j, src in enumerate(srcs):
                    p = src.shape[0]
                    m = src.shape[1]
                    ins = pe.transpose(b[0:m, j * p:j * p + p], src, ident[0:p, 0:p])
                G.close(ins, name)

            pending = []

            def mod_turn():
                i = pending.pop()
                b = G.open(pe, ("mod_t", i))
                G.read(pe, ("mod", i))
                turn(("mod_t", i), b, [mrow[:, j * 128:j * 128 + 128] for j in range(4)])

            def mod(i):
                x = w3(weights(pe, ("mod", i)), KD, 512)
                b = G.open(pe, ("mod", i))
                for half in range(2):
                    for q in range(4):
                        k = q + 4 * half
                        ins = pe.matmul(b[32 * q:32 * q + 32, :], cond[:, 0 if i < 12 else 1, k, :], x[:, k, :],
                                        start=(half == 0), stop=(half == 1), skip_group_check=True)
                G.close(ins, ("mod", i))
                G.over(("mod", i))
                if pending:
                    mod_turn()
                pending.append(i)

            def norm(c):
                b = G.open(pe, ("ms", c))
                for k in range(KD):
                    pe.wait_ge(sem("squares"), KD * c + k + 1)
                    ins = pe.matmul(b[:, 0:T], ones, sq[:, k, :], start=(k == 0), stop=(k == KD - 1))
                G.close(ins, ("ms", c))

            def normed(c, k=KD):
                pe.wait_ge(sem("normed"), KD * (c - (c > 3)) + k)

            def token_major(name, x, n, tb, c0=0):
                b = G.open(pe, (name, tb))
                chain((name, tb), b[:, 0:n], lambda k: hT[:, k, tb * 128:tb * 128 + 128],
                      lambda k: x[:, k, c0:c0 + n], KD)

            def attend(tag, heads, qt, kt, v, pr, fill):
                def scores(i):
                    b = G.open(pe, (tag, "s", i), second=True)
                    h, qb = i // 2, i % 2
                    G.close(pe.matmul(b, qt(h)[:, qb * 128:qb * 128 + 128], kt(h), start=True, stop=True),
                            (tag, "s", i))

                def output(hp):
                    b = G.open(pe, (tag, "o", hp), second=True)
                    for m in range(4):
                        G.read(pe, (tag, "pt", 4 * hp + m))
                    pt = (probT, e_probT)[tag == "gqa"]
                    for j in range(4):
                        for h2 in range(2):
                            ins = pe.matmul(b[64 * h2:64 * h2 + 64, 0:T], v(2 * hp + h2, j), pt[:, h2, j * T:j * T + T],
                                            start=(j == 0), stop=(j == 3), skip_group_check=True)
                    G.close(ins, (tag, "o", hp))

                scores(0)
                for i in range(2 * heads):
                    if i + 1 < 2 * heads:
                        scores(i + 1)
                    fill(i)
                    if i and i % 4 == 0:
                        output(i // 4 - 1)
                    b = G.open(pe, (tag, "pt", i))
                    pe.wait_ge(sem(tag + "_prob"), i + 1)
                    turn((tag, "pt", i), b, [pr[:, i % 2, j * 128:j * 128 + 128] for j in range(4)])
                output(heads // 2 - 1)

            pe.wait_ge(sem("tables_in"), 16)
            pe.wait_ge(sem("vectors_in"), 16 * n_vdma)
            b = G.open(pe, "vec")
            for t in range(4):
                n = tiles[t]
                ins = pe.transpose(b[:, 128 * t:128 * t + n], vrow[0:n, 128 * t:128 * t + 128], ident[0:n, 0:n])
            G.close(ins, "vec")
            pe.wait_ge(sem("x_in"), 32)
            for k in range(KD):
                b = G.open(pe, ("xt", k))
                turn(("xt", k), b, [x_tm[:, tb, k * 128:k * 128 + 128] for tb in range(4)])
            pe.wait_ge(sem("cond_ready"), 4)
            for i in range(4):
                mod(i)
            mod_turn()
            norm(0)
            norm(1)

            x = w3(weights(pe, "kvr"), KD, 288)
            for tb in range(4):
                if tb % 2 == 0:
                    normed(tb // 2)
                token_major("kvr", x, 288, tb)
            G.over("kvr")
            for j in range(2):
                b = G.open(pe, ("kvt", j))
                pe.wait_ge(sem("kv_norm"), 4)
                turn(("kvt", j), b, [kvr[:, tb, j * 128:j * 128 + 128] for tb in range(4)])
            x = w3(weights(pe, "w_ukv"), 2, 1024)
            for tb in range(4):
                for hf in range(2):
                    b = G.open(pe, ("kv", tb, hf))
                    for k in range(2):
                        G.read(pe, ("kvt", k))
                    chain(("kv", tb, hf), b, lambda k: kvT[:, k, tb * 128:tb * 128 + 128],
                          lambda k: x[:, k, hf * 512:hf * 512 + 512], 2)
            G.over("w_ukv")
            x = w3(weights(pe, "qc"), KD, Q_LORA)
            for tb in range(TB):
                token_major("qc", x, Q_LORA, tb)
            G.over("qc")
            pe.wait_ge(sem("k_rope"), 4)
            for tb in range(4):
                for hf in range(2):
                    G.read(pe, ("kv", tb, hf))
            for h in range(4):
                b = G.open(pe, ("kT", h))
                turn(("kT", h), b, [kcat[:, tb, h * QH:h * QH + QH] for tb in range(4)])
            for j in range(3):
                b = G.open(pe, ("qct", j))
                pe.wait_ge(sem("q_norm"), 2)
                turn(("qct", j), b, [qc[:, tb, j * 128:j * 128 + 128] for tb in range(TB)])
            x = w3(weights(pe, "w_uq"), 3, MLA_H * QH)
            for tb in range(TB):
                for hf in range(2):
                    b = G.open(pe, ("q", tb, hf))
                    for k in range(3):
                        G.read(pe, ("qct", k))
                    chain(("q", tb, hf), b[:, 0:384], lambda k: qcT[:, k, tb * 128:tb * 128 + 128],
                          lambda k: x[:, k, hf * 384:hf * 384 + 384], 3)
            G.over("w_uq")
            for h in range(4, MLA_H):
                b = G.open(pe, ("kT", h))
                turn(("kT", h), b, [kcat[:, tb, h * QH:h * QH + QH] for tb in range(4)])
            pe.wait_ge(sem("q_rope"), 2)
            for hp in range(4):
                b = G.open(pe, ("qT", hp))
                turn(("qT", hp), b, [q_tm[:, tb, h * QH:h * QH + QH] for h in (2 * hp, 2 * hp + 1) for tb in range(TB)])
            for h in range(MLA_H):
                G.read(pe, ("kT", h))
            for hp in range(4):
                G.read(pe, ("qT", hp))
            attend("mla", MLA_H, lambda h: qT[0:QH, h, :], lambda h: kT[0:QH, h, :],
                   lambda h, j: v_tm[:, j, h * VH:h * VH + VH], prob,
                   lambda i: mod(4 + i // 2) if i % 2 == 0 else None)

            for tag, n_tb in (("gk", 4), ("gv", 4), ("gq", 2)):
                x = w3(weights(pe, tag), KD, 512)
                for tb in range(n_tb):
                    token_major(tag, x, 512, tb)
                G.over(tag)
                mod({"gk": 12, "gv": 13, "gq": 14}[tag])
            x = w3(weights(pe, "gr"), KD, 512)
            for j in range(4):
                b = G.open(pe, ("gr", j))
                chain(("gr", j), b[:, 0:T], lambda k: x[:, k, j * 128:j * 128 + 128], lambda k: hT[:, k, 0:T], KD)
            G.over("gr")
            mod(15)
            mod_turn()
            x = w3(weights(pe, "low"), KD, 32)
            b = G.open(pe, "low")
            chain("low", b[0:32, :], lambda k: x[:, k, :], lambda k: hT[:, k, :], KD)
            G.over("low")
            pe.wait_ge(sem("decay_in"), 3 * 16)
            pe.wait_ge(sem("low_ready"), 1)
            for tb in range(4):
                for d in range(2):
                    b = G.open(pe, ("z", tb, d))
                    G.close(pe.matmul(b, low[0:33, tb * 128:tb * 128 + 128], wdec[0:33, d * 512:d * 512 + 512],
                                      start=True, stop=True), ("z", tb, d))
            b = G.open(pe, "tot")
            for tb in range(4):
                for d in range(2):
                    G.read(pe, ("z", tb, d))
                    ins = pe.matmul(b[0:32, :], c_("chunk_pick", (d * 4 + tb) * 32, 32), gg[:, tb, d * 512:d * 512 + 512],
                                    start=(tb + d == 0), stop=(tb == 3 and d == 1))
            G.close(ins, "tot")
            for tb in range(TB):
                for d in range(2):
                    b = G.open(pe, ("bc", tb, d))
                    G.close(pe.matmul(b, c_(("sum_upto64", "sum_from64")[d]), gg[:, tb, d * 512:d * 512 + 512],
                                      start=True, stop=True), ("bc", tb, d))
                    b = G.open(pe, ("aft", tb, d))
                    G.close(pe.matmul(b, c_(("sum_after64", "sum_before64")[d]), gg[:, tb, d * 512:d * 512 + 512],
                                      start=True, stop=True), ("aft", tb, d))
                    for tag, j in (("qe", 0), ("ke", 1)):
                        b = G.open(pe, (tag, tb, d))
                        pe.wait_ge(sem("gla_scaled"), 2 * (2 * tb + d) + j + 1)
                        turn((tag, tb, d), b, [gex[:, j, h * 128:h * 128 + 128] for h in range(4)])
            for tb in range(2, 4):
                for d in range(2):
                    b = G.open(pe, ("aft", tb, d))
                    G.close(pe.matmul(b, c_(("sum_after64", "sum_before64")[d]), gg[:, tb, d * 512:d * 512 + 512],
                                      start=True, stop=True), ("aft", tb, d))
            b = G.open(pe, "dec")
            G.read(pe, "tot")
            for h in range(4):
                ins = pe.transpose(b[:, 32 * h:32 * h + 32], dtm[0:32, h * 128:h * 128 + 128], ident[0:32, 0:32])
            G.close(ins, "dec")
            for tb in range(TB):
                for d in range(2):
                    G.read(pe, ("qe", tb, d))
                    G.read(pe, ("ke", tb, d))
            def inner(i):
                tb, h = i // 4, i % 4
                b = G.open(pe, ("A", i))
                for d in range(2):
                    r = slice(h * T + tb * 128, h * T + tb * 128 + 128)
                    ins = pe.matmul(b[:, d * 128:d * 128 + 128], keT[:, d, r], qeT[:, d, r],
                                    start=(d == 0), stop=(d == 1), skip_group_check=True)
                G.close(ins, ("A", i))

            inner(0)
            for i in range(8):
                if i < 7:
                    inner(i + 1)
                tb, h = i // 4, i % 4
                pe.wait_ge(sem("gla_masked"), i + 1)
                o = (h % 2) * T + tb * 128
                G.close(pe.matmul(acc[h // 2][:, o:o + 128], gv[:, tb, h * 128:h * 128 + 128], atT[:, i, :],
                                  start=(i in (0, 2)), stop=False, skip_group_check=True), ("AV", i))
            for s in range(8):
                for d in range(2):
                    pos = (s % 4) if d == 0 else 3 - s % 4
                    tb, c = (2 if s < 4 else 0) + pos // 2, pos % 2
                    if s < 7:
                        b = G.open(pe, ("U", s, d))
                        pe.wait_ge(sem("gla_keys"), 8)
                        for h in range(4):
                            r = slice(64 * c, 64 * c + 64)
                            ins = pe.matmul(b[:, h * 128:h * 128 + 128], gg[r, tb, d * 512 + h * 128:d * 512 + h * 128 + 128],
                                            gv[r, tb, h * 128:h * 128 + 128], start=(h == 0), stop=(h == 3),
                                            skip_group_check=True)
                        G.close(ins, ("U", s, d))
                    if s >= 4:
                        pe.wait_ge(sem("gla_state"), 2 * (s - 1) + d + 1)
                        for h in range(4):
                            o = (h % 2) * T + pos * 64
                            ins = pe.matmul(acc[h // 2][:, o:o + 64], st[(s - 1) % 2][:, d, h * 128:h * 128 + 128],
                                            qeT[:, d, h * T + pos * 64:h * T + pos * 64 + 64],
                                            start=False, stop=False, skip_group_check=True)
                        G.close(ins, ("I", s, d))
            for hp in range(2):
                b = G.open(pe, ("gn", hp))
                pe.wait_ge(sem("gla_squares"), hp + 1)
                G.close(pe.matmul(b, ones, sqg[:, hp, :], start=True, stop=True), ("gn", hp))
            xm, xg = w3(weights(pe, "w_br_mla"), 4, D), w3(weights(pe, "w_br_gla"), 4, D)
            for n in range(KD):
                for tag, key in (("gm", "gate_mla"), ("gG", "gate_gla")):
                    x = w3(weights(pe, (key, n // 4)), KD, 512)
                    b = G.open(pe, (tag, n))
                    chain((tag, n), b[:, 0:T], lambda k: x[:, k, (n % 4) * 128:(n % 4) * 128 + 128],
                          lambda k: hT[:, k, 0:T], KD)
                if n == 0:
                    for hp in range(4):
                        G.read(pe, ("mla", "o", hp))
                    pe.wait_ge(sem("gla_out"), 2)
                b = G.open(pe, ("bm", n))
                chain(("bm", n), b[:, 0:T], lambda k: xm[:, k, n * 128:n * 128 + 128], lambda k: o_mla[:, k, :], 4)
                b = G.open(pe, ("bg", n))
                chain(("bg", n), b[:, 0:T], lambda k: xg[:, k, n * 128:n * 128 + 128], lambda k: o_gla[:, k, :], 4)
                if n % 4 == 3:
                    G.over(("gate_mla", n // 4), ("gate_gla", n // 4))
            G.over("w_br_mla", "w_br_gla")
            pe.wait_ge(sem("merged"), KD)
            xs = [w3(weights(pe, ("w_out", g)), 4, D) for g in range(2)]
            for n in range(KD):
                b = G.open(pe, ("wo", n))
                chain(("wo", n), b[:, 0:T], lambda k: xs[k // 4][:, k % 4, n * 128:n * 128 + 128],
                      lambda k: merged[:, k, :], KD)
            G.over(("w_out", 0), ("w_out", 1))
            norm(2)
            for g in range(6):
                xg, xv = (w3(weights(pe, (key, g)), KD, min(512, D_FF - 512 * g)) for key in ("up_gate", "up_val"))
                for j in range(min(4, KF - 4 * g)):
                    for tag, x in (("ug", xg), ("uv", xv)):
                        b = G.open(pe, (tag, 4 * g + j))
                        for k in range(KD):
                            if g + j == 0:
                                normed(2, k + 1)
                            ins = pe.matmul(b[:, 0:T], x[:, k, j * 128:j * 128 + 128], hT[:, k, 0:T],
                                            start=(k == 0), stop=(k == KD - 1))
                        G.close(ins, (tag, 4 * g + j))
                G.over(("up_gate", g), ("up_val", g))
                mod(16 + g)
            mod_turn()
            for g in range(6):
                x = w3(weights(pe, ("down", g)), min(4, KF - 4 * g), D)
                for k in range(min(4, KF - 4 * g)):
                    j = 4 * g + k
                    pe.wait_ge(sem("ff_ready"), j + 1)
                    for n in range(KD):
                        ins = pe.matmul(acc[n // 2][:, (n % 2) * T:(n % 2) * T + T], x[:, k, n * 128:n * 128 + 128],
                                        ff[:, j, :], start=(j == 0 and n % 2 == 0), stop=(j == KF - 1),
                                        skip_group_check=True)
                G.close(ins, ("down", g))
                G.over(("down", g))
            for g in range(4):
                b = G.open(pe, ("ct", g))
                pe.wait_ge(sem("ctx2_in"), 16)
                turn(("ct", g), b, [xc2[:, tb, k * 128:k * 128 + 128] for k in (2 * g, 2 * g + 1) for tb in range(TB)])
            norm(3)
            norm(4)
            norm(5)
            normed(4)
            normed(5)
            for tag, n0 in (("e_k", 4), ("e_q", 0)):
                x = w3(weights(pe, tag), KD, 512)
                width = 512 if n0 else T
                for j in range(4):
                    b = G.open(pe, ("eq", n0 + j))
                    chain(("eq", n0 + j), b[:, 0:width], lambda k: x[:, k, j * 128:j * 128 + 128],
                          lambda k: hT[:, k, 0:width], KD)
                G.over(tag)
            x = w3(weights(pe, "e_kv"), KD, 256)
            for tb in range(4):
                token_major("ekv", x, 256, tb)
            G.over("e_kv")
            x = w3(weights(pe, "e_gt"), KD, 16)
            for tb in range(4):
                token_major("egt", x, 16, tb)
            G.over("e_gt")
            x = w3(weights(pe, "e_qa"), KD, 512)
            for tb in range(TB):
                token_major("eqa", x, 512, tb)
            G.over("e_qa")
            x = w3(weights(pe, "e_ob"), KD, 512)
            for j in range(4):
                b = G.open(pe, ("eob", j))
                chain(("eob", j), b[:, 0:T], lambda k: x[:, k, j * 128:j * 128 + 128], lambda k: hT[:, k, 0:T], KD)
            G.over("e_ob")
            pe.wait_ge(sem("heads_ready"), 1)
            for g in range(A_KV):
                b = G.open(pe, ("ekT", g))
                turn(("ekT", g), b, [e_kv[:, tb, g * A_D:g * A_D + A_D] for tb in range(4)])
            for hp in range(4):
                b = G.open(pe, ("eqT", hp))
                turn(("eqT", hp), b, [e_qa[:, tb, h * A_D:h * A_D + A_D] for h in (2 * hp, 2 * hp + 1) for tb in range(TB)])
            for g in range(A_KV):
                G.read(pe, ("ekT", g))
            for hp in range(4):
                G.read(pe, ("eqT", hp))
            attend("gqa", A_H, lambda h: e_qT[0:A_D, h, :], lambda h: e_kT[0:A_D, h // 4, :],
                   lambda h, j: e_kv[:, j, 128 + (h // 4) * A_D:128 + (h // 4) * A_D + A_D], e_prob,
                   lambda i: mod(22 + i // 2) if i % 2 == 0 else None)
            x = w3(weights(pe, "e_vb"), KD, 512)
            for tb in range(4):
                token_major("evb", x, 512, tb)
            G.over("e_vb")
            pe.wait_ge(sem("m_gates"), 1)
            for tb in range(4):
                b = G.open(pe, ("eb", tb))
                pe.matmul(b[:, 0:4], c_("upto128"), m_lf[:, tb, 0:4], start=True, stop=True, skip_group_check=True)
                pe.matmul(b[:, 4:8], c_("from128"), m_lf[:, tb, 4:8], start=True, stop=True, skip_group_check=True)
                G.close(pe.matmul(b[:, 8:16], ones, m_lf[:, tb, :], start=True, stop=True, skip_group_check=True),
                        ("eb", tb))
            for tb in range(4):
                b = G.open(pe, ("ekt", tb))
                if tb == 0:
                    pe.wait_ge(sem("qk_ready"), KD)
                turn(("ekt", tb), b, [qk[:, 4 + h, tb * 128:tb * 128 + 128] for h in range(4)])

            def spread(tb):
                for d in range(2):
                    b = G.open(pe, ("eR", tb, d))
                    pe.wait_ge(sem("m_r"), 4)
                    for h in range(4):
                        c = m_r[:, tb, d * 4 + h:d * 4 + h + 1]
                        ins = pe.transpose(b[:, h * 128:h * 128 + 128], c.to_broadcast([128, 128]), ident)
                    G.close(ins, ("eR", tb, d))

            for tb in (2, 3, 1, 0):
                spread(tb)
            mod(30)
            for j in range(3):
                for d in range(2):
                    tb = BLOCKS[d][j]
                    for hp in range(2):
                        b = G.open(pe, ("eU", j, d, hp))
                        pe.wait_ge(sem("m_keys"), 2 * j + d + 1)
                        for h in (2 * hp, 2 * hp + 1):
                            o = (h % 2) * 129
                            ins = pe.matmul(b[:, o:o + 129], kw[:, d * 4 + h, :],
                                            v1[:, tb, h * 130 + 1 - d:h * 130 + 130 - d], start=(h % 2 == 0),
                                            stop=(h % 2 == 1), skip_group_check=True)
                        G.close(ins, ("eU", j, d, hp))
                if j < 2:
                    mod(31 + j)
            for tb in (1, 0):
                b = G.open(pe, ("eS", tb))
                for h in range(4):
                    ins = pe.matmul(b[:, h * 128:h * 128 + 128], qk[:, h, tb * 128:tb * 128 + 128],
                                    qk[:, 4 + h, tb * 128:tb * 128 + 128], start=(h == 0), stop=(h == 3),
                                    skip_group_check=True)
                G.close(ins, ("eS", tb))
                if tb == 1:
                    pe.wait_ge(sem("m_state"), 12)
                for h in range(4):
                    b = G.open(pe, ("eC", tb, h), second=True)
                    G.close(pe.matmul(b[:, 0:258], qk[:, h, tb * 128:tb * 128 + 128], cn[tb][:, h, :],
                                      start=True, stop=True), ("eC", tb, h))
                mod(33 if tb else 34)
                b = G.open(pe, ("eW", tb))
                pe.wait_ge(sem("m_weights"), 2 - tb)
                turn(("eW", tb), b, [wm[:, h, :] for h in range(4)])
                b = G.open(pe, ("eH", tb))
                G.read(pe, ("eW", tb))
                for h in range(4):
                    ins = pe.matmul(b[:, h * 128:h * 128 + 128], dm[:, h, :], v1[:, tb, h * 130 + 1:h * 130 + 129],
                                    start=(h == 0), stop=(h == 3), skip_group_check=True)
                G.close(ins, ("eH", tb))
                if tb == 0:
                    mod(35)
                b = G.open(pe, ("eT", tb))
                pe.wait_ge(sem("m_out"), 2 - tb)
                turn(("eT", tb), b, [h_e[:, h, :] for h in range(4)])
            mod_turn()
            xs = [w3(weights(pe, ("e_out", g)), 4, D) for g in range(2)]
            for hp in range(4):
                G.read(pe, ("gqa", "o", hp))
            G.read(pe, ("eT", 1))
            G.read(pe, ("eT", 0))
            for n in range(KD):
                b = G.open(pe, ("eo", n))
                chain(("eo", n), b[:, 0:T], lambda k: xs[k // 4][:, k % 4, n * 128:n * 128 + 128],
                      lambda k: (e_oT if k < 4 else e_mT)[:, k % 4, :], KD)
            G.over(("e_out", 0), ("e_out", 1))

            def output(c):
                pe.wait_ge(sem("scaled"), KD * (c + 1))
                for j in range(4):
                    tb, half = j // 2, j % 2
                    b = G.open(pe, ("out", j))
                    turn(("out", j), b, [xT[:, half * 4 + m, tb * 128:tb * 128 + 128] for m in range(4)])

            def experts(layer, c):
                norm(c)
                normed(c)
                for j in range(4):
                    tb, half = j // 2, j % 2
                    b = G.open(pe, ("ht", layer, j))
                    turn(("ht", layer, j), b, [hT[:, half * 4 + m, tb * 128:tb * 128 + 128] for m in range(4)])
                x = w3(weights(pe, ("router", layer)), KD, N_EXP)
                for tb in range(TB):
                    b = G.open(pe, ("lg", layer, tb))
                    chain(("lg", layer, tb), b[:, 0:N_EXP], lambda k: hT[:, k, tb * 128:tb * 128 + 128],
                          lambda k: x[:, k, :], KD)
                G.over(("router", layer))
                b = G.open(pe, ("aT", layer))
                pe.wait_ge(sem("affinity"), 2 * layer + 2)
                turn(("aT", layer), b, [aff[:, tb, :] for tb in range(TB)])
                b = G.open(pe, ("mT", layer))
                pe.wait_ge(sem("chosen"), layer + 1)
                for tb in range(TB):
                    ins = pe.transpose(b[:, tb * N_EXP:(tb + 1) * N_EXP], mask_e[0:N_EXP, tb * 128:tb * 128 + 128],
                                       ident[0:N_EXP, 0:N_EXP])
                G.close(ins, ("mT", layer))
                b = G.open(pe, ("cs", layer))
                G.read(pe, ("mT", layer))
                pe.matmul(b[:, 0:N_EXP], c_("upto128"), mask_t[:, 0, :], start=True, stop=True, skip_group_check=True)
                pe.matmul(b[:, 16:32], ones, mask_t[:, 0, :], start=True, stop=False, skip_group_check=True)
                G.close(pe.matmul(b[:, 16:32], c_("upto128"), mask_t[:, 1, :], start=False, stop=True,
                                  skip_group_check=True), ("cs", layer))
                pe.wait_ge(sem("one_hot"), layer + 1)
                for j in range(4):
                    G.read(pe, ("ht", layer, j))
                for k in range(KD):
                    b = G.open(pe, ("xs", layer, k))
                    for tb in range(TB):
                        ins = pe.matmul(b, h_tm[:, tb, k * 128:k * 128 + 128], hot[:, tb, :], start=(tb == 0),
                                        stop=(tb == 1))
                    G.close(ins, ("xs", layer, k))
                pe.wait_ge(sem("gated_hot"), layer + 1)
                for e2 in range(N_EXP // 2):
                    b = G.open(pe, ("gT", layer, e2))
                    for m in range(4):
                        e, tb = 2 * e2 + m // 2, m % 2
                        ins = pe.transpose(b[:, m * 128:m * 128 + 128], hotg[:, tb, e * 128:e * 128 + 128], ident)
                    G.close(ins, ("gT", layer, e2))
                for e2 in range(N_EXP // 2):
                    G.read(pe, ("gT", layer, e2))
                for b in acc:
                    pe.matmul(b[:, 0:2], ones, nul, start=True, stop=False, skip_group_check=True)
                first, base, came = moe_first[layer], G.count, moe_sent[layer]
                moe_base[layer] = base
                for b in range(RING):
                    G.drain(pe, b)

                def slot(j, e, pe):
                    s = (first + j) % SLOTS
                    pe.wait_ge(slot_full[s], e * (32 if j < 4 else 16) + came[s] + (32 if j < 4 else 16))
                    return ring[:, s * SLOT:(s + 1) * SLOT]

                with pe.Fori(0, N_EXP // 2) as pair:
                    for par in range(2):
                        e = pair * 2 + par
                        pe.wait_ge(sem("rows_ready"), e + (N_EXP * layer + 1))
                        for j in range(4):
                            x = slot(j, e, pe)
                            for kk in range(2):
                                k = 2 * j + kk
                                for q in range(4):
                                    o = (q // 2) * 2048 + kk * D + (q % 2) * 512
                                    ins = pe.matmul(bank[0][32 * q:32 * q + 32, :], xe[:, par, k * CAP:(k + 1) * CAP],
                                                    x[:, o:o + 512], start=(k == 0), stop=(k == KD - 1),
                                                    skip_group_check=True)
                        ins.then_inc(done, 1)
                        pe.wait_ge(sem("gu_copied"), e + (N_EXP * layer + 1))
                        for j in range(4):
                            ins = pe.transpose(bank[1][:, j * 128:j * 128 + 128], gu[:, j * 128:j * 128 + 128], ident)
                        ins.then_inc(done, 1)
                        pe.wait_ge(sem("act_ready"), e + (N_EXP * layer + 1))
                        for j in range(2):
                            x = w3(slot(4 + j, e, pe), 4, D)
                            for h in range(2):
                                for q in range(4):
                                    ins = pe.matmul(bank[2 + h][32 * q:32 * q + 32, :], act_t[:, 4 * j + q, :],
                                                    x[:, q, h * 512:h * 512 + 512], start=(j == 0), stop=(j == 1),
                                                    skip_group_check=True)
                        ins.then_inc(done, 1)
                        pe.wait_ge(sem("down_copied"), e * 2 + (2 * N_EXP * layer + 2))
                        for n in range(KD):
                            ins = pe.matmul(acc[n // 2][:, (n % 2) * T:(n % 2) * T + T],
                                            dsb[:, n // 4, (n % 4) * 128:(n % 4) * 128 + 128],
                                            gates_flat[:, bass.ds(e * T, T)], start=False, stop=False,
                                            skip_group_check=True)
                        ins.then_inc(done, 1)
                G.count += 4 * N_EXP

            experts(0, 6)
            norm(7)
            normed(7)
            xs = [w3(weights(pe, ("o_in", g)), KD, 512) for g in range(2)]
            for tb in range(TB):
                for g in range(2):
                    b = G.open(pe, ("u", tb, g))
                    chain(("u", tb, g), b, lambda k: hT[:, k, tb * 128:tb * 128 + 128], lambda k: xs[g][:, k, :], KD)
            G.over(("o_in", 0), ("o_in", 1))
            for tb in range(TB):
                for g in range(2):
                    G.read(pe, ("u", tb, g))
            x = w3(weights(pe, "pool"), TB, 4 * T)
            for c in range(KD):
                b = G.open(pe, ("p", c))
                chain(("p", c), b[:, 0:T], lambda k: u_tm[:, k, c * 128:c * 128 + 128],
                      lambda k: x[:, k, (c // 2) * T:(c // 2) * T + T], TB)
            G.over("pool")
            x = w3(weights(pe, "w_grp"), KD, 256)
            for n in range(KD):
                b = G.open(pe, ("y", n))
                for k in range(2):
                    G.read(pe, ("p", n - n % 2 + k))
                chain(("y", n), b[:, 0:T], lambda k: x[:, n - n % 2 + k, (n % 2) * 128:(n % 2) * 128 + 128],
                      lambda k: pT[:, n - n % 2 + k, :], 2)
            G.over("w_grp")
            experts(1, 8)
            norm(9)
            output(9)

        @block.sync
        def _(sp):
            def send(items, limit):
                for n, (key, pieces) in enumerate(items):
                    sl, _ = place[key]
                    if limit + n >= SLOTS:
                        sp.wait_ge(done, G.last_user[sequence[limit + n - SLOTS]])
                    for (lo, hi), k, src in pieces:
                        sp.dma_start(ring[:, sl * SLOT + lo:sl * SLOT + hi].rearrange("p (k n) -> p k n", k=k),
                                     src).then_inc(slot_full[sl], 16)

            sequence = [key for key, _ in before]
            send(before, 0)
            def send_experts(layer, ahead):
                first, base = moe_first[layer], moe_base[layer]
                gate, up, down = (w[n] for n in ("w_exp_gate_2", "w_exp_up_2", "w_exp_down_2"))

                def pieces(e):
                    for j in range(4):
                        for a, m in ((0, gate), (1, up)):
                            yield j, 2 * a, m[layer, bass.ds(e, 1), 256 * j:256 * j + 256, :], 2
                    for j in range(2):
                        yield 4 + j, 0, down[layer, bass.ds(e, 1), 512 * j:512 * j + 512, :], 4

                def put(j, lo, src, k):
                    s = (first + j) % SLOTS
                    sp.dma_start(ring[:, s * SLOT + lo * D:s * SLOT + (lo + k) * D].rearrange("p (k n) -> p k n", k=k),
                                 src.rearrange("e (k p) n -> p (e k) n", p=128)).then_inc(slot_full[s], 16)

                last = -1
                for j, lo, src, k in pieces(0):
                    if j != last and ahead[j] is not None:
                        sp.wait_ge(done, ahead[j])
                    last = j
                    put(j, lo, src, k)
                with sp.Fori(1, N_EXP) as e:
                    last = -1
                    for j, lo, src, k in pieces(e):
                        if j != last:
                            sp.wait_ge(done, e * 4 + (base - 3 if j < 4 else base - 1))
                        last = j
                        put(j, lo, src, k)

            send_experts(0, [G.last_user[k] for k in sequence[-SLOTS:]])
            base = moe_base[0] + 4 * (N_EXP - 1)
            for n, (key, pieces_) in enumerate(between):
                sp.wait_ge(done, base + (1 if n < 4 else 3))
                sl, _ = place[key]
                for (lo, hi), k, src in pieces_:
                    sp.dma_start(ring[:, sl * SLOT + lo:sl * SLOT + hi].rearrange("p (k n) -> p k n", k=k),
                                 src).then_inc(slot_full[sl], 16)
            ahead = [base + (1 if n < 4 else 3) for n in range(len(between), SLOTS)]
            send_experts(1, ahead + [G.last_user[key] for key, _ in between])

        @block.scalar
        def _(act):
            count = [0]

            def link(ins):
                ins.then_inc(sem("act_step"), 1)
                count[0] += 1
                act.wait_ge(sem("act_step"), count[0])

            act.dma_start(cst[:, :], w["tables"]).then_inc(sem("tables_in"), 16)
            for t in range(4):
                for r, src in vparts[t]:
                    act.dma_start(vrow[r:r + src.shape[0], 128 * t:128 * t + 128], src).then_inc(sem("vectors_in"), 16)
            act.dma_start(x_tm[:, 0:2, :], w["x"][0].rearrange("(b p) d -> p b d", p=128)).then_inc(sem("x_in"), 16)
            act.dma_start(x_tm[:, 2:4, :], w["ctx"][0].rearrange("(b p) d -> p b d", p=128)).then_inc(sem("x_in"), 16)

            def evict(name, to, func=ACT.Copy, n=None, **kw):
                b = G.take(act, name)
                src = b[:, 0:n] if n else b
                G.give(act.activation(to, src, func, **kw), name)

            def squares(c, src):
                if c:
                    act.wait_ge(done, G.number[("ms", c - 1)])
                for k in range(KD):
                    act.activation(sq[:, k, :], src[:, k, :], ACT.Square).then_inc(sem("squares"), 1)

            def root(c, shift=None, dst=None):
                b = G.take(act, ("ms", c))
                if c:
                    act.wait_ge(sem("scaled"), KD * c)
                G.give(act.activation(rs, b[:, 0:T], ACT.Sqrt, bias=eps, scale=1.0 / D), ("ms", c))
                if dst is not None:
                    for k in range(KD):
                        act.wait_ge(sem("scaled"), KD * c + k + 1)
                        act.activation(dst[:, k, :], dst[:, k, :], ACT.Identity,
                                       bias=shift[:, k:k + 1]).then_inc(sem("normed"), 1)

            def mod(i):
                G_take = G.take(act, ("mod", i))
                if i:
                    act.wait_ge(done, G.number[("mod_t", i - 1)])
                G.give(act.activation(mrow, G_take, ACT.Copy), ("mod", i))

            act.wait_ge(sem("eps_ready"), 1)
            act.wait_ge(sem("vcol_ready"), 1)
            act.wait_ge(sem("cond_cleared"), 1)
            for which, names in enumerate((("c", "cc"), ("c2", "cc2"))):
                for r, name in enumerate(names):
                    act.activation(cond[:, which, :, r], vc(name, 0, KD), ACT.Silu).then_inc(sem("cond_ready"), 1)
            for k in range(1, KD, 2):
                b = G.take(act, ("xt", k))
                act.copy(xT[:, k, :], b[:, 0:T])
                G.give(act.copy(xcT[:, k, :], b[:, T:2 * T]), ("xt", k))
            for k in range(KD):
                G.read(act, ("xt", k))
            squares(0, xT)
            for i in range(4):
                mod(i)
            root(0, mc(0, 0), hT[:, :, 0:T])
            squares(1, xcT)
            root(1, mc(0, 0, 1), hT[:, :, T:2 * T])

            def rms_root(tag, tb, n, dim, at_):
                b = G.take(act, (tag, tb))
                link(act.activation(junk[:, 0:n], b[:, 0:n], ACT.Square, accum_out=small[:, at_ + tb:at_ + tb + 1]))
                act.activation(small[:, at_ + tb:at_ + tb + 1], small[:, at_ + tb:at_ + tb + 1], ACT.Sqrt,
                               bias=eps, scale=1.0 / dim).then_inc(sem(tag + "_root"), 1)

            for tb in range(4):
                rms_root("kvr", tb, KV_LORA, KV_LORA, 8)
            for j in range(2):
                evict(("kvt", j), kvT[:, j, :], ACT.Copy, scale=vc("kvn", j))
            for tb in range(4):
                b = G.take(act, ("kv", tb, 1))
                v = b.rearrange("p (h c) -> p h c", h=4)
                act.copy(kcat[:, tb, 4 * QH:].rearrange("p (h c) -> p h c", h=4)[:, :, 0:NOPE], v[:, :, 0:NOPE])
                G.give(act.copy(v_tm[:, tb, 256:512].rearrange("p (h c) -> p h c", h=4), v[:, :, NOPE:]), ("kv", tb, 1))
            for tb in range(TB):
                rms_root("qc", tb, Q_LORA, Q_LORA, 12)
            for h in (1, 3):
                G.give(act.copy(kT[0:QH, h, :], G.take(act, ("kT", h))[0:QH, :]), ("kT", h))
            for j in range(3):
                evict(("qct", j), qcT[:, j, :], ACT.Copy, n=T, scale=vc("qn", j))
            for tb in range(TB):
                evict(("q", tb, 1), q_tm[:, tb, 384:768], n=384)
            for h in (5, 7):
                G.give(act.copy(kT[0:QH, h, :], G.take(act, ("kT", h))[0:QH, :]), ("kT", h))
            for hp in (1, 3):
                G.give(act.copy(qT[0:QH, 2 * hp:2 * hp + 2, :].rearrange("p a b -> p (a b)"),
                                G.take(act, ("qT", hp))[0:QH, :]), ("qT", hp))

            def attend(tag, heads, scale, pr, prT, fill):
                for i in range(2 * heads + 1):
                    if i < 2 * heads:
                        b = G.take(act, (tag, "s", i))
                        act.wait_ge(sem(tag + "_max"), i + 1)
                        if i >= 2:
                            act.wait_ge(done, G.number[(tag, "pt", i - 2)])
                        act.activation(pr[:, i % 2, :], b, ACT.Exp, bias=small[:, 32 + i:33 + i], scale=scale,
                                       accum_out=small[:, 64 + i:65 + i]).then_inc(sem(tag + "_exp"), 1)
                    if i and i % 2 == 0:
                        transposed(act, tag, i - 1, prT)
                    if i < 2 * heads:
                        fill(i)

            def transposed(eng, tag, i, prT):
                h, qb = i // 2, i % 2
                b = G.take(eng, (tag, "pt", i))
                if h >= 2:
                    eng.wait_ge(done, G.number[(tag, "o", h // 2 - 1)])
                to = prT[:, h % 2, :].rearrange("p (j t) -> p j t", j=4)[:, :, qb * 128:qb * 128 + 128]
                src = b.rearrange("p (j t) -> p j t", j=4)
                G.give((act.copy if eng is act else eng.tensor_copy)(to, src), (tag, "pt", i))

            attend("mla", MLA_H, QH ** -0.5, prob, probT, lambda i: mod(4 + i // 2) if i % 2 == 0 else None)
            act.wait_ge(sem("wdec_cleared"), 1)
            act.dma_start(wdec[0:16, 0:512], w["gla_w_decay"][0, 0]).then_inc(sem("decay_in"), 16)
            act.dma_start(wdec[16:32, 512:1024], w["gla_w_decay"][0, 1]).then_inc(sem("decay_in"), 16)
            act.dma_start(wdec[32:33, :], w["gla_b_decay"].rearrange("a b c -> a (b c)")).then_inc(sem("decay_in"), 16)
            for tb in range(4):
                if tb % 2:
                    evict(("gk", tb), gk[:, tb, :])
            mod(12)
            for tb in range(4):
                if tb % 2:
                    evict(("gv", tb), gv[:, tb, :])
            mod(13)
            evict(("gq", 1), gq[:, 1, :], scale=128 ** -0.5)
            mod(14)
            for j in range(4):
                evict(("gr", j), grT[:, j, :], ACT.Silu, n=T)
            mod(15)
            for tb in range(4):
                for d in range(2):
                    g = gg[:, tb, d * 512:d * 512 + 512]
                    link(act.activation(g, G.take(act, ("z", tb, d)), ACT.Abs))
                    link(act.activation(g, g, ACT.Exp, scale=-1.0))
                    act.activation(g, g, ACT.Ln, bias=one).then_inc(sem("gate_log"), 1)
            b = G.take(act, "tot")
            G.give(act.activation(dtm[0:32, :], b[0:32, :], ACT.Exp), "tot")
            for tb in range(TB):
                for d in range(2):
                    b = G.take(act, ("bc", tb, d))
                    if tb + d:
                        act.wait_ge(done, G.number[("ke",) + ((tb, 0) if d else (tb - 1, 1))])
                    act.activation(gex[:, 0, :], b, ACT.Exp)
                    G.give(act.activation(gex[:, 1, :], b, ACT.Exp, scale=-1.0), ("bc", tb, d))
                    evict(("aft", tb, d), gg[:, tb, d * 512:d * 512 + 512], ACT.Exp)
                    b = G.take(act, ("ke", tb, d))
                    to = keT[:, d, :].rearrange("p (h t) -> p h t", h=4)[:, :, tb * 128:tb * 128 + 128]
                    G.give(act.copy(to, b.rearrange("p (h t) -> p h t", h=4)), ("ke", tb, d))
            for tb in range(2, 4):
                for d in range(2):
                    evict(("aft", tb, d), gg[:, tb, d * 512:d * 512 + 512], ACT.Exp)
            for hp in range(2):
                act.wait_ge(done, G.number[("I", 7, 1)])
                act.activation(sqg[:, hp, :], acc[hp], ACT.Square).then_inc(sem("gla_squares"), 1)
            for hp in range(2):
                evict(("gn", hp), rtg[:, hp, :], ACT.Sqrt, bias=eps, scale=1.0 / 128)
            for n in range(KD):
                if n >= 2:
                    act.wait_ge(sem("merged"), n - 1)
                evict(("gm", n), sig[:, 2 * (n % 2), :], ACT.Sigmoid, n=T)
                evict(("gG", n), sig[:, 2 * (n % 2) + 1, :], ACT.Sigmoid, n=T)
            for n in range(KD):
                G.read(act, ("wo", n))
            act.dma_start(xc2[:, :, :], w["ctx_2"][0].rearrange("(b p) d -> p b d", p=128)).then_inc(sem("ctx2_in"), 16)
            squares(2, xT)
            root(2, mc(0, 3), hT[:, :, 0:T])
            for j in range(KF):
                b = G.take(act, ("ug", j))
                if j >= 3:
                    act.wait_ge(sem("conv_done"), j - 2)
                else:
                    act.wait_ge(sem("pad_cleared"), 1)
                grid = pad[:, j % 3, :].rearrange("p (r c) -> p r c", r=ROWS + 2)[:, 1:ROWS + 1, 1:GRID_W + 1]
                G.give(act.copy(grid, b[:, 0:T].rearrange("p (r c) -> p r c", r=ROWS)), ("ug", j))
                evict(("uv", j), ff[:, j, :], n=T)
                if j % 4 == 3:
                    mod(16 + j // 4)
                if j:
                    act.wait_ge(sem("conv_done"), j)
                    act.activation(gel[:, (j - 1) % 3, :], gel[:, (j - 1) % 3, :], ACT.Gelu).then_inc(sem("gelu_done"), 1)
            mod(21)
            act.wait_ge(sem("conv_done"), KF)
            act.activation(gel[:, (KF - 1) % 3, :], gel[:, (KF - 1) % 3, :], ACT.Gelu).then_inc(sem("gelu_done"), 1)
            for g in (1, 3):
                evict(("ct", g), xc2T[:, 2 * g:2 * g + 2, :].rearrange("p a b -> p (a b)"))
            act.wait_ge(sem("ff_added"), KD)
            squares(3, xT)
            root(3)
            act.dma_start(small[:, 640:704], w["g_qnorm_2"].to_broadcast([128, A_D])).then_inc(sem("heads_in"), 16)
            act.dma_start(small[:, 704:768], w["g_knorm_2"].to_broadcast([128, A_D])).then_inc(sem("heads_in"), 16)
            act.dma_start(small[:, 112:128], w["b_gate_2"].to_broadcast([128, 16])).then_inc(sem("heads_in"), 16)
            act.wait_ge(sem("scaled"), KD * 4)
            squares(4, xT)
            root(4, mc(1, 0), hT[:, :, 0:T])
            G.read(act, ("ct", 0))
            G.read(act, ("ct", 2))
            squares(5, xc2T)
            root(5, mc(1, 0, 1), hT[:, :, T:2 * T])

            def silu(i):
                act.wait_ge(sem("conv2_done"), i + 1)
                n = (i + 4) % 8
                v = qk[:, n, 0:512 if n >= 4 else T]
                act.activation(v, v, ACT.Silu).then_inc(sem("qk_ready"), 1)

            for i in range(8):
                n = (i + 4) % 8
                b = G.take(act, ("eq", n))
                if i >= 3:
                    act.wait_ge(sem("conv2_done"), i - 2)
                else:
                    act.wait_ge(sem("raw_cleared"), 1)
                to = raw[:, i % 3, :].rearrange("p (s t) -> p s t", s=2)[:, 0:2 if n >= 4 else 1, 1:T + 1]
                G.give(act.copy(to, b[:, 0:512 if n >= 4 else T].rearrange("p (s t) -> p s t", t=T)), ("eq", n))
                if i:
                    silu(i - 1)
            silu(7)
            for tb in (1, 3):
                evict(("ekv", tb), e_kv[:, tb, :], n=256)
            evict(("eqa", 1), e_qa[:, 1, :])
            act.wait_ge(sem("heads_squared"), 1)
            act.activation(small[:, 8:32], small[:, 8:32], ACT.Sqrt, bias=eps, scale=1.0 / A_D).then_inc(sem("heads_root"), 1)
            for j in range(4):
                evict(("eob", j), e_ob[:, j, :], ACT.Sigmoid, n=T)
            G.give(act.copy(e_kT[0:A_D, 1, :], G.take(act, ("ekT", 1))[0:A_D, :]), ("ekT", 1))
            for hp in (1, 3):
                G.give(act.copy(e_qT[0:A_D, 2 * hp:2 * hp + 2, :].rearrange("p a b -> p (a b)"),
                                G.take(act, ("eqT", hp))[0:A_D, :]), ("eqT", hp))
            attend("gqa", A_H, A_D ** -0.5, e_prob, e_probT, lambda i: mod(22 + i // 2) if i % 2 == 0 else None)
            act.wait_ge(sem("v1_set"), 1)
            for tb in (1, 3):
                b = G.take(act, ("evb", tb))
                G.give(act.copy(v1[:, tb, :].rearrange("p (h c) -> p h c", h=4)[:, :, 1:129],
                                b.rearrange("p (h c) -> p h c", h=4)), ("evb", tb))
            f = gsm[:, 0:64].rearrange("p (x y) -> p x y", x=8)[:, :, 4:8]
            ln = gsm[:, 224:256].rearrange("p (x y) -> p x y", x=8)
            act.wait_ge(sem("m_biased"), 1)
            link(act.activation(ln, f, ACT.Abs))
            link(act.activation(ln, ln, ACT.Exp, scale=-1.0))
            act.activation(ln, ln, ACT.Ln, bias=one).then_inc(sem("m_log"), 1)
            for tb in (1, 3):
                evict(("ekt", tb), ktm[:, tb, :])
            mod(30)
            for j in range(3):
                for d in range(2):
                    act.wait_ge(sem("m_args"), 2 * j + d + 1)
                    x = m_x[:, 2 * j + d, 0:8 if j else 4]
                    act.activation(x, x, ACT.Exp).then_inc(sem("m_exps"), 1)
                if j < 2:
                    mod(31 + j)
            for tb in (1, 0):
                act.wait_ge(sem("m_shifted"), 2 - tb)
                act.activation(wm[:, :, :], dmx[tb], ACT.Exp)
                x = gsm[:, 352:368]
                act.activation(x, x, ACT.Exp).then_inc(sem("m_wexp"), 1)
                mod(33 if tb else 34)
                b = G.take(act, ("eW", tb))
                G.give(act.copy(dm[:, 0:4, :].rearrange("p a b -> p (a b)"), b), ("eW", tb))
                if tb == 0:
                    mod(35)
                act.wait_ge(sem("m_hsq"), 2 - tb)
                act.activation(m_ss[:, 0:4], m_ss[:, 0:4], ACT.Sqrt, bias=eps, scale=1.0 / 128).then_inc(sem("m_hroot"), 1)
            def after_update(tag, names):
                for n in names:
                    G.read(act, n)

            def output(c):
                for j in (1, 3):
                    evict(("out", j), x_tm[:, j // 2, 512:1024])
                for j in range(4):
                    G.read(act, ("out", j))
                act.dma_start(out[0].rearrange("(b p) d -> p b d", p=128), x_tm[:, 0:2, :]).then_inc(sem("out_sent"), 16)
                act.wait_ge(sem("out_sent"), 16)

            for n in range(KD):
                G.read(act, ("eo", n))
            def experts(layer, c):
                squares(c, xT)
                root(c, mc(1 + layer, 3), hT[:, :, 0:T])
                for j in (1, 3):
                    evict(("ht", layer, j), h_tm[:, j // 2, 512:1024])
                for tb in range(TB):
                    b = G.take(act, ("lg", layer, tb))
                    act.wait_ge(sem("router_max"), 2 * layer + tb + 1)
                    act.activation(aff[:, tb, :], b[:, 0:N_EXP], ACT.Exp, bias=small[:, 32 + tb:33 + tb],
                                   accum_out=small[:, 64 + tb:65 + tb]).then_inc(sem("router_exp"), 1)
                for k in range(1, KD, 2):
                    evict(("xs", layer, k), xsel[:, k, :])
                for e2 in range(1, N_EXP // 2, 2):
                    evict(("gT", layer, e2), gates_flat[:, e2 * 512:e2 * 512 + 512])
                base = moe_base[layer]
                with act.Fori(0, N_EXP) as e:
                    act.wait_ge(done, e * 4 + (base + 1))
                    act.copy(gu, bank[0]).then_inc(sem("gu_copied"), 1)
                    act.wait_ge(done, e * 4 + (base + 2))
                    t = bank[1].rearrange("p (j c) -> p j c", j=4)
                    act.activation(sil.rearrange("p a b -> p (a b)").rearrange("p (j c) -> p j c", j=4), t[:, :, 0:64],
                                   ACT.Silu).then_inc(sem("silu_ready"), 1)
                    act.wait_ge(done, e * 4 + (base + 3))
                    act.copy(dsb[:, 1, :], bank[3]).then_inc(sem("down_copied"), 1)
                act.wait_ge(sem("moe_added"), KD * (layer + 1))

            experts(0, 6)
            squares(7, xT)
            root(7, mc(2, 0), hT[:, :, 0:T])
            for tb in range(TB):
                evict(("u", tb, 1), u_tm[:, tb, 512:1024])
            for c in range(1, KD, 2):
                evict(("p", c), pT[:, c, :], n=T)
            for n in range(KD):
                G.read(act, ("y", n))
            experts(1, 8)
            squares(9, xT)
            root(9)
            output(9)

        @block.vector
        def _(dve):
            count = [0]

            def link(ins):
                ins.then_inc(sem("dve_step"), 1)
                count[0] += 1
                dve.wait_ge(sem("dve_step"), count[0])

            def evict(name, to, n=None):
                b = G.take(dve, name)
                G.give(dve.tensor_copy(to, b[:, 0:n] if n else b), name)

            def mod(i):
                which, jj = i // 12, (i % 12) * 4
                to = modc[:, 96 * which + 2 * jj:96 * which + 2 * jj + 8].rearrange("p (j r) -> p j r", r=2)
                b = G.take(dve, ("mod_t", i))
                G.give(dve.tensor_reduce(to, b.rearrange("p (j q r) -> p j r q", j=4, q=4)[:, :, 0:2, :], AX.X, ALU.add),
                       ("mod_t", i))
                G.read(dve, ("mod_t", i))
                bias = vc("b_ada", jj, 4) if which == 0 else vc("b_mod", 48 * (which - 1) + jj, 4)
                link(dve.tensor_tensor(to, to, bias.unsqueeze(2).to_broadcast([128, 4, 2]), ALU.add))

            def set_gain(i, scale, g):
                link(dve.scalar_tensor_tensor(gains(i), scale, 1.0, g, ALU.add, ALU.mult))

            def norm(c, src, g, dst):
                G.read(dve, ("ms", c))
                link(dve.reciprocal(rs, rs))
                for k in range(KD):
                    dve.scalar_tensor_tensor(dst[:, k, :], src[:, k, :], g[:, k:k + 1], rs,
                                             ALU.mult, ALU.mult).then_inc(sem("scaled"), 1)

            def rope(src, dst, tab, tb, tmp, n, q):
                a, size = at[tab]
                t = cst[:, a + tb * size // 2:a + (tb + 1) * size // 2].rearrange("p (c x q) -> p c x q", c=2, x=2)
                s1, s2 = src[:, :, :, 0, :], src[:, :, :, 1, :]
                cos, sin = (t[:, c].unsqueeze(1).to_broadcast([128, n, 2, q]) for c in range(2))
                t1, t2, t3, t4 = (tmp[:, i * n * 2 * q:(i + 1) * n * 2 * q].rearrange("p (n x q) -> p n x q", n=n, x=2)
                                  for i in range(4))
                dve.tensor_tensor(t1, s1, cos, ALU.mult)
                dve.tensor_tensor(t2, s2, sin, ALU.mult)
                dve.tensor_tensor(t3, s2, cos, ALU.mult)
                link(dve.tensor_tensor(t4, s1, sin, ALU.mult))
                dve.tensor_tensor(dst[:, :, :, 0, :], t1, t2, ALU.subtract)
                return dve.tensor_tensor(dst[:, :, :, 1, :], t3, t4, ALU.add)

            dve.memset(eps, EPS)
            dve.memset(nul, 0.0)
            dve.memset(one, 1.0).then_inc(sem("eps_ready"), 1)
            dve.memset(cond[:, :, :, :], 0.0).then_inc(sem("cond_cleared"), 1)
            b = G.take(dve, "vec")
            for t in range(3):
                dve.tensor_copy(vcol[:, 128 * t:128 * t + tiles[t]], b[:, 128 * t:128 * t + tiles[t]])
            G.give(dve.tensor_copy(vcol[:, 384:384 + tiles[3]], b[:, 384:384 + tiles[3]]), "vec")
            G.read(dve, "vec")
            dve.sem_inc(sem("vcol_ready"), 1)
            for k in range(0, KD, 2):
                b = G.take(dve, ("xt", k))
                dve.tensor_copy(xT[:, k, :], b[:, 0:T])
                G.give(dve.tensor_copy(xcT[:, k, :], b[:, T:2 * T]), ("xt", k))
            for i in range(4):
                mod(i)
            set_gain(0, mc(0, 1), vc("n1", 0, KD))
            set_gain(1, mc(0, 1, 1), vc("n1", 0, KD))
            norm(0, xT, gains(0), hT[:, :, 0:T])
            norm(1, xcT, gains(1), hT[:, :, T:2 * T])

            def low_rank(tag, tb, to, n, at_, say):
                b = G.take(dve, (tag, tb))
                dve.wait_ge(sem(tag + "_root"), tb + 1)
                r = small[:, at_ + tb:at_ + tb + 1]
                link(dve.reciprocal(r, r))
                link(dve.tensor_scalar(to, b[:, 0:n], r, None, ALU.mult))
                dve.sem_inc(sem(say), 1)
                return b

            for tb in range(4):
                b = low_rank("kvr", tb, kvr[:, tb, 0:KV_LORA], KV_LORA, 8, "kv_norm")
                G.give(dve.tensor_copy(kvr[:, tb, KV_LORA:288], b[:, KV_LORA:288]), ("kvr", tb))
                G.read(dve, ("kvr", tb))
                src = kvr[:, tb, KV_LORA:288]
                if tb < TB:
                    link(rope(src.rearrange("p (n x h q) -> p n x h q", n=1, x=2, h=2),
                              src.rearrange("p (n x h q) -> p n x h q", n=1, x=2, h=2), "rope32", tb, small[:, 128:384], 1, 8))
                dve.tensor_copy(kcat[:, tb, :].rearrange("p (h c) -> p h c", h=MLA_H)[:, :, NOPE:],
                                src.unsqueeze(1).to_broadcast([128, MLA_H, ROPE])).then_inc(sem("k_rope"), 1)
            for tb in range(4):
                b = G.take(dve, ("kv", tb, 0))
                v = b.rearrange("p (h c) -> p h c", h=4)
                dve.tensor_copy(kcat[:, tb, 0:4 * QH].rearrange("p (h c) -> p h c", h=4)[:, :, 0:NOPE], v[:, :, 0:NOPE])
                G.give(dve.tensor_copy(v_tm[:, tb, 0:256].rearrange("p (h c) -> p h c", h=4), v[:, :, NOPE:]), ("kv", tb, 0))
            for tb in range(TB):
                low_rank("qc", tb, qc[:, tb, :], Q_LORA, 12, "q_norm")
                dve.sem_inc(freed[G.bank[("qc", tb)]], 1)
            for h in (0, 2):
                G.give(dve.tensor_copy(kT[0:QH, h, :], G.take(dve, ("kT", h))[0:QH, :]), ("kT", h))
            for tb in range(TB):
                evict(("q", tb, 0), q_tm[:, tb, 0:384], 384)
                G.read(dve, ("q", tb, 0))
                G.read(dve, ("q", tb, 1))
                v = q_tm[:, tb, :].rearrange("p (h c) -> p h c", h=MLA_H)[:, :, NOPE:].rearrange(
                    "p n (x h q) -> p n x h q", x=2, h=2)
                rope(v, v, "rope32", tb, small[:, 128:640], MLA_H, 8).then_inc(sem("q_rope"), 1)
            for h in (4, 6):
                G.give(dve.tensor_copy(kT[0:QH, h, :], G.take(dve, ("kT", h))[0:QH, :]), ("kT", h))
            for hp in (0, 2):
                G.give(dve.tensor_copy(qT[0:QH, 2 * hp:2 * hp + 2, :].rearrange("p a b -> p (a b)"),
                                       G.take(dve, ("qT", hp))[0:QH, :]), ("qT", hp))

            def transposed(tag, i, prT):
                h, qb = i // 2, i % 2
                b = G.take(dve, (tag, "pt", i))
                if h >= 2:
                    dve.wait_ge(done, G.number[(tag, "o", h // 2 - 1)])
                to = prT[:, h % 2, :].rearrange("p (j t) -> p j t", j=4)[:, :, qb * 128:qb * 128 + 128]
                G.give(dve.tensor_copy(to, b.rearrange("p (j t) -> p j t", j=4)), (tag, "pt", i))

            def attend(tag, heads, scale, pr, prT, oT, fill):
                def top(i):
                    b = G.take(dve, (tag, "s", i))
                    link(dve.tensor_reduce(small[:, 96 + i:97 + i], b, AX.X, ALU.max))
                    dve.tensor_scalar(small[:, 32 + i:33 + i], small[:, 96 + i:97 + i], -scale, None,
                                      ALU.mult).then_inc(sem(tag + "_max"), 1)

                top(0)
                for i in range(2 * heads):
                    if i + 1 < 2 * heads:
                        top(i + 1)
                    dve.wait_ge(sem(tag + "_exp"), i + 1)
                    r = small[:, 64 + i:65 + i]
                    G.give(dve.reciprocal(r, r), (tag, "s", i))
                    G.read(dve, (tag, "s", i))
                    dve.tensor_scalar(pr[:, i % 2, :], pr[:, i % 2, :], r, None, ALU.mult).then_inc(sem(tag + "_prob"), 1)
                    fill(i)
                    if i >= 4 and i % 4 == 0:
                        evict((tag, "o", i // 4 - 1), oT[:, i // 4 - 1, :], T)
                    if i % 2 == 0:
                        transposed(tag, i, prT)
                evict((tag, "o", heads // 2 - 1), oT[:, heads // 2 - 1, :], T)

            attend("mla", MLA_H, QH ** -0.5, prob, probT, o_mla,
                   lambda i: mod(4 + i // 2 - 1) if i % 2 == 0 and i else None)
            dve.memset(wdec[0:33, :], 0.0).then_inc(sem("wdec_cleared"), 1)
            for tb in (0, 2):
                evict(("gk", tb), gk[:, tb, :])
            mod(11)
            for tb in (0, 2):
                evict(("gv", tb), gv[:, tb, :])
            mod(12)
            b = G.take(dve, ("gq", 0))
            G.give(dve.tensor_scalar(gq[:, 0, :], b, 128 ** -0.5, None, ALU.mult), ("gq", 0))
            mod(13)
            mod(14)
            mod(15)
            b = G.take(dve, "low")
            dve.memset(low[32:33, :], 1.0)
            G.give(dve.tensor_copy(low[0:32, :], b[0:32, :]), "low")
            G.read(dve, "low")
            dve.sem_inc(sem("low_ready"), 1)

            for i in range(8):
                tb, d = i // 2, i % 2
                g = gg[:, tb, d * 512:d * 512 + 512]
                dve.wait_ge(sem("gate_log"), i + 1)
                G.give(dve.scalar_tensor_tensor(g, G.take(dve, ("z", tb, d)), 0.0, g, ALU.min, ALU.subtract), ("z", tb, d))

            def state_keys(tb, d):
                g = gg[:, tb, d * 512:d * 512 + 512]
                G.read(dve, ("aft", tb, d))
                dve.tensor_tensor(g, g, gk[:, tb, :], ALU.mult).then_inc(sem("gla_keys"), 1)

            for tb in range(TB):
                for d in range(2):
                    G.read(dve, ("bc", tb, d))
                    dve.tensor_tensor(gex[:, 0, :], gex[:, 0, :], gq[:, tb, :], ALU.mult).then_inc(sem("gla_scaled"), 1)
                    dve.tensor_tensor(gex[:, 1, :], gex[:, 1, :], gk[:, tb, :], ALU.mult).then_inc(sem("gla_scaled"), 1)
                    b = G.take(dve, ("qe", tb, d))
                    to = qeT[:, d, :].rearrange("p (h t) -> p h t", h=4)[:, :, tb * 128:tb * 128 + 128]
                    G.give(dve.tensor_copy(to, b.rearrange("p (h t) -> p h t", h=4)), ("qe", tb, d))
                    state_keys(tb, d)
            for tb in range(2, 4):
                for d in range(2):
                    state_keys(tb, d)
            decay = small[:, 128:256]
            b = G.take(dve, "dec")
            G.give(dve.tensor_copy(decay, b[:, 0:128]), "dec")
            decay = decay.rearrange("p (h r) -> p h r", h=4)
            masks = cst[:, at["upto64"][0]:at["upto64"][0] + 256]
            dve.wait_ge(sem("gla_keys"), 8)
            for i in range(8):
                b = G.take(dve, ("A", i))
                if i >= 2:
                    dve.wait_ge(sem("gla_masked"), i - 1)
                G.give(dve.tensor_tensor(atM[:, i % 2, :], b[:, 0:256], masks, ALU.mult), ("A", i))
                G.read(dve, ("A", i))
                dve.tensor_tensor(atT[:, i, :], atM[:, i % 2, 0:128], atM[:, i % 2, 128:256],
                                  ALU.add).then_inc(sem("gla_masked"), 1)
            G.read(dve, "dec")
            for s in range(7):
                for d in range(2):
                    pos = (s % 4) if d == 0 else 3 - s % 4
                    row = d * 8 + (4 if s < 4 else 0) + pos
                    b = G.take(dve, ("U", s, d))
                    new, old = st[s % 2][:, d, :], st[(s - 1) % 2][:, d, :]
                    if s >= 6:
                        dve.wait_ge(done, G.number[("I", s - 1, d)])
                    if s == 0:
                        G.give(dve.tensor_copy(new, b), ("U", s, d))
                    else:
                        for h in range(4):
                            r = slice(h * 128, h * 128 + 128)
                            ins = dve.scalar_tensor_tensor(new[:, r], old[:, r], decay[:, h, row:row + 1], b[:, r],
                                                           ALU.mult, ALU.add)
                        G.give(ins, ("U", s, d))
                    G.read(dve, ("U", s, d))
                    dve.sem_inc(sem("gla_state"), 1)
            for hp in range(2):
                G.read(dve, ("gn", hp))
                r = rtg[:, hp, :]
                link(dve.reciprocal(r, r))
                o = o_gla[:, 2 * hp:2 * hp + 2, :].rearrange("p a b -> p (a b)")
                link(dve.scalar_tensor_tensor(o, acc[hp], vc("glan"), r, ALU.mult, ALU.mult))
                dve.tensor_tensor(o, o, grT[:, 2 * hp:2 * hp + 2, :].rearrange("p a b -> p (a b)"),
                                  ALU.mult).then_inc(sem("gla_out"), 1)
            for n in range(KD):
                m = merged[:, n, :]
                G.read(dve, ("gm", n))
                G.give(dve.tensor_tensor(m, G.take(dve, ("bm", n))[:, 0:T], sig[:, 2 * (n % 2), :], ALU.mult), ("bm", n))
                G.read(dve, ("gG", n))
                G.give(dve.tensor_tensor(part[:, n % 2, :], G.take(dve, ("bg", n))[:, 0:T], sig[:, 2 * (n % 2) + 1, :],
                                         ALU.mult), ("bg", n))
                G.read(dve, ("bm", n))
                G.read(dve, ("bg", n))
                dve.tensor_tensor(m, m, part[:, n % 2, :], ALU.add).then_inc(sem("merged"), 1)
            gate = mc(0, 2)
            for n in range(KD):
                b = G.take(dve, ("wo", n))
                G.give(dve.scalar_tensor_tensor(xT[:, n, :], b[:, 0:T], gate[:, n:n + 1], xT[:, n, :], ALU.mult, ALU.add),
                       ("wo", n))
            dve.memset(pad[:, :, :], 0.0).then_inc(sem("pad_cleared"), 1)
            set_gain(2, mc(0, 4), vc("n2", 0, KD))
            for n in range(KD):
                G.read(dve, ("wo", n))
            norm(2, xT, gains(2), hT[:, :, 0:T])
            for j in range(KF):
                G.read(dve, ("ug", j))
                if j >= 3:
                    dve.wait_ge(sem("ff_ready"), j - 2)
                grid = pad[:, j % 3, :].rearrange("p (r c) -> p r c", r=ROWS + 2)
                y = gel[:, j % 3, :].rearrange("p (r c) -> p r c", r=ROWS)
                for i in range(9):
                    win = grid[:, i // 3:i // 3 + ROWS, i % 3:i % 3 + GRID_W]
                    if i == 0:
                        link(dve.tensor_scalar(y, win, tap(0, j), vc("conv_b", j), ALU.mult, ALU.add))
                    else:
                        ins = dve.scalar_tensor_tensor(y, win, tap(i, j), y, ALU.mult, ALU.add)
                        if i < 8:
                            link(ins)
                ins.then_inc(sem("conv_done"), 1)
                if j % 4 == 3 and j > 3:
                    mod(16 + j // 4 - 1)
            mod(20)
            mod(21)
            gate = mc(0, 5)
            dve.wait_ge(done, G.number[("down", 5)])
            for n in range(KD):
                dve.scalar_tensor_tensor(xT[:, n, :], acc[n // 2][:, (n % 2) * T:(n % 2) * T + T], gate[:, n:n + 1],
                                         xT[:, n, :], ALU.mult, ALU.add).then_inc(sem("ff_added"), 1)
            for g in (0, 2):
                evict(("ct", g), xc2T[:, 2 * g:2 * g + 2, :].rearrange("p a b -> p (a b)"))
            dve.wait_ge(sem("ff_added"), KD)
            norm(3, xT, vc("fin", 0, KD), xT)
            set_gain(3, mc(1, 1), vc("n1_2", 0, KD))
            set_gain(4, mc(1, 1, 1), vc("n1_2", 0, KD))
            dve.wait_ge(sem("scaled"), KD * 4)
            norm(4, xT, gains(3), hT[:, :, 0:T])
            G.read(dve, ("ct", 1))
            G.read(dve, ("ct", 3))
            norm(5, xc2T, gains(4), hT[:, :, T:2 * T])
            dve.wait_ge(done, G.number[("ms", 5)])
            dve.wait_ge(sem("scaled"), KD * 6)
            dve.memset(raw[:, :, :], 0.0).then_inc(sem("raw_cleared"), 1)
            for i in range(8):
                n = (i + 4) % 8
                G.read(dve, ("eq", n))
                s = 2 if n >= 4 else 1
                x = raw[:, i % 3, :].rearrange("p (s t) -> p s t", s=2)[:, 0:s]
                y = qk[:, n, 0:s * T].rearrange("p (s t) -> p s t", s=s)
                link(dve.tensor_scalar(y, x[:, :, 0:T], vc("w_conv", n), None, ALU.mult))
                link(dve.scalar_tensor_tensor(y, x[:, :, 1:T + 1], vc("w_conv", 8 + n), y, ALU.mult, ALU.add))
                dve.scalar_tensor_tensor(y, x[:, :, 2:T + 2], vc("w_conv", 16 + n), y, ALU.mult,
                                         ALU.add).then_inc(sem("conv2_done"), 1)
            for tb in (0, 2):
                evict(("ekv", tb), e_kv[:, tb, :], 256)
            dve.wait_ge(sem("heads_in"), 48)
            for tb in range(4):
                b = G.take(dve, ("egt", tb))
                G.give(dve.tensor_tensor(m_gt[:, tb, :], b[:, 0:16], small[:, 112:128], ALU.add), ("egt", tb))
            G.read(dve, ("egt", 3))
            dve.sem_inc(sem("m_biased"), 1)
            evict(("eqa", 0), e_qa[:, 0, :])
            for name in [("ekv", tb) for tb in range(4)] + [("eqa", 0), ("eqa", 1)]:
                G.read(dve, name)
            tmp = small[:, 128:640]

            def heads(x, n):
                return x.rearrange("p (h c) -> p h c", h=n)

            def head_squares(x, n, to):
                link(dve.tensor_tensor(tmp[:, 0:n * A_D], x, x, ALU.mult))
                link(dve.tensor_reduce(to, heads(tmp[:, 0:n * A_D], n), AX.X, ALU.add))

            for tb in range(4):
                head_squares(e_kv[:, tb, 0:128], A_KV, small[:, 8 + 2 * tb:10 + 2 * tb])
            for tb in range(TB):
                head_squares(e_qa[:, tb, :], A_H, small[:, 16 + 8 * tb:24 + 8 * tb])
            dve.sem_inc(sem("heads_squared"), 1)
            dve.wait_ge(sem("heads_root"), 1)
            link(dve.reciprocal(small[:, 8:32], small[:, 8:32]))

            def head_scale(x, n, r, g):
                v = heads(x, n)
                link(dve.tensor_tensor(v, v, r.unsqueeze(2).to_broadcast([128, n, A_D]), ALU.mult))
                link(dve.tensor_tensor(v, v, g.unsqueeze(1).to_broadcast([128, n, A_D]), ALU.mult))

            def halves(x, n):
                return x.rearrange("p (n x h q) -> p n x h q", n=n, x=2, h=2)

            for tb in range(4):
                head_scale(e_kv[:, tb, 0:128], A_KV, small[:, 8 + 2 * tb:10 + 2 * tb], small[:, 704:768])
                if tb < TB:
                    v = halves(e_kv[:, tb, 0:128], A_KV)
                    link(rope(v, v, "rope64", tb, tmp, A_KV, 16))
            for tb in range(TB):
                head_scale(e_qa[:, tb, :], A_H, small[:, 16 + 8 * tb:24 + 8 * tb], small[:, 640:704])
                for g in range(2):
                    v = halves(e_qa[:, tb, g * 256:g * 256 + 256], 4)
                    link(rope(v, v, "rope64", tb, tmp, 4, 16))
            dve.sem_inc(sem("heads_ready"), 1)
            G.give(dve.tensor_copy(e_kT[0:A_D, 0, :], G.take(dve, ("ekT", 0))[0:A_D, :]), ("ekT", 0))
            for hp in (0, 2):
                G.give(dve.tensor_copy(e_qT[0:A_D, 2 * hp:2 * hp + 2, :].rearrange("p a b -> p (a b)"),
                                       G.take(dve, ("eqT", hp))[0:A_D, :]), ("eqT", hp))
            attend("gqa", A_H, A_D ** -0.5, e_prob, e_probT, e_oT,
                   lambda i: mod(22 + i // 2 - 1) if i % 2 == 0 and i else None)
            dve.memset(v1[:, :, :], 1.0).then_inc(sem("v1_set"), 1)
            dve.wait_ge(sem("v1_set"), 1)
            for tb in (0, 2):
                b = G.take(dve, ("evb", tb))
                G.give(dve.tensor_copy(v1[:, tb, :].rearrange("p (h c) -> p h c", h=4)[:, :, 1:129],
                                       b.rearrange("p (h c) -> p h c", h=4)), ("evb", tb))
            dve.wait_ge(sem("m_log"), 1)
            f = gsm[:, 0:64].rearrange("p (x y) -> p x y", x=8)[:, :, 4:8]
            lf = gsm[:, 64:96].rearrange("p (x y) -> p x y", x=8)
            ln = gsm[:, 224:256].rearrange("p (x y) -> p x y", x=8)
            dve.scalar_tensor_tensor(lf, f, 0.0, ln, ALU.min, ALU.subtract).then_inc(sem("m_gates"), 1)

            def pair(v):
                return v.rearrange("p (d h) -> p d h", d=2)

            for tb in range(4):
                b = G.take(dve, ("eb", tb))
                dve.tensor_copy(m_b[:, tb, :], b[:, 0:8])
                G.give(dve.tensor_copy(m_end[:, tb, :], b[:, 8:16]), ("eb", tb))
                G.read(dve, ("eb", tb))
                i_gate = m_gt[:, tb, :].rearrange("p (d y) -> p d y", d=2)[:, :, 0:4]
                dve.tensor_tensor(pair(m_r[:, tb, :]), i_gate, pair(m_b[:, tb, :]), ALU.subtract).then_inc(sem("m_r"), 1)
            for tb in (0, 2):
                evict(("ekt", tb), ktm[:, tb, :])
            for tb in (2, 3, 1, 0):
                for d in range(2):
                    b = G.take(dve, ("eR", tb, d))
                    v = b.rearrange("p (h s) -> p h s", h=4)
                    ins = dve.tensor_reduce(m_top[:, tb, d * 4:d * 4 + 4], v, AX.X, ALU.max)
                    if tb < TB:
                        bar = c_(("bar_later", "bar_earlier")[d]).unsqueeze(1).to_broadcast([128, 4, 128])
                        ins = dve.tensor_tensor(dmx[tb][:, d * 4:d * 4 + 4, :], v, bar, ALU.add)
                    G.give(ins, ("eR", tb, d))
            G.read(dve, ("eR", 0, 0))
            G.read(dve, ("eR", 0, 1))
            G.read(dve, ("ekt", 1))
            G.read(dve, ("ekt", 3))
            mod(29)
            for j in range(3):
                for d in range(2):
                    tb, c = BLOCKS[d][j], slice(4 * d, 4 * d + 4)
                    m, top, x = m_m[:, j, c], m_top[:, tb, c], m_x[:, 2 * j + d, :]
                    mx = top
                    if j:
                        mx = m_mx[:, c]
                        link(dve.tensor_tensor(mx, m, top, ALU.max))
                        dve.tensor_tensor(x[:, 4:8], m, mx, ALU.subtract)
                    dve.tensor_tensor(x[:, 0:4], m_r[:, tb, c], mx, ALU.subtract).then_inc(sem("m_args"), 1)
                    link(dve.tensor_tensor(m_m[:, j + 1, c], m_end[:, tb, c], mx, ALU.add))
                for d in range(2):
                    tb, x = BLOCKS[d][j], m_x[:, 2 * j + d, :]
                    dve.wait_ge(sem("m_exps"), 2 * j + d + 1)
                    if j:
                        dve.wait_ge(done, G.number[("eU", j - 1, d, 1)])
                    for h in range(4):
                        ins = dve.tensor_scalar(kw[:, d * 4 + h, :], ktm[:, tb, h * 128:h * 128 + 128], x[:, h:h + 1],
                                                128 ** -0.5, ALU.mult, ALU.mult)
                    ins.then_inc(sem("m_keys"), 1)
                for d in range(2):
                    to = cn[1 - d] if j == 2 else cn[d]
                    x = m_x[:, 2 * j + d, :]
                    for hp in range(2):
                        b = G.take(dve, ("eU", j, d, hp))
                        for h in (2 * hp, 2 * hp + 1):
                            new, old = to[:, h, 129 * d:129 * d + 129], cn[d][:, h, 129 * d:129 * d + 129]
                            u = b[:, (h % 2) * 129:(h % 2) * 129 + 129]
                            if j:
                                ins = dve.scalar_tensor_tensor(new, old, x[:, 4 + h:5 + h], u, ALU.mult, ALU.add)
                            else:
                                ins = dve.tensor_copy(new, u)
                        G.give(ins, ("eU", j, d, hp))
                        G.read(dve, ("eU", j, d, hp))
                        dve.sem_inc(sem("m_state"), 1)
                if j < 2:
                    mod(30 + j)
            for tb in (1, 0):
                n = 2 - tb
                ms = [m_m[:, 2 + tb, 0:4], m_m[:, 3 - tb, 4:8]]
                link(dve.tensor_reduce(m_M, dmx[tb], AX.X, ALU.max))
                for d in range(2):
                    c = slice(4 * d, 4 * d + 4)
                    link(dve.tensor_tensor(m_M[:, c], m_M[:, c], ms[d], ALU.max))
                    dve.tensor_tensor(m_in[:, c], ms[d], m_M[:, c], ALU.subtract)
                link(dve.tensor_tensor(m_em, m_b[:, tb, :], m_M, ALU.add))
                link(dve.tensor_scalar(m_em, m_em, -1.0, None, ALU.mult))
                dve.tensor_tensor(dmx[tb], dmx[tb], m_M.unsqueeze(2).to_broadcast([128, 8, 128]),
                                  ALU.subtract).then_inc(sem("m_shifted"), 1)
                for h in range(4):
                    b = G.take(dve, ("eC", tb, h))
                    link(dve.tensor_copy(pair(m_nq)[:, :, h], b[:, 128:130]))
                mod(32 if tb else 33)
                dve.wait_ge(sem("m_wexp"), n)
                b = G.take(dve, ("eS", tb))
                for d in range(2):
                    v = wm[:, 4 * d:4 * d + 4, :].rearrange("p a b -> p (a b)")
                    ins = dve.scalar_tensor_tensor(v, b, 128 ** -0.5, v, ALU.mult, ALU.mult)
                G.give(ins, ("eS", tb))
                G.read(dve, ("eS", tb))
                link(dve.tensor_reduce(m_sum, wm[:, :, :], AX.X, ALU.add))
                link(dve.tensor_tensor(m_nq, m_nq, m_in, ALU.mult))
                link(dve.tensor_tensor(m_den, m_nq, m_sum, ALU.add))
                link(dve.scalar_tensor_tensor(m_den, m_den, -1.0, m_den, ALU.mult, ALU.max))
                link(dve.tensor_tensor(m_den, m_den, m_em, ALU.max))
                link(dve.reciprocal(m_den, m_den))
                dve.tensor_tensor(m_wr, m_in, m_den, ALU.mult)
                link(dve.tensor_tensor(wm[:, :, :], wm[:, :, :], m_den.unsqueeze(2).to_broadcast([128, 8, 128]), ALU.mult))
                link(dve.tensor_tensor(wm[:, 0:4, :], wm[:, 0:4, :], wm[:, 4:8, :], ALU.add))
                dve.sem_inc(sem("m_weights"), 1)
                for d in range(2):
                    for h in range(4):
                        b = G.take(dve, ("eC", tb, h))
                        q, r = b[:, 130 * d:130 * d + 128], m_wr[:, 4 * d + h:4 * d + h + 1]
                        if d == 0:
                            ins = dve.tensor_scalar(h_e[:, h, :], q, r, None, ALU.mult)
                            if h == 3:
                                link(ins)
                        else:
                            G.give(dve.scalar_tensor_tensor(h_e[:, h, :], q, r, h_e[:, h, :], ALU.mult, ALU.add),
                                   ("eC", tb, h))
                for h in range(4):
                    G.read(dve, ("eC", tb, h))
                b = G.take(dve, ("eH", tb))
                v = h_e[:, :, :].rearrange("p a b -> p (a b)")
                G.give(dve.tensor_tensor(v, b, v, ALU.add), ("eH", tb))
                G.read(dve, ("eH", tb))
                sqv = wm[:, 4:8, :]
                link(dve.tensor_tensor(sqv, h_e[:, :, :], h_e[:, :, :], ALU.mult))
                dve.tensor_reduce(m_ss[:, 0:4], sqv, AX.X, ALU.add).then_inc(sem("m_hsq"), 1)
                if tb == 0:
                    mod(34)
                dve.wait_ge(sem("m_hroot"), n)
                link(dve.reciprocal(m_ss[:, 0:4], m_ss[:, 0:4]))
                dve.tensor_tensor(h_e[:, :, :], h_e[:, :, :], m_ss[:, 0:4].unsqueeze(2).to_broadcast([128, 4, 128]),
                                  ALU.mult).then_inc(sem("m_out"), 1)
                b = G.take(dve, ("eT", tb))
                for h in range(4):
                    ins = dve.scalar_tensor_tensor(e_mT[:, h, tb * 128:tb * 128 + 128], b[:, h * 128:h * 128 + 128],
                                                   vc("hn", h), e_ob[:, h, tb * 128:tb * 128 + 128], ALU.mult, ALU.mult)
                G.give(ins, ("eT", tb))
                G.read(dve, ("eT", tb))
            mod(35)

            def add_output(tag, gate):
                for n in range(KD):
                    b = G.take(dve, (tag, n))
                    G.give(dve.scalar_tensor_tensor(xT[:, n, :], b[:, 0:T], gate[:, n:n + 1], xT[:, n, :], ALU.mult,
                                                    ALU.add), (tag, n))
                for n in range(KD):
                    G.read(dve, (tag, n))

            add_output("eo", mc(1, 2))

            def output():
                for j in (0, 2):
                    evict(("out", j), x_tm[:, j // 2, 0:512])

            def experts(layer, c):
                set_gain(c - 1 - layer, mc(1 + layer, 4), vc("n2_2", KD * layer, KD))
                norm(c, xT, gains(c - 1 - layer), hT[:, :, 0:T])
                for j in (0, 2):
                    evict(("ht", layer, j), h_tm[:, j // 2, 0:512])
                for tb in range(TB):
                    b = G.take(dve, ("lg", layer, tb))
                    dve.tensor_reduce(small[:, 32 + tb:33 + tb], b[:, 0:N_EXP], AX.X, ALU.max,
                                      negate=True).then_inc(sem("router_max"), 1)
                for tb in range(TB):
                    dve.wait_ge(sem("router_exp"), 2 * layer + tb + 1)
                    r = small[:, 64 + tb:65 + tb]
                    G.give(dve.reciprocal(r, r), ("lg", layer, tb))
                    G.read(dve, ("lg", layer, tb))
                    link(dve.tensor_scalar(aff[:, tb, :], aff[:, tb, :], r, None, ALU.mult))
                    dve.sem_inc(sem("affinity"), 1)
                wk = work[0:N_EXP, :]
                b = G.take(dve, ("aT", layer))
                G.give(dve.tensor_copy(wk, b[0:N_EXP, 0:T]), ("aT", layer))
                G.read(dve, ("aT", layer))
                for _ in range(CAP // 8):
                    link(dve.max(top8, wk))
                    link(dve.match_replace(wk, top8, wk, -1.0))
                dve.tensor_scalar(mask_e[0:N_EXP, :], wk, 0.0, None, ALU.is_lt).then_inc(sem("chosen"), 1)
                b = G.take(dve, ("mT", layer))
                G.give(dve.tensor_copy(mask_t.rearrange("p b e -> p (b e)"), b[:, 0:32]), ("mT", layer))
                G.read(dve, ("mT", layer))
                b = G.take(dve, ("cs", layer))
                v = turn_of.rearrange("p b e -> p (b e)")
                G.give(dve.tensor_tensor(v, b[:, 0:32], mask_t.rearrange("p b e -> p (b e)"), ALU.mult), ("cs", layer))
                G.read(dve, ("cs", layer))
                link(dve.tensor_scalar(v, v, -1.0, None, ALU.add))
                hots = [hot[:, tb, :].rearrange("p (e c) -> p e c", e=N_EXP) for tb in range(TB)]
                for tb in range(TB):
                    ins = dve.tensor_tensor(hots[tb], c_("slot_numbers").unsqueeze(1).to_broadcast([128, N_EXP, CAP]),
                                            turn_of[:, tb, :].unsqueeze(2).to_broadcast([128, N_EXP, CAP]), ALU.is_equal)
                link(ins)
                dve.sem_inc(sem("one_hot"), 1)
                for tb in range(TB):
                    ins = dve.tensor_tensor(hotg[:, tb, :].rearrange("p (e q c) -> p e q c", e=N_EXP, q=4),
                                            hots[tb].unsqueeze(2).to_broadcast([128, N_EXP, 4, CAP]),
                                            aff[:, tb, :].unsqueeze(2).unsqueeze(3).to_broadcast([128, N_EXP, 4, CAP]),
                                            ALU.mult)
                ins.then_inc(sem("gated_hot"), 1)
                for k in range(0, KD, 2):
                    evict(("xs", layer, k), xsel[:, k, :])
                for e2 in range(0, N_EXP // 2, 2):
                    evict(("gT", layer, e2), gates_flat[:, e2 * 512:e2 * 512 + 512])
                base = moe_base[layer]
                with dve.Fori(0, N_EXP) as e:
                    dve.wait_ge(sem("silu_ready"), e + (N_EXP * layer + 1))
                    t = bank[1].rearrange("p (j c) -> p j c", j=4)
                    to = act_t.rearrange("p (h j) c -> p j h c", h=2)
                    dve.tensor_tensor(to, sil.rearrange("p (j h) c -> p j h c", h=2),
                                      t[:, :, 64:128].rearrange("p j (h c) -> p j h c", h=2),
                                      ALU.mult).then_inc(sem("act_ready"), 1)
                    dve.wait_ge(done, e * 4 + (base + 3))
                    dve.tensor_copy(dsb[:, 0, :], bank[2]).then_inc(sem("down_copied"), 1)
                gate = mc(1 + layer, 5)
                dve.wait_ge(done, base + 4 * N_EXP)
                for n in range(KD):
                    dve.scalar_tensor_tensor(xT[:, n, :], acc[n // 2][:, (n % 2) * T:(n % 2) * T + T], gate[:, n:n + 1],
                                             xT[:, n, :], ALU.mult, ALU.add).then_inc(sem("moe_added"), 1)
                dve.wait_ge(sem("moe_added"), KD * (layer + 1))

            experts(0, 6)
            set_gain(6, mc(2, 1), vc("n1_2", KD, KD))
            link(dve.tensor_tensor(gains(0), mc(2, 2), vc("s_pool", 0, KD), ALU.mult))
            norm(7, xT, gains(6), hT[:, :, 0:T])
            for tb in range(TB):
                evict(("u", tb, 0), u_tm[:, tb, 0:512])
            for c in range(0, KD, 2):
                evict(("p", c), pT[:, c, :], T)
            add_output("y", gains(0))
            experts(1, 8)
            norm(9, xT, vc("fin2", 0, KD), xT)
            output()

        @block.gpsimd
        def _(pool):
            for j in range(KF):
                pool.wait_ge(sem("gelu_done"), j + 1)
                nc.gpsimd.tensor_tensor(ff[:, j, :], ff[:, j, :], gel[:, j % 3, :], ALU.mult).then_inc(sem("ff_ready"), 1)
            def experts(layer):
                for k in range(KD):
                    G.read(pool, ("xs", layer, k))
                base = moe_base[layer]
                pairs = xe
                flat = xsel

                def take(par, sel):
                    nc.gpsimd.tensor_copy(pairs[:, par, :].rearrange("p (k c) -> p k c", k=KD),
                                          sel).then_inc(sem("rows_ready"), 1)

                for par in range(2):
                    take(par, flat[:, :, par * CAP:(par + 1) * CAP])
                with pool.Fori(1, N_EXP // 2) as pair:
                    for par in range(2):
                        pool.wait_ge(done, pair * 8 + (base + 4 * par - 7))
                        take(par, flat[:, :, bass.ds(pair * (2 * CAP) + par * CAP, CAP)])

            experts(0)
            experts(1)


NAMES = [
    "x", "c", "ctx", "c_ctx", "w_ada", "b_ada", "norm1_g", "w_in", "q_norm_g", "w_uq", "kv_norm_g", "w_ukv",
    "gla_w_decay", "gla_b_decay", "gla_norm_g", "w_br_mla", "w_br_gla", "w_out", "norm2_g", "w_up", "conv_w",
    "conv_b", "w_down", "final_g", "c_2", "ctx_2", "c_ctx_2", "w_mod_2", "b_mod_2", "g_norm1_2", "g_norm2_2",
    "w_in_even_2", "w_out_even_2", "g_qnorm_2", "g_knorm_2", "w_conv_2", "b_gate_2", "g_hnorm_2", "w_in_odd_2",
    "w_pool_grp_2", "s_pool_2", "w_router_2", "w_exp_gate_2", "w_exp_up_2", "w_exp_down_2", "g_final_2",
]


def kernel(**inputs):
    import numpy as _np
    import concourse.bacc as _bacc
    from concourse.bass_utils import run_bass_kernel_spmd as _run

    nc = _bacc.Bacc("TRN2", target_bir_lowering=False, num_devices=1)
    arrays, w = {}, {}
    table, at = shape_tables()
    for name, a in [(n, inputs[n]) for n in NAMES] + [("tables", table), ("pool", pool_table())]:
        a = _np.ascontiguousarray(a)
        arrays[f"in_{name}_dram"] = a
        w[name] = nc.dram_tensor(f"in_{name}_dram", a.shape, mybir.dt.from_np(a.dtype), kind="ExternalInput").ap()
    out = nc.dram_tensor("out_0_dram", (1, T, D), F32, kind="ExternalOutput").ap()
    build(nc, w, (table, at), out)
    r = _run(nc, [arrays], core_ids=[0])
    return r.results[0]["out_0_dram"]
```

```python
from contextlib import ExitStack

import numpy as np

import concourse.bass as bass
from concourse import mybir

F32 = mybir.dt.float32
ACT = mybir.ActivationFunctionType
ALU = mybir.AluOpType
AX = mybir.AxisListType

D = 1024
KD = D // 128
T = 256
TB = T // 128
GRID_W = 64
ROWS = T // GRID_W
EPS = 1e-6
Q_LORA, KV_LORA, ROPE = 384, 256, 32
MLA_H, NOPE, VH = 8, 64, 64
QH = NOPE + ROPE
GH = 4
GCH = 64
D_FF = 2816
KF = D_FF // 128
A_H, A_KV, A_D = 8, 2, 64
B_H = 4
N_EXP, CAP = 16, 32

IN_KV, IN_GQ, IN_GK, IN_GV, IN_GR, IN_LOW, IN_GATE = 384, 672, 1184, 1696, 2208, 2720, 2752
EV_KA, EV_QB, EV_VB, EV_OB, EV_GT = 512, 768, 1792, 2304, 2816

MLA_FILL = {1: ("gk", 0), 3: ("gk", 1), 5: ("gk", 2), 7: ("gk", 3), 9: ("gv", 0), 11: ("gv", 1), 13: ("gv", 2)}
GQA_FILL = {3: 0, 5: 1, 7: 2, 9: 3}

CTX_NORM = 12

SLOTS = 6
SLOT = 4096
RING = 4


def shape_tables():
    s, t = np.arange(128)[:, None], np.arange(128)[None, :]
    same = (s // GCH) == (t // GCH)
    parts, at = [], {}

    def add(name, a):
        a = np.asarray(a, np.float32).reshape(128, -1)
        at[name] = (sum(p.shape[1] for p in parts), a.shape[1])
        parts.append(a)

    add("ident", s == t)
    add("ones", np.ones((128, 128)))
    add("upto64", same & (s <= t))
    add("from64", same & (s >= t))
    add("sum_upto64", (same & (s <= t)) / 16.0)
    add("sum_from64", (same & (s >= t)) / 16.0)
    add("sum_after64", (same & (s > t)) / 16.0)
    add("sum_before64", (same & (s < t)) / 16.0)
    add("upto128", s <= t)
    add("from128", s >= t)
    add("bar_later", np.where(t > s, -1e30, 0.0))
    add("bar_earlier", np.where(t < s, -1e30, 0.0))
    pick = np.zeros((128, 2, 4, 32), np.float32)
    for d in range(2):
        for tb in range(4):
            for c in range(2):
                pick[c * 64:(c + 1) * 64, d, tb, d * 8 + tb * 2 + c] = 1 / 16.0
    add("chunk_pick", pick)
    add("slot_numbers", np.broadcast_to(np.arange(CAP, dtype=np.float32), (128, CAP)))
    tok = np.arange(T).reshape(TB, 128)
    for name, dim in (("rope32", ROPE), ("rope64", A_D)):
        half = dim // 2
        inv = np.float32(10000.0) ** (-np.arange(0, half, 2, dtype=np.float32) / np.float32(half))
        ang = np.stack([(tok // GRID_W)[..., None] * inv, (tok % GRID_W)[..., None] * inv], 2).astype(np.float32)
        both = np.stack([np.cos(ang), np.sin(ang)], 1)
        add(name, both.transpose(2, 0, 1, 3, 4))
    return np.concatenate(parts, 1), at


VECTORS = (
    (0, "b_ada"), (0, "norm1_g"), (0, "norm2_g"), (0, "q_norm_g"), (0, "kv_norm_g"), (0, "gla_norm_g"), (0, "conv_b"),
    (0, "c"), (0, "c_ctx"), (0, "s_pool_2"), (0, "g_hnorm_2"),
    (1, "b_mod_2"), (1, "c_2"), (1, "c_ctx_2"), (1, "g_norm1_2"),
    (3, "w_conv_2"), (3, "g_norm2_2"), (3, "final_g"), (3, "g_final_2"),
)


def vector_rows(inputs):
    rows, vat, tiles = np.zeros((128, 4 * 128), np.float32), {}, [0, 0, 128, 9 * KF - 128]
    taps = np.reshape(inputs["conv_w"], (9 * KF, 128))
    rows[:, 256:384] = taps[0:128]
    rows[0:tiles[3], 384:512] = taps[128:]
    for t, name in VECTORS:
        a = np.reshape(inputs[name], (-1, 128))
        rows[tiles[t]:tiles[t] + len(a), 128 * t:128 * t + 128] = a
        vat[name] = (t, tiles[t], len(a))
        tiles[t] += len(a)
    return rows, vat, tiles


def pool_table():
    m = np.zeros((T, 4, T), np.float32)
    for g, w in enumerate((2, 4, 8, 16)):
        lo, hi = w // 2, w - 1 - w // 2
        for t in range(T):
            a, e = max(t - lo, 0), min(t + hi, T - 1)
            m[a:e + 1, g, t] = 1.0 / (e - a + 1)
            m[t, g, t] -= 1.0
    return m.reshape(TB, 128, 4 * T)


class Groups:

    def __init__(self, banks, done, freed):
        self.banks, self.done, self.freed = banks, done, freed
        self.count, self.turns, self.number, self.bank, self.use, self.last_user = 0, [0, 0], {}, {}, {}, {}

    def open(self, pe, name, second=False):
        turn = self.turns[second]
        b, use = turn % RING + RING * second, turn // RING
        self.turns[second] += 1
        if use:
            pe.wait_ge(self.freed[b], use)
        self.bank[name], self.use[name] = b, use
        return self.banks[b]

    def close(self, ins, name):
        ins.then_inc(self.done, 1)
        self.count += 1
        self.number[name] = self.count

    def over(self, *items):
        for item in items:
            self.last_user[item] = self.count

    def take(self, eng, name):
        eng.wait_ge(self.done, self.number[name])
        return self.banks[self.bank[name]] if name in self.bank else None

    def drain(self, eng, b):
        uses = (self.turns[0] - b + RING - 1) // RING
        eng.wait_ge(self.freed[b], uses)

    def read(self, eng, name):
        eng.wait_ge(self.freed[self.bank[name]], self.use[name] + 1)

    def give(self, ins, name):
        ins.then_inc(self.freed[self.bank[name]], 1)


def weight_items(w):
    items = []

    def cols(key, a, c0, n, k=KD):
        items.append((key, [((0, k * n), k, a[0:k * 128, c0:c0 + n].rearrange("(k p) n -> p k n", p=128))]))

    def rows(key, a, r0, k, n=D):
        items.append((key, [((0, k * n), k, a[r0:r0 + k * 128, :].rearrange("(k p) n -> p k n", p=128))]))

    def mod(i):
        src = w["w_ada"][0] if i < 12 else w["w_mod_2"][0] if i < 24 else w["w_mod_2"][1]
        cols(("mod", i), src, (i % 12) * 512, 512)

    mods = iter(range(36))
    for _ in range(4):
        mod(next(mods))
    w_in = w["w_in"][0]
    cols("kvr", w_in, IN_KV, IN_GQ - IN_KV)
    cols("w_ukv", w["w_ukv"][0], 0, 1024, 2)
    cols("qc", w_in, 0, Q_LORA)
    cols("w_uq", w["w_uq"][0], 0, MLA_H * QH, 3)
    for j in range(MLA_H):
        mod(next(mods))
        if j == 0:
            cols("gk", w_in, IN_GK, 512)
        if j == 4:
            cols("gv", w_in, IN_GV, 512)
    cols("gq", w_in, IN_GQ, 512)
    for _ in range(2):
        mod(next(mods))
    cols("low", w_in, IN_LOW, 32)
    cols("gr", w_in, IN_GR, 512)
    for _ in range(2):
        mod(next(mods))
    for g in range(2):
        cols(("gate_mla", g), w_in, IN_GATE + 512 * g, 512)
        cols(("gate_gla", g), w_in, IN_GATE + D + 512 * g, 512)
        if g == 0:
            rows("w_br_mla", w["w_br_mla"][0], 0, 4)
            rows("w_br_gla", w["w_br_gla"][0], 0, 4)
    for g in range(2):
        rows(("w_out", g), w["w_out"][0], 512 * g, 4)
    for g in range(6):
        n = min(512, D_FF - 512 * g)
        cols(("up_gate", g), w["w_up"][0], D_FF + 512 * g, n)
        cols(("up_val", g), w["w_up"][0], 512 * g, n)
        mod(next(mods))
    for g in range(6):
        rows(("down", g), w["w_down"][0], 512 * g, min(4, KF - 4 * g))
    even = w["w_in_even_2"][0]
    cols("e_k", even, EV_QB + 512, 512)
    cols("e_kv", even, EV_KA, 256)
    cols("e_gt", even, EV_GT, 16)
    cols("e_qa", even, 0, 512)
    cols("e_ob", even, EV_OB, 512)
    for j in range(A_H):
        mod(next(mods))
        if j == 0:
            cols("e_q", even, EV_QB, 512)
    cols("e_vb", even, EV_VB, 512)
    for i in mods:
        mod(i)
    for g in range(2):
        rows(("e_out", g), w["w_out_even_2"][0], 512 * g, 4)
    cols(("router", 0), w["w_router_2"][0], 0, N_EXP)
    between = []
    mine, items = items, between
    for g in range(2):
        cols(("o_in", g), w["w_in_odd_2"][0], 512 * g, 512)
    items.append(("pool", [((0, TB * 4 * T), TB, w["pool"].rearrange("b p n -> p b n"))]))
    groups = w["w_pool_grp_2"][0].rearrange("g c e -> (g c) e")
    cols("w_grp", groups, 0, 256)
    cols(("router", 1), w["w_router_2"][1], 0, N_EXP)
    return mine, between


def build(nc, w, consts, out):
    table, at, vat, tiles = consts
    before, between = weight_items(w)
    ctx = ExitStack()
    with ctx:
        def sb(name, shape):
            return ctx.enter_context(nc.sbuf_tensor(name, shape, F32))[:]

        sems = {}

        def sem(name):
            if name not in sems:
                sems[name] = ctx.enter_context(nc.semaphore(name))
            return sems[name]

        ring = sb("ring", [128, SLOTS * SLOT])
        cst = sb("cst", [128, table.shape[1]])
        vcol = sb("vcol", [128, 512])
        modc = sb("modc", [128, 3 * 96])
        cond = sb("cond", [128, 2, KD, 32])
        mrow = sb("mrow", [128, 512])
        gain = sb("gain", [128, 8 * KD])
        rs = sb("rs", [128, T])
        xT = sb("xT", [128, KD, T])
        hT = sb("hT", [128, KD, 2 * T])
        small = sb("small", [128, 768])
        AR = 17536
        arena = sb("arena", [128, AR])
        bank = [ctx.enter_context(nc.psum_tensor(f"bank{i}", [128, 512], F32))[:, :] for i in range(8)]
        acc = bank[RING:]

        def c_(name, lo=0, n=None):
            a, k = at[name]
            return cst[:, a + lo:a + lo + (n or k)]

        ident, ones = c_("ident"), c_("ones")

        def ar(off, *shape):
            n = int(np.prod(shape))
            assert off + n <= AR, (off, shape)
            v = arena[:, off:off + n]
            if len(shape) == 2:
                v = v.rearrange("p (a b) -> p a b", a=shape[0])
            if len(shape) == 3:
                v = v.rearrange("p (a b c) -> p a b c", a=shape[0], b=shape[1])
            return v

        def vc(name, lo=0, n=1):
            t, r, _ = vat[name]
            return vcol[:, 128 * t + r + lo:128 * t + r + lo + n]

        def tap(i, j):
            r = i * KF + j
            return vcol[:, 256 + r:257 + r]

        def mc(which, part, r=0, lo=0, n=KD):
            v = modc[:, 96 * which:96 * which + 96].rearrange("p (j r) -> p j r", r=2)
            return v[:, KD * part + lo:KD * part + lo + n, r]

        def gains(i):
            return gain[:, KD * i:KD * i + KD]

        x_tm = ar(0, 4, D)
        xcT = ar(4096, KD, T)
        vrow = ar(6144, 512)
        sq = ar(AR - 2048, KD, T)
        kvr = ar(0, 4, 288)
        qc = ar(1152, 2, Q_LORA)
        qcT = ar(1920, 3, T)
        kvT = ar(2688, 2, 512)
        q_tm = ar(3712, TB, MLA_H * QH)
        v_tm = ar(5248, 4, MLA_H * VH)
        kcat = ar(7296, 4, MLA_H * QH)
        qT = ar(10368, MLA_H, T)
        kT = ar(12416, MLA_H, 512)
        prob = ar(3712, 2, 512)
        probT = ar(7296, 2, 4 * T)
        o_mla = ar(16512, 4, T)
        gk = ar(0, 4, 512)
        gv = ar(2048, 4, 512)
        gq = ar(4096, 2, 512)
        grT = ar(5120, 4, T)
        gg = ar(6144, 4, 1024)
        gex = ar(10240, 2, 512)
        wdec = ar(11264, 1024)
        qeT = ar(11264, 2, 4 * T)
        keT = ar(13312, 2, 4 * T)
        low = ar(15360, 512)
        dtm = ar(15872, 512)
        st = [ar(15360, 2, 512), ar(10240, 2, 512)]
        atT = ar(0, 8, 128)
        atM = ar(1024, 2, 256)
        o_gla = ar(4096, 4, T)
        sqg = ar(11264, 2, 512)
        rtg = ar(13312, 2, 512)
        merged = ar(8192, KD, T)
        sig = ar(10240, 4, T)
        part = ar(11264, 2, T)
        ff = ar(0, KF, T)
        pad = ar(5632, 3, 6 * 66)
        gel = ar(7168, 3, T)
        e_oT = ar(0, 4, T)
        e_mT = ar(1024, 4, T)
        e_qa = ar(2048, TB, 512)
        e_kv = ar(3072, 4, 256)
        e_qT = ar(4096, A_H, T)
        e_kT = ar(6144, A_KV, 512)
        e_prob = ar(7168, 2, 512)
        e_probT = ar(8192, 2, 4 * T)
        raw = ar(10240, 3, 2 * 258)
        qk = ar(11840, KD, 512)
        e_ob = ar(15936, 4, T)
        v1 = ar(2048, 4, 4 * 130)
        cn = [ar(4128, 4, 258), ar(5160, 4, 258)]
        kw = ar(6192, 8, 128)
        ktm = ar(7216, 4, 512)
        dm = ar(9264, 8, 128)
        wm = ar(10288, 8, 128)
        h_e = ar(11312, 4, 128)
        h_tm = ar(0, TB, D)
        hot = ar(6144, TB, N_EXP * CAP)
        hot_flat = ar(6144, TB * N_EXP * CAP)
        gates = ar(7168, N_EXP, T)
        hotg = ar(11264, TB, 4 * 512)
        gu = ar(11264, 512)
        act_t = ar(11776, 8, CAP)
        sil = ar(12032, 8, CAP)
        dsb = ar(12288, 2, 512)
        xe = ar(15360, KD * CAP)
        row_parts = ar(2048, 512)
        gsm = ar(16960, 576)
        xc2 = ar(8192, TB, D)
        xc2T = ar(10240, KD, T)
        u_tm = ar(0, TB, D)
        pT = ar(2048, KD, T)

        eps, one = small[:, 0:1], small[:, 1:2]
        junk = small[:, 384:768]
        nul = small[:, 2:4]
        m_gt = gsm[:, 0:64].rearrange("p (b c) -> p b c", b=4)
        m_lf, m_b, m_r, m_end, m_top, m_ln = (
            gsm[:, 64 + 32 * i:96 + 32 * i].rearrange("p (b c) -> p b c", b=4) for i in range(6))
        m_m = gsm[:, 256:288].rearrange("p (j c) -> p j c", j=4)
        m_mx = gsm[:, 288:296]
        m_x = gsm[:, 296:344].rearrange("p (i c) -> p i c", i=6)
        m_M, m_in, m_em, m_sum, m_nq, m_wr, m_den = (gsm[:, 344 + 8 * i:352 + 8 * i] for i in range(7))
        m_ss = gsm[:, 400:408]
        dmx = [hT[:, 0:2, :].rearrange("p a b -> p (a b)").rearrange("p (c s) -> p c s", c=8), ar(1024, 8, 128)]
        aff = small[:, 128:160].rearrange("p (b e) -> p b e", b=TB)
        mask_t = small[:, 160:192].rearrange("p (b e) -> p b e", b=TB)
        top8 = small[0:N_EXP, 192:200]
        turn_of = small[:, 200:232].rearrange("p (b e) -> p b e", b=TB)
        work, mask_e = ar(13824, T), ar(14080, T)
        gates_flat = ar(7168, N_EXP * T)
        moe_base = {}
        BLOCKS = ((2, 3, 0, 1), (3, 2, 1, 0))

        done, freed = sem("matmuls_done"), [sem(f"bank_read_{b}") for b in range(8)]
        G = Groups(bank, done, freed)
        slot_full = [sem(f"slot_full_{i}") for i in range(SLOTS)]
        place, sent, items_of = {}, [0] * SLOTS, {}

        def queue(items, first):
            for i, (key, pieces) in enumerate(items):
                sl = (first + i) % SLOTS
                sent[sl] += 16
                place[key] = (sl, sent[sl])
            return (first + len(items)) % SLOTS

        moe_first = [queue(before, 0), 0]
        moe_sent = [list(sent), None]
        per_expert = [32 if (s - moe_first[0]) % SLOTS < 4 else 16 for s in range(SLOTS)]
        for s in range(SLOTS):
            sent[s] += N_EXP * per_expert[s]
        moe_first[1] = queue(between, moe_first[0])
        moe_sent[1] = list(sent)

        def weights(pe, key):
            sl, count = place[key]
            pe.wait_ge(slot_full[sl], count)
            return ring[:, sl * SLOT:(sl + 1) * SLOT]

        def w3(v, k, n):
            return v[:, 0:k * n].rearrange("p (k n) -> p k n", k=k)

        block = ctx.enter_context(nc.Block())

        @block.tensor
        def _(pe):
            def chain(name, b, lhs, rhs, n):
                for k in range(n):
                    ins = pe.matmul(b, lhs(k), rhs(k), start=(k == 0), stop=(k == n - 1))
                G.close(ins, name)

            def turn(name, b, srcs):
                for j, src in enumerate(srcs):
                    p = src.shape[0]
                    m = src.shape[1]
                    ins = pe.transpose(b[0:m, j * p:j * p + p], src, ident[0:p, 0:p])
                G.close(ins, name)

            pending = []

            def mod_turn():
                i = pending.pop()
                b = G.open(pe, ("mod_t", i))
                G.read(pe, ("mod", i))
                turn(("mod_t", i), b, [mrow[:, j * 128:j * 128 + 128] for j in range(4)])

            def mod(i):
                x = w3(weights(pe, ("mod", i)), KD, 512)
                b = G.open(pe, ("mod", i))
                for half in range(2):
                    for q in range(4):
                        k = q + 4 * half
                        ins = pe.matmul(b[32 * q:32 * q + 32, :], cond[:, 0 if i < 12 else 1, k, :], x[:, k, :],
                                        start=(half == 0), stop=(half == 1), skip_group_check=True)
                G.close(ins, ("mod", i))
                G.over(("mod", i))
                if pending:
                    mod_turn()
                pending.append(i)

            def norm(c, second=False):
                norm_part(c, G.open(pe, ("ms", c), second), 0, KD)

            def norm_part(c, b, lo, hi):
                for k in range(lo, hi):
                    pe.wait_ge(sem("squares"), KD * c + k + 1)
                    ins = pe.matmul(b[:, 0:T], ones, sq[:, k, :], start=(k == 0), stop=(k == KD - 1))
                if hi == KD:
                    G.close(ins, ("ms", c))

            def outputs_and_norm(c, group):
                b = None
                for n in range(KD):
                    group(n)
                    if n == 3:
                        b = G.open(pe, ("ms", c), second=True)
                    if n >= 3:
                        norm_part(c, b, 0 if n == 3 else n - 3, n - 2)
                norm_part(c, b, KD - 3, KD)

            def normed(c, k=KD):
                pe.wait_ge(sem("normed"), KD * (c - (c > 4)) + k)

            def token_major(name, x, n, tb, c0=0, second=False):
                b = G.open(pe, (name, tb), second)
                chain((name, tb), b[:, 0:n], lambda k: hT[:, k, tb * 128:tb * 128 + 128],
                      lambda k: x[:, k, c0:c0 + n], KD)

            def attend(tag, heads, qt, kt, v, pr, fill):
                def scores(i):
                    b = G.open(pe, (tag, "s", i), second=True)
                    h, qb = i // 2, i % 2
                    G.close(pe.matmul(b, qt(h)[:, qb * 128:qb * 128 + 128], kt(h), start=True, stop=True),
                            (tag, "s", i))

                def output(hp):
                    b = G.open(pe, (tag, "o", hp), second=True)
                    for m in range(4):
                        G.read(pe, (tag, "pt", 4 * hp + m))
                    pt = (probT, e_probT)[tag == "gqa"]
                    for j in range(4):
                        for h2 in range(2):
                            ins = pe.matmul(b[64 * h2:64 * h2 + 64, 0:T], v(2 * hp + h2, j), pt[:, h2, j * T:j * T + T],
                                            start=(j == 0), stop=(j == 3), skip_group_check=True)
                    G.close(ins, (tag, "o", hp))

                scores(0)
                scores(1)
                for i in range(2 * heads):
                    if i + 2 < 2 * heads:
                        scores(i + 2)
                    fill(i)
                    if i and i % 4 == 0:
                        output(i // 4 - 1)
                    b = G.open(pe, (tag, "pt", i))
                    pe.wait_ge(sem(tag + "_prob"), i + 1)
                    turn((tag, "pt", i), b, [pr[:, i % 2, j * 128:j * 128 + 128] for j in range(4)])
                output(heads // 2 - 1)

            pe.wait_ge(sem("vectors_in"), 32)
            b = G.open(pe, "vec")
            for t in range(4):
                n = tiles[t]
                ins = pe.transpose(b[:, 128 * t:128 * t + n], vrow[0:n, 128 * t:128 * t + 128], ident[0:n, 0:n])
            G.close(ins, "vec")
            pe.wait_ge(sem("x_in"), 32)
            for k in range(KD):
                b = G.open(pe, ("xt", k))
                turn(("xt", k), b, [x_tm[:, tb, k * 128:k * 128 + 128] for tb in range(4)])
            pe.wait_ge(sem("cond_ready"), 4)
            mod(0)
            norm(0, second=True)
            mod(1)
            norm(1, second=True)
            mod(2)
            mod(3)
            mod_turn()

            x = w3(weights(pe, "kvr"), KD, 288)
            for tb in range(4):
                if tb % 2 == 0:
                    normed(tb // 2)
                token_major("kvr", x, 288, tb)
            G.over("kvr")
            for j in range(2):
                b = G.open(pe, ("kvt", j))
                pe.wait_ge(sem("kv_norm"), 4)
                turn(("kvt", j), b, [kvr[:, tb, j * 128:j * 128 + 128] for tb in range(4)])
            x = w3(weights(pe, "w_ukv"), 2, 1024)
            for tb in range(4):
                for hf in range(2):
                    b = G.open(pe, ("kv", tb, hf))
                    for k in range(2):
                        G.read(pe, ("kvt", k))
                    chain(("kv", tb, hf), b, lambda k: kvT[:, k, tb * 128:tb * 128 + 128],
                          lambda k: x[:, k, hf * 512:hf * 512 + 512], 2)
            G.over("w_ukv")
            x = w3(weights(pe, "qc"), KD, Q_LORA)
            for tb in range(TB):
                token_major("qc", x, Q_LORA, tb)
            G.over("qc")
            pe.wait_ge(sem("k_rope"), 4)
            for tb in range(4):
                for hf in range(2):
                    G.read(pe, ("kv", tb, hf))
            for h in range(4):
                b = G.open(pe, ("kT", h))
                turn(("kT", h), b, [kcat[:, tb, h * QH:h * QH + QH] for tb in range(4)])
            for j in range(3):
                b = G.open(pe, ("qct", j))
                pe.wait_ge(sem("q_norm"), 2)
                turn(("qct", j), b, [qc[:, tb, j * 128:j * 128 + 128] for tb in range(TB)])
            x = w3(weights(pe, "w_uq"), 3, MLA_H * QH)
            for tb in range(TB):
                for hf in range(2):
                    b = G.open(pe, ("q", tb, hf))
                    for k in range(3):
                        G.read(pe, ("qct", k))
                    chain(("q", tb, hf), b[:, 0:384], lambda k: qcT[:, k, tb * 128:tb * 128 + 128],
                          lambda k: x[:, k, hf * 384:hf * 384 + 384], 3)
            G.over("w_uq")
            for h in range(4, MLA_H):
                b = G.open(pe, ("kT", h))
                turn(("kT", h), b, [kcat[:, tb, h * QH:h * QH + QH] for tb in range(4)])
            pe.wait_ge(sem("q_rope"), 2)
            for hp in range(4):
                b = G.open(pe, ("qT", hp))
                turn(("qT", hp), b, [q_tm[:, tb, h * QH:h * QH + QH] for h in (2 * hp, 2 * hp + 1) for tb in range(TB)])
            for h in range(MLA_H):
                G.read(pe, ("kT", h))
            for hp in range(4):
                G.read(pe, ("qT", hp))

            def mla_fill(i):
                if i % 2 == 0:
                    mod(4 + i // 2)
                elif i in MLA_FILL:
                    tag, tb = MLA_FILL[i]
                    token_major(tag, w3(weights(pe, tag), KD, 512), 512, tb)
                    if (tag, tb) == ("gk", 3):
                        G.over("gk")

            attend("mla", MLA_H, lambda h: qT[0:QH, h, :], lambda h: kT[0:QH, h, :],
                   lambda h, j: v_tm[:, j, h * VH:h * VH + VH], prob,
                   mla_fill)

            pe.wait_ge(sem("tables_in"), 16)
            token_major("gv", w3(weights(pe, "gv"), KD, 512), 512, 3)
            G.over("gv")
            x = w3(weights(pe, "gq"), KD, 512)
            for tb in range(TB):
                token_major("gq", x, 512, tb)
                if tb == 0:
                    mod(12)
            G.over("gq")
            mod(13)
            x = w3(weights(pe, "low"), KD, 32)
            b = G.open(pe, "low")
            chain("low", b[0:32, :], lambda k: x[:, k, :], lambda k: hT[:, k, :], KD)
            G.over("low")
            pe.wait_ge(sem("decay_in"), 3 * 16)
            pe.wait_ge(sem("low_ready"), 1)
            for tb in range(4):
                for d in range(2):
                    b = G.open(pe, ("z", tb, d), second=tb >= 2)
                    G.close(pe.matmul(b, low[0:33, tb * 128:tb * 128 + 128], wdec[0:33, d * 512:d * 512 + 512],
                                      start=True, stop=True), ("z", tb, d))
            x = w3(weights(pe, "gr"), KD, 512)
            for j in range(4):
                b = G.open(pe, ("gr", j))
                chain(("gr", j), b[:, 0:T], lambda k: x[:, k, j * 128:j * 128 + 128], lambda k: hT[:, k, 0:T], KD)
            G.over("gr")
            mod(14)
            mod(15)
            mod_turn()
            b = G.open(pe, "tot")
            for tb in range(4):
                for d in range(2):
                    G.read(pe, ("z", tb, d))
                    ins = pe.matmul(b[0:32, :], c_("chunk_pick", (d * 4 + tb) * 32, 32), gg[:, tb, d * 512:d * 512 + 512],
                                    start=(tb + d == 0), stop=(tb == 3 and d == 1))
            G.close(ins, "tot")
            for tb in range(TB):
                for d in range(2):
                    b = G.open(pe, ("bc", tb, d))
                    G.close(pe.matmul(b, c_(("sum_upto64", "sum_from64")[d]), gg[:, tb, d * 512:d * 512 + 512],
                                      start=True, stop=True), ("bc", tb, d))
                    b = G.open(pe, ("aft", tb, d))
                    G.close(pe.matmul(b, c_(("sum_after64", "sum_before64")[d]), gg[:, tb, d * 512:d * 512 + 512],
                                      start=True, stop=True), ("aft", tb, d))
                    for tag, j in (("qe", 0), ("ke", 1)):
                        b = G.open(pe, (tag, tb, d))
                        pe.wait_ge(sem("gla_scaled"), 2 * (2 * tb + d) + j + 1)
                        turn((tag, tb, d), b, [gex[:, j, h * 128:h * 128 + 128] for h in range(4)])
            for tb in range(2, 4):
                for d in range(2):
                    b = G.open(pe, ("aft", tb, d))
                    G.close(pe.matmul(b, c_(("sum_after64", "sum_before64")[d]), gg[:, tb, d * 512:d * 512 + 512],
                                      start=True, stop=True), ("aft", tb, d))
            b = G.open(pe, "dec")
            G.read(pe, "tot")
            for h in range(4):
                ins = pe.transpose(b[:, 32 * h:32 * h + 32], dtm[0:32, h * 128:h * 128 + 128], ident[0:32, 0:32])
            G.close(ins, "dec")
            for tb in range(TB):
                for d in range(2):
                    G.read(pe, ("qe", tb, d))
                    G.read(pe, ("ke", tb, d))

            def inner(i):
                tb, h = i // 4, i % 4
                b = G.open(pe, ("A", i))
                for d in range(2):
                    r = slice(h * T + tb * 128, h * T + tb * 128 + 128)
                    ins = pe.matmul(b[:, d * 128:d * 128 + 128], keT[:, d, r], qeT[:, d, r],
                                    start=(d == 0), stop=(d == 1), skip_group_check=True)
                G.close(ins, ("A", i))

            inner(0)
            for i in range(8):
                if i < 7:
                    inner(i + 1)
                tb, h = i // 4, i % 4
                pe.wait_ge(sem("gla_masked"), i + 1)
                o = (h % 2) * T + tb * 128
                G.close(pe.matmul(acc[h // 2][:, o:o + 128], gv[:, tb, h * 128:h * 128 + 128], atT[:, i, :],
                                  start=(i in (0, 2)), stop=False, skip_group_check=True), ("AV", i))
            for s in range(8):
                for d in range(2):
                    pos = (s % 4) if d == 0 else 3 - s % 4
                    tb, c = (2 if s < 4 else 0) + pos // 2, pos % 2
                    if s < 7:
                        b = G.open(pe, ("U", s, d))
                        pe.wait_ge(sem("gla_keys"), 8)
                        for h in range(4):
                            r = slice(64 * c, 64 * c + 64)
                            ins = pe.matmul(b[:, h * 128:h * 128 + 128], gg[r, tb, d * 512 + h * 128:d * 512 + h * 128 + 128],
                                            gv[r, tb, h * 128:h * 128 + 128], start=(h == 0), stop=(h == 3),
                                            skip_group_check=True)
                        G.close(ins, ("U", s, d))
                    if s >= 4:
                        pe.wait_ge(sem("gla_state"), 2 * (s - 1) + d + 1)
                        for h in range(4):
                            o = (h % 2) * T + pos * 64
                            ins = pe.matmul(acc[h // 2][:, o:o + 64], st[(s - 1) % 2][:, d, h * 128:h * 128 + 128],
                                            qeT[:, d, h * T + pos * 64:h * T + pos * 64 + 64],
                                            start=False, stop=False, skip_group_check=True)
                        G.close(ins, ("I", s, d))
            for hp in range(2):
                b = G.open(pe, ("gn", hp))
                pe.wait_ge(sem("gla_squares"), hp + 1)
                G.close(pe.matmul(b, ones, sqg[:, hp, :], start=True, stop=True), ("gn", hp))
            xm, xg = w3(weights(pe, "w_br_mla"), 4, D), w3(weights(pe, "w_br_gla"), 4, D)
            for n in range(KD):
                for tag, key in (("gm", "gate_mla"), ("gG", "gate_gla")):
                    x = w3(weights(pe, (key, n // 4)), KD, 512)
                    b = G.open(pe, (tag, n))
                    chain((tag, n), b[:, 0:T], lambda k: x[:, k, (n % 4) * 128:(n % 4) * 128 + 128],
                          lambda k: hT[:, k, 0:T], KD)
                if n == 0:
                    for hp in range(4):
                        G.read(pe, ("mla", "o", hp))
                    pe.wait_ge(sem("gla_out"), 2)
                b = G.open(pe, ("bm", n))
                chain(("bm", n), b[:, 0:T], lambda k: xm[:, k, n * 128:n * 128 + 128], lambda k: o_mla[:, k, :], 4)
                b = G.open(pe, ("bg", n))
                chain(("bg", n), b[:, 0:T], lambda k: xg[:, k, n * 128:n * 128 + 128], lambda k: o_gla[:, k, :], 4)
                if n % 4 == 3:
                    G.over(("gate_mla", n // 4), ("gate_gla", n // 4))
            G.over("w_br_mla", "w_br_gla")
            pe.wait_ge(sem("merged"), KD)
            xs = [w3(weights(pe, ("w_out", g)), 4, D) for g in range(2)]

            def way_out(n):
                b = G.open(pe, ("wo", n))
                chain(("wo", n), b[:, 0:T], lambda k: xs[k // 4][:, k % 4, n * 128:n * 128 + 128],
                      lambda k: merged[:, k, :], KD)

            outputs_and_norm(2, way_out)
            G.over(("w_out", 0), ("w_out", 1))
            for g in range(6):
                xg, xv = (w3(weights(pe, (key, g)), KD, min(512, D_FF - 512 * g)) for key in ("up_gate", "up_val"))
                for j in range(min(4, KF - 4 * g)):
                    for tag, x in (("ug", xg), ("uv", xv)):
                        b = G.open(pe, (tag, 4 * g + j))
                        for k in range(KD):
                            if g + j == 0:
                                normed(2, k + 1)
                            ins = pe.matmul(b[:, 0:T], x[:, k, j * 128:j * 128 + 128], hT[:, k, 0:T],
                                            start=(k == 0), stop=(k == KD - 1))
                        G.close(ins, (tag, 4 * g + j))
                    if 4 * g + j == CTX_NORM:
                        norm(3)
                G.over(("up_gate", g), ("up_val", g))
                mod(16 + g)
                if 4 * g + 4 == CTX_NORM:
                    pe.wait_ge(sem("ctx2_in"), 16)
                    for i in range(4):
                        b = G.open(pe, ("ct", i))
                        turn(("ct", i), b, [xc2[:, tb, k * 128:k * 128 + 128] for k in (2 * i, 2 * i + 1)
                                            for tb in range(TB)])
            mod_turn()
            for g in range(6):
                x = w3(weights(pe, ("down", g)), min(4, KF - 4 * g), D)
                for k in range(min(4, KF - 4 * g)):
                    j = 4 * g + k
                    pe.wait_ge(sem("ff_ready"), j + 1)
                    for n in range(KD):
                        ins = pe.matmul(acc[n // 2][:, (n % 2) * T:(n % 2) * T + T], x[:, k, n * 128:n * 128 + 128],
                                        ff[:, j, :], start=(j == 0 and n % 2 == 0), stop=(j == KF - 1),
                                        skip_group_check=True)
                        if j == KF - 1 and n % 2:
                            G.close(ins, ("ff", n // 2))
                if g < 5:
                    G.close(ins, ("down", g))
                G.over(("down", g))
            norm(4)
            x = w3(weights(pe, "e_k"), KD, 512)
            normed(3)
            bs = [G.open(pe, ("eq", 4 + j)) for j in range(4)]

            def keys(lo, k):
                for j in range(4):
                    ins = pe.matmul(bs[j][:, lo:lo + T], x[:, k, j * 128:j * 128 + 128], hT[:, k, lo:lo + T],
                                    start=(k == 0 and lo > 0), stop=(k == KD - 1), skip_group_check=True)
                    if k == KD - 1 and lo == 0:
                        G.close(ins, ("eq", 4 + j))

            for k in range(KD):
                keys(T, k)
            norm(5, second=True)
            xkv, xgt = w3(weights(pe, "e_kv"), KD, 256), w3(weights(pe, "e_gt"), KD, 16)
            for tb in (2, 3):
                token_major("ekv", xkv, 256, tb, second=True)
            for tb in (2, 3):
                token_major("egt", xgt, 16, tb, second=True)
            for k in range(KD):
                normed(5, k + 1)
                keys(0, k)
            G.over("e_k")
            for tb in (0, 1):
                token_major("egt", xgt, 16, tb)
            G.over("e_gt")
            for tb in (0, 1):
                token_major("ekv", xkv, 256, tb)
            G.over("e_kv")
            x = w3(weights(pe, "e_qa"), KD, 512)
            for tb in range(TB):
                token_major("eqa", x, 512, tb)
            G.over("e_qa")
            x = w3(weights(pe, "e_ob"), KD, 512)
            for j in range(4):
                b = G.open(pe, ("eob", j))
                chain(("eob", j), b[:, 0:T], lambda k: x[:, k, j * 128:j * 128 + 128], lambda k: hT[:, k, 0:T], KD)
            G.over("e_ob")
            pe.wait_ge(sem("heads_ready"), 1)
            for g in range(A_KV):
                b = G.open(pe, ("ekT", g))
                turn(("ekT", g), b, [e_kv[:, tb, g * A_D:g * A_D + A_D] for tb in range(4)])
            pe.wait_ge(sem("heads_ready"), 3)
            for hp in range(4):
                b = G.open(pe, ("eqT", hp))
                turn(("eqT", hp), b, [e_qa[:, tb, h * A_D:h * A_D + A_D] for h in (2 * hp, 2 * hp + 1) for tb in range(TB)])
            for g in range(A_KV):
                G.read(pe, ("ekT", g))
            for hp in range(4):
                G.read(pe, ("eqT", hp))

            def gqa_fill(i):
                if i % 2 == 0:
                    mod(22 + i // 2)
                elif i in GQA_FILL:
                    j = GQA_FILL[i]
                    x = w3(weights(pe, "e_q"), KD, 512)
                    b = G.open(pe, ("eq", j))
                    chain(("eq", j), b[:, 0:T], lambda k: x[:, k, j * 128:j * 128 + 128], lambda k: hT[:, k, 0:T], KD)
                    if j == 3:
                        G.over("e_q")

            attend("gqa", A_H, lambda h: e_qT[0:A_D, h, :], lambda h: e_kT[0:A_D, h // 4, :],
                   lambda h, j: e_kv[:, j, 128 + (h // 4) * A_D:128 + (h // 4) * A_D + A_D], e_prob,
                   gqa_fill)
            pe.wait_ge(sem("m_gates"), 1)
            for tb in range(4):
                b = G.open(pe, ("eb", tb))
                pe.matmul(b[:, 0:4], c_("upto128"), m_lf[:, tb, 0:4], start=True, stop=True, skip_group_check=True)
                pe.matmul(b[:, 4:8], c_("from128"), m_lf[:, tb, 4:8], start=True, stop=True, skip_group_check=True)
                G.close(pe.matmul(b[:, 8:16], ones, m_lf[:, tb, :], start=True, stop=True, skip_group_check=True),
                        ("eb", tb))
            for tb in range(4):
                b = G.open(pe, ("ekt", tb))
                if tb == 0:
                    pe.wait_ge(sem("qk_ready"), 1)
                turn(("ekt", tb), b, [qk[:, 4 + h, tb * 128:tb * 128 + 128] for h in range(4)])

            def spread(tb):
                for d in range(2):
                    b = G.open(pe, ("eR", tb, d))
                    pe.wait_ge(sem("m_r"), 4)
                    for h in range(4):
                        c = m_r[:, tb, d * 4 + h:d * 4 + h + 1]
                        ins = pe.transpose(b[:, h * 128:h * 128 + 128], c.to_broadcast([128, 128]), ident)
                    G.close(ins, ("eR", tb, d))

            def values(tb):
                token_major("evb", w3(weights(pe, "e_vb"), KD, 512), 512, tb)

            def update(j):
                for d in range(2):
                    tb = BLOCKS[d][j]
                    G.read(pe, ("evb", tb))
                    for hp in range(2):
                        b = G.open(pe, ("eU", j, d, hp))
                        pe.wait_ge(sem("m_keys"), 2 * j + d + 1)
                        for h in (2 * hp, 2 * hp + 1):
                            o = (h % 2) * 129
                            ins = pe.matmul(b[:, o:o + 129], kw[:, d * 4 + h, :],
                                            v1[:, tb, h * 130 + 1 - d:h * 130 + 130 - d], start=(h % 2 == 0),
                                            stop=(h % 2 == 1), skip_group_check=True)
                        G.close(ins, ("eU", j, d, hp))

            for tb in (2, 3, 1):
                spread(tb)
            values(2)
            values(3)
            update(0)
            values(0)
            update(1)
            values(1)
            G.over("e_vb")
            spread(0)
            mod(30)
            update(2)
            mod(31)
            for tb in (1, 0):
                pe.wait_ge(sem("qk_ready"), 2)
                b = G.open(pe, ("eS", tb))
                for h in range(4):
                    ins = pe.matmul(b[:, h * 128:h * 128 + 128], qk[:, h, tb * 128:tb * 128 + 128],
                                    qk[:, 4 + h, tb * 128:tb * 128 + 128], start=(h == 0), stop=(h == 3),
                                    skip_group_check=True)
                G.close(ins, ("eS", tb))
                if tb == 1:
                    pe.wait_ge(sem("m_state"), 12)
                for h in range(4):
                    b = G.open(pe, ("eC", tb, h), second=True)
                    G.close(pe.matmul(b[:, 0:258], qk[:, h, tb * 128:tb * 128 + 128], cn[tb][:, h, :],
                                      start=True, stop=True), ("eC", tb, h))
                for i in (32, 33) if tb else (34,):
                    mod(i)
                b = G.open(pe, ("eW", tb))
                pe.wait_ge(sem("m_weights"), 2 - tb)
                turn(("eW", tb), b, [wm[:, h, :] for h in range(4)])
                b = G.open(pe, ("eH", tb))
                G.read(pe, ("eW", tb))
                for h in range(4):
                    ins = pe.matmul(b[:, h * 128:h * 128 + 128], dm[:, h, :], v1[:, tb, h * 130 + 1:h * 130 + 129],
                                    start=(h == 0), stop=(h == 3), skip_group_check=True)
                G.close(ins, ("eH", tb))
                if tb == 0:
                    mod(35)
                b = G.open(pe, ("eT", tb))
                pe.wait_ge(sem("m_out"), 2 - tb)
                turn(("eT", tb), b, [h_e[:, h, :] for h in range(4)])
            mod_turn()
            xs = [w3(weights(pe, ("e_out", g)), 4, D) for g in range(2)]
            for hp in range(4):
                G.read(pe, ("gqa", "o", hp))
            G.read(pe, ("eT", 1))
            G.read(pe, ("eT", 0))

            def even_out(n):
                b = G.open(pe, ("eo", n))
                chain(("eo", n), b[:, 0:T], lambda k: xs[k // 4][:, k % 4, n * 128:n * 128 + 128],
                      lambda k: (e_oT if k < 4 else e_mT)[:, k % 4, :], KD)

            outputs_and_norm(6, even_out)
            G.over(("e_out", 0), ("e_out", 1))

            def output(c):
                pe.wait_ge(sem("scaled"), KD * (c + 1))
                for j in range(4):
                    tb, half = j // 2, j % 2
                    b = G.open(pe, ("out", j))
                    turn(("out", j), b, [xT[:, half * 4 + m, tb * 128:tb * 128 + 128] for m in range(4)])

            def experts(layer, c):
                x = w3(weights(pe, ("router", layer)), KD, N_EXP)
                bs = [G.open(pe, ("lg", layer, tb)) for tb in range(TB)]
                for k in range(KD):
                    normed(c, k + 1)
                    for tb in range(TB):
                        ins = pe.matmul(bs[tb][:, 0:N_EXP], hT[:, k, tb * 128:tb * 128 + 128], x[:, k, :],
                                        start=(k == 0), stop=(k == KD - 1))
                        if k == KD - 1:
                            G.close(ins, ("lg", layer, tb))
                G.over(("router", layer))
                def token_rows(j):
                    tb, half = j // 2, j % 2
                    b = G.open(pe, ("ht", layer, j))
                    turn(("ht", layer, j), b, [hT[:, half * 4 + m, tb * 128:tb * 128 + 128] for m in range(4)])

                token_rows(0)
                token_rows(1)
                b = G.open(pe, ("aT", layer))
                pe.wait_ge(sem("affinity"), 2 * layer + 2)
                turn(("aT", layer), b, [aff[:, tb, :] for tb in range(TB)])
                token_rows(2)
                token_rows(3)
                b = G.open(pe, ("mT", layer))
                pe.wait_ge(sem("chosen"), layer + 1)
                for tb in range(TB):
                    ins = pe.transpose(b[:, tb * N_EXP:(tb + 1) * N_EXP], mask_e[0:N_EXP, tb * 128:tb * 128 + 128],
                                       ident[0:N_EXP, 0:N_EXP])
                G.close(ins, ("mT", layer))
                b = G.open(pe, ("cs", layer))
                G.read(pe, ("mT", layer))
                pe.matmul(b[:, 0:N_EXP], c_("upto128"), mask_t[:, 0, :], start=True, stop=True, skip_group_check=True)
                pe.matmul(b[:, 16:32], ones, mask_t[:, 0, :], start=True, stop=False, skip_group_check=True)
                G.close(pe.matmul(b[:, 16:32], c_("upto128"), mask_t[:, 1, :], start=False, stop=True,
                                  skip_group_check=True), ("cs", layer))
                pe.wait_ge(sem("one_hot"), 2 * layer + 1)
                for j in range(4):
                    G.read(pe, ("ht", layer, j))
                for b in range(RING):
                    G.drain(pe, b)
                first, came = moe_first[layer], moe_sent[layer]

                def slot(j, e):
                    s = (first + j) % SLOTS
                    pe.wait_ge(slot_full[s], e * (32 if j < 4 else 16) + (came[s] + (32 if j < 4 else 16)))
                    return ring[:, s * SLOT:(s + 1) * SLOT]

                def first_rows():
                    for q in range(4):
                        half, tb = q // 2, q % 2
                        ins = pe.matmul(bank[1][32 * q:32 * q + 32, :], hot[:, tb, 0:CAP],
                                        h_tm[:, tb, half * 512:half * 512 + 512], start=True, stop=True,
                                        skip_group_check=True)
                    ins.then_inc(sem("rows_untransposed"), 1)
                    pe.wait_ge(sem("rows_copied"), layer + 1)
                    for m in range(4):
                        ins = pe.transpose(bank[0][:, m * 128:m * 128 + 128], row_parts[:, m * 128:m * 128 + 128], ident)
                    ins.then_inc(sem("rows_selected"), 1)

                def rows(e):
                    for k in range(KD):
                        for tb in range(TB):
                            ins = pe.matmul(bank[0][:, k * CAP:(k + 1) * CAP], h_tm[:, tb, k * 128:k * 128 + 128],
                                            hot_flat[:, bass.ds(e * CAP + tb * N_EXP * CAP, CAP)],
                                            start=(k + tb == 0), stop=(k == KD - 1 and tb == 1), skip_group_check=True)
                    ins.then_inc(sem("rows_selected"), 1)

                def gate_up(e):
                    pe.wait_ge(sem("rows_ready"), e + (N_EXP * layer + 1))
                    for j in range(4):
                        x = slot(j, e)
                        for kk in range(2):
                            k = 2 * j + kk
                            for q in range(4):
                                o = (q // 2) * 2048 + kk * D + (q % 2) * 512
                                ins = pe.matmul(bank[0][32 * q:32 * q + 32, :], xe[:, k * CAP:(k + 1) * CAP],
                                                x[:, o:o + 512], start=(k == 0), stop=(k == KD - 1),
                                                skip_group_check=True)
                        ins.then_inc(sem("gate_up_done"), 1)

                def down(e, last=False):
                    pe.wait_ge(sem("gu_copied"), e + (N_EXP * layer + 1))
                    for j in range(4):
                        ins = pe.transpose(bank[1][:, j * 128:j * 128 + 128], gu[:, j * 128:j * 128 + 128], ident)
                    ins.then_inc(done, 1)
                    pe.wait_ge(sem("act_ready"), e + (N_EXP * layer + 1))
                    for j in range(2):
                        x = w3(slot(4 + j, e), 4, D)
                        for h in range(2):
                            for q in range(4):
                                ins = pe.matmul(bank[2 + h][32 * q:32 * q + 32, :], act_t[:, 4 * j + q, :],
                                                x[:, q, h * 512:h * 512 + 512], start=(j == 0), stop=(j == 1),
                                                skip_group_check=True)
                    ins.then_inc(done, 1)
                    pe.wait_ge(sem("down_copied"), e * 2 + (2 * N_EXP * layer + 2))
                    for n in range(KD):
                        ins = pe.matmul(acc[n // 2][:, (n % 2) * T:(n % 2) * T + T],
                                        dsb[:, n // 4, (n % 4) * 128:(n % 4) * 128 + 128],
                                        gates_flat[:, bass.ds(e * T, T)], start=False, stop=False,
                                        skip_group_check=True)
                        if n == KD - 1 or (last and n % 2):
                            ins.then_inc(done, 1)

                first_rows()
                gate_up(0)
                pe.wait_ge(sem("one_hot"), 2 * layer + 2)
                pe.wait_ge(sem("gated_hot"), layer + 1)
                for e2 in range(N_EXP // 2):
                    b = G.open(pe, ("gT", layer, e2), second=True)
                    for m in range(4):
                        e, tb = 2 * e2 + m // 2, m % 2
                        ins = pe.transpose(b[:, m * 128:m * 128 + 128], hotg[:, tb, e * 128:e * 128 + 128], ident)
                    G.close(ins, ("gT", layer, e2))
                for e2 in range(N_EXP // 2):
                    G.read(pe, ("gT", layer, e2))
                for b in acc:
                    pe.matmul(b[:, 0:2], ones, nul, start=True, stop=False, skip_group_check=True)
                moe_base[layer] = G.count
                with pe.Fori(0, N_EXP - 1) as e:
                    down(e)
                    rows(e + 1)
                    gate_up(e + 1)
                down(N_EXP - 1, last=True)
                G.count += 3 * (N_EXP - 1) + 2 + RING

            experts(0, 6)
            norm(7)
            xs = [w3(weights(pe, ("o_in", g)), KD, 512) for g in range(2)]
            bs = [[G.open(pe, ("u", tb, g)) for g in range(2)] for tb in range(TB)]
            for k in range(KD):
                normed(7, k + 1)
                for tb in range(TB):
                    for g in range(2):
                        ins = pe.matmul(bs[tb][g], hT[:, k, tb * 128:tb * 128 + 128], xs[g][:, k, :],
                                        start=(k == 0), stop=(k == KD - 1))
                        if k == KD - 1:
                            G.close(ins, ("u", tb, g))
            G.over(("o_in", 0), ("o_in", 1))
            for tb in range(TB):
                for g in range(2):
                    G.read(pe, ("u", tb, g))
            x = w3(weights(pe, "pool"), TB, 4 * T)
            for c in range(KD):
                b = G.open(pe, ("p", c))
                chain(("p", c), b[:, 0:T], lambda k: u_tm[:, k, c * 128:c * 128 + 128],
                      lambda k: x[:, k, (c // 2) * T:(c // 2) * T + T], TB)
            G.over("pool")
            x = w3(weights(pe, "w_grp"), KD, 256)

            def pooled_out(n):
                b = G.open(pe, ("y", n))
                for k in range(2):
                    G.read(pe, ("p", n - n % 2 + k))
                chain(("y", n), b[:, 0:T], lambda k: x[:, n - n % 2 + k, (n % 2) * 128:(n % 2) * 128 + 128],
                      lambda k: pT[:, n - n % 2 + k, :], 2)

            outputs_and_norm(8, pooled_out)
            G.over("w_grp")
            experts(1, 8)
            norm(9)
            output(9)

        @block.sync
        def _(sp):
            def send(items, limit):
                for n, (key, pieces) in enumerate(items):
                    sl, _ = place[key]
                    if limit + n >= SLOTS:
                        sp.wait_ge(done, G.last_user[sequence[limit + n - SLOTS]])
                    for (lo, hi), k, src in pieces:
                        sp.dma_start(ring[:, sl * SLOT + lo:sl * SLOT + hi].rearrange("p (k n) -> p k n", k=k),
                                     src).then_inc(slot_full[sl], 16)

            sequence = [key for key, _ in before]
            sp.dma_start(vrow, w["vectors"]).then_inc(sem("vectors_in"), 16)
            sp.dma_start(cst[:, 0:256], w["tables"][:, 0:256]).then_inc(sem("vectors_in"), 16)
            sp.dma_start(x_tm[:, 0:2, :], w["x"][0].rearrange("(b p) d -> p b d", p=128)).then_inc(sem("x_in"), 16)
            sp.dma_start(x_tm[:, 2:4, :], w["ctx"][0].rearrange("(b p) d -> p b d", p=128)).then_inc(sem("x_in"), 16)
            send(before[:5], 0)
            sp.dma_start(cst[:, 256:], w["tables"][:, 256:]).then_inc(sem("tables_in"), 16)
            send(before[5:], 5)
            def used_up(layer, j, e):
                if j < 4:
                    sp.wait_ge(sem("gate_up_done"), e * 4 + (4 * N_EXP * layer + 1 + j))
                else:
                    sp.wait_ge(done, e * 3 + (moe_base[layer] + 2))

            def send_experts(layer, ahead):
                first = moe_first[layer]
                gate, up, down = (w[n] for n in ("w_exp_gate_2", "w_exp_up_2", "w_exp_down_2"))

                def pieces(e):
                    for j in range(4):
                        for a, m in ((0, gate), (1, up)):
                            yield j, 2 * a, m[layer, bass.ds(e, 1), 256 * j:256 * j + 256, :], 2
                    for j in range(2):
                        yield 4 + j, 0, down[layer, bass.ds(e, 1), 512 * j:512 * j + 512, :], 4

                def put(j, lo, src, k):
                    s = (first + j) % SLOTS
                    sp.dma_start(ring[:, s * SLOT + lo * D:s * SLOT + (lo + k) * D].rearrange("p (k n) -> p k n", k=k),
                                 src.rearrange("e (k p) n -> p (e k) n", p=128)).then_inc(slot_full[s], 16)

                last = -1
                for j, lo, src, k in pieces(0):
                    if j != last:
                        ahead[j]()
                    last = j
                    put(j, lo, src, k)
                with sp.Fori(1, N_EXP) as e:
                    last = -1
                    for j, lo, src, k in pieces(e):
                        if j != last:
                            used_up(layer, j, e - 1)
                        last = j
                        put(j, lo, src, k)

            def item_used(key):
                return lambda: sp.wait_ge(done, G.last_user[key])

            send_experts(0, [item_used(k) for k in sequence[-SLOTS:]])
            for n, (key, pieces_) in enumerate(between):
                used_up(0, n, N_EXP - 1)
                sl, _ = place[key]
                for (lo, hi), k, src in pieces_:
                    sp.dma_start(ring[:, sl * SLOT + lo:sl * SLOT + hi].rearrange("p (k n) -> p k n", k=k),
                                 src).then_inc(slot_full[sl], 16)
            ahead = [lambda n=n: used_up(0, n, N_EXP - 1) for n in range(len(between), SLOTS)]
            send_experts(1, ahead + [item_used(key) for key, _ in between])

        @block.scalar
        def _(act):
            count = [0]

            def link(ins):
                ins.then_inc(sem("act_step"), 1)
                count[0] += 1
                act.wait_ge(sem("act_step"), count[0])


            def evict(name, to, func=ACT.Copy, n=None, **kw):
                b = G.take(act, name)
                src = b[:, 0:n] if n else b
                G.give(act.activation(to, src, func, **kw), name)

            def squares(c, src, updated=None):
                if c:
                    act.wait_ge(done, G.number[("ms", c - 1)])
                for k in range(KD):
                    if updated:
                        updated(k)
                    act.activation(sq[:, k, :], src[:, k, :], ACT.Square).then_inc(sem("squares"), 1)

            def root(c, then=None):
                b = G.take(act, ("ms", c))
                if c:
                    act.wait_ge(sem("scaled"), KD * c)
                G.give(act.activation(rs, b[:, 0:T], ACT.Sqrt, bias=eps, scale=1.0 / D), ("ms", c))
                if then:
                    act.activation(small[:, 4:5], one, then)

            def shift(c, by, dst):
                for k in range(KD):
                    act.wait_ge(sem("scaled"), KD * c + k + 1)
                    act.activation(dst[:, k, :], dst[:, k, :], ACT.Identity, bias=by[:, k:k + 1]).then_inc(sem("normed"), 1)

            def mod(i):
                b = G.take(act, ("mod", i))
                if i:
                    act.wait_ge(done, G.number[("mod_t", i - 1)])
                G.give(act.activation(mrow, b, ACT.Copy), ("mod", i))

            act.wait_ge(sem("eps_ready"), 1)
            act.wait_ge(sem("vcol_ready"), 1)
            act.wait_ge(sem("cond_cleared"), 1)
            for which, names in enumerate((("c", "c_ctx"), ("c_2", "c_ctx_2"))):
                for r, name in enumerate(names):
                    act.activation(cond[:, which, :, r], vc(name, 0, KD), ACT.Silu).then_inc(sem("cond_ready"), 1)
            for k in range(1, KD, 2):
                b = G.take(act, ("xt", k))
                act.copy(xT[:, k, :], b[:, 0:T])
                G.give(act.copy(xcT[:, k, :], b[:, T:2 * T]), ("xt", k))
            for k in range(KD):
                G.read(act, ("xt", k))
            squares(0, xT)
            mod(0)
            root(0)
            squares(1, xcT)
            for i in (1, 2, 3):
                mod(i)
            shift(0, mc(0, 0), hT[:, :, 0:T])
            root(1)
            shift(1, mc(0, 0, 1), hT[:, :, T:2 * T])

            def rms_root(tag, tb, n, dim, at_):
                b = G.take(act, (tag, tb))
                link(act.activation(junk[:, 0:n], b[:, 0:n], ACT.Square, accum_out=small[:, at_ + tb:at_ + tb + 1]))
                act.activation(small[:, at_ + tb:at_ + tb + 1], small[:, at_ + tb:at_ + tb + 1], ACT.Sqrt,
                               bias=eps, scale=1.0 / dim).then_inc(sem(tag + "_root"), 1)

            for tb in range(4):
                rms_root("kvr", tb, KV_LORA, KV_LORA, 8)
            for j in range(2):
                evict(("kvt", j), kvT[:, j, :], ACT.Copy, scale=vc("kv_norm_g", j))
            for tb in range(4):
                b = G.take(act, ("kv", tb, 1))
                v = b.rearrange("p (h c) -> p h c", h=4)
                act.copy(kcat[:, tb, 4 * QH:].rearrange("p (h c) -> p h c", h=4)[:, :, 0:NOPE], v[:, :, 0:NOPE])
                G.give(act.copy(v_tm[:, tb, 256:512].rearrange("p (h c) -> p h c", h=4), v[:, :, NOPE:]), ("kv", tb, 1))
            for tb in range(TB):
                rms_root("qc", tb, Q_LORA, Q_LORA, 12)
            for h in (1, 3):
                G.give(act.copy(kT[0:QH, h, :], G.take(act, ("kT", h))[0:QH, :]), ("kT", h))
            for j in range(3):
                evict(("qct", j), qcT[:, j, :], ACT.Copy, n=T, scale=vc("q_norm_g", j))
            for tb in range(TB):
                evict(("q", tb, 1), q_tm[:, tb, 384:768], n=384)
            for h in (5, 7):
                G.give(act.copy(kT[0:QH, h, :], G.take(act, ("kT", h))[0:QH, :]), ("kT", h))
            for hp in (1, 3):
                G.give(act.copy(qT[0:QH, 2 * hp:2 * hp + 2, :].rearrange("p a b -> p (a b)"),
                                G.take(act, ("qT", hp))[0:QH, :]), ("qT", hp))

            def attend(tag, heads, scale, pr, prT, fill):
                for i in range(2 * heads + 1):
                    if i < 2 * heads:
                        b = G.take(act, (tag, "s", i))
                        act.wait_ge(sem(tag + "_max"), i + 1)
                        if i >= 2:
                            act.wait_ge(done, G.number[(tag, "pt", i - 2)])
                        act.activation(pr[:, i % 2, :], b, ACT.Exp, bias=small[:, 32 + i:33 + i], scale=scale,
                                       accum_out=small[:, 64 + i:65 + i]).then_inc(sem(tag + "_exp"), 1)
                    if i and i % 2 == 0:
                        transposed(act, tag, i - 1, prT)
                    if i:
                        fill(i - 1)

            def transposed(eng, tag, i, prT):
                h, qb = i // 2, i % 2
                b = G.take(eng, (tag, "pt", i))
                if h >= 2:
                    eng.wait_ge(done, G.number[(tag, "o", h // 2 - 1)])
                to = prT[:, h % 2, :].rearrange("p (j t) -> p j t", j=4)[:, :, qb * 128:qb * 128 + 128]
                src = b.rearrange("p (j t) -> p j t", j=4)
                G.give((act.copy if eng is act else eng.tensor_copy)(to, src), (tag, "pt", i))

            def mla_fill(i):
                if i % 2 == 0:
                    mod(4 + i // 2)
                elif i in MLA_FILL:
                    tag, tb = MLA_FILL[i]
                    if tb % 2:
                        evict((tag, tb), (gk if tag == "gk" else gv)[:, tb, :])

            attend("mla", MLA_H, QH ** -0.5, prob, probT, mla_fill)
            act.wait_ge(sem("wdec_cleared"), 1)
            act.dma_start(wdec[0:16, 0:512], w["gla_w_decay"][0, 0]).then_inc(sem("decay_in"), 16)
            act.dma_start(wdec[16:32, 512:1024], w["gla_w_decay"][0, 1]).then_inc(sem("decay_in"), 16)
            act.dma_start(wdec[32:33, :], w["gla_b_decay"].rearrange("a b c -> a (b c)")).then_inc(sem("decay_in"), 16)
            evict(("gv", 3), gv[:, 3, :])
            mod(12)
            evict(("gq", 1), gq[:, 1, :], scale=128 ** -0.5)
            mod(13)
            for half in range(2):
                for tb in (2 * half, 2 * half + 1):
                    for d in range(2):
                        link(act.activation(gg[:, tb, d * 512:d * 512 + 512], G.take(act, ("z", tb, d)), ACT.Abs))
                g = gg[:, 2 * half:2 * half + 2, :]
                link(act.activation(g, g, ACT.Exp, scale=-1.0))
                act.activation(g, g, ACT.Ln, bias=one).then_inc(sem("gate_log"), 1)
            mod(14)
            mod(15)
            b = G.take(act, "tot")
            G.give(act.activation(dtm[0:32, :], b[0:32, :], ACT.Exp), "tot")
            for tb in range(TB):
                for d in range(2):
                    b = G.take(act, ("bc", tb, d))
                    if tb + d:
                        act.wait_ge(done, G.number[("ke",) + ((tb, 0) if d else (tb - 1, 1))])
                    act.activation(gex[:, 0, :], b, ACT.Exp)
                    G.give(act.activation(gex[:, 1, :], b, ACT.Exp, scale=-1.0), ("bc", tb, d))
                    evict(("aft", tb, d), gg[:, tb, d * 512:d * 512 + 512], ACT.Exp)
                    b = G.take(act, ("ke", tb, d))
                    to = keT[:, d, :].rearrange("p (h t) -> p h t", h=4)[:, :, tb * 128:tb * 128 + 128]
                    G.give(act.copy(to, b.rearrange("p (h t) -> p h t", h=4)), ("ke", tb, d))
            for tb in range(2, 4):
                for d in range(2):
                    evict(("aft", tb, d), gg[:, tb, d * 512:d * 512 + 512], ACT.Exp)
            for j in range(4):
                G.read(act, ("gr", j))
            act.activation(grT, grT, ACT.Silu).then_inc(sem("gr_gated"), 1)
            for hp in range(2):
                act.wait_ge(done, G.number[("I", 7, 1)])
                act.activation(sqg[:, hp, :], acc[hp], ACT.Square).then_inc(sem("gla_squares"), 1)
            for hp in range(2):
                evict(("gn", hp), rtg[:, hp, :], ACT.Sqrt, bias=eps, scale=1.0 / 128)
            for n in range(KD):
                if n >= 2:
                    act.wait_ge(sem("merged"), n - 1)
                evict(("gm", n), sig[:, 2 * (n % 2), :], ACT.Sigmoid, n=T)
                evict(("gG", n), sig[:, 2 * (n % 2) + 1, :], ACT.Sigmoid, n=T)
            squares(2, xT, lambda k: G.read(act, ("wo", k)))
            act.dma_start(xc2[:, :, :], w["ctx_2"][0].rearrange("(b p) d -> p b d", p=128)).then_inc(sem("ctx2_in"), 16)
            root(2)
            shift(2, mc(0, 3), hT[:, :, 0:T])
            for j in range(KF):
                b = G.take(act, ("ug", j))
                if j >= 3:
                    act.wait_ge(sem("conv_done"), j - 2)
                else:
                    act.wait_ge(sem("pad_cleared"), 1)
                grid = pad[:, j % 3, :].rearrange("p (r c) -> p r c", r=ROWS + 2)[:, 1:ROWS + 1, 1:GRID_W + 1]
                G.give(act.copy(grid, b[:, 0:T].rearrange("p (r c) -> p r c", r=ROWS)), ("ug", j))
                evict(("uv", j), ff[:, j, :], n=T)
                if j % 4 == 3:
                    mod(16 + j // 4)
                if j == CTX_NORM - 1:
                    for i in range(4):
                        evict(("ct", i), xc2T[:, 2 * i:2 * i + 2, :].rearrange("p a b -> p (a b)"))
                    squares(3, xc2T, lambda k: G.read(act, ("ct", k // 2)))
                if j == CTX_NORM:
                    root(3)
                if j:
                    act.wait_ge(sem("conv_done"), j)
                    act.activation(gel[:, (j - 1) % 3, :], gel[:, (j - 1) % 3, :], ACT.Gelu).then_inc(sem("gelu_done"), 1)
                if j == CTX_NORM + 2:
                    shift(3, mc(1, 0, 1), hT[:, :, T:2 * T])
            mod(21)
            act.wait_ge(sem("conv_done"), KF)
            act.activation(gel[:, (KF - 1) % 3, :], gel[:, (KF - 1) % 3, :], ACT.Gelu).then_inc(sem("gelu_done"), 1)
            squares(4, xT, lambda k: act.wait_ge(sem("ff_added"), k + 1))
            root(4)
            act.dma_start(small[:, 640:704], w["g_qnorm_2"].to_broadcast([128, A_D])).then_inc(sem("heads_in"), 16)
            act.dma_start(small[:, 704:768], w["g_knorm_2"].to_broadcast([128, A_D])).then_inc(sem("heads_in"), 16)
            act.dma_start(small[:, 112:128], w["b_gate_2"].to_broadcast([128, 16])).then_inc(sem("heads_in"), 16)
            squares(5, xT, lambda k: act.wait_ge(sem("scaled"), KD * 4 + k + 1))
            root(5)
            evict(("ekv", 3), e_kv[:, 3, :], n=256)
            shift(5, mc(1, 0), hT[:, :, 0:T])

            def to_raw(i):
                n = (i + 4) % 8
                b = G.take(act, ("eq", n))
                if i >= 3:
                    act.wait_ge(sem("conv2_done"), i - 2)
                else:
                    act.wait_ge(sem("raw_cleared"), 1)
                to = raw[:, i % 3, :].rearrange("p (s t) -> p s t", s=2)[:, 0:2 if n >= 4 else 1, 1:T + 1]
                G.give(act.copy(to, b[:, 0:512 if n >= 4 else T].rearrange("p (s t) -> p s t", t=T)), ("eq", n))

            for i in range(4):
                to_raw(i)
            evict(("ekv", 1), e_kv[:, 1, :], n=256)
            for n, v in ((1, small[:, 8:16]), (2, small[:, 16:32])):
                if n == 2:
                    f = gsm[:, 0:64].rearrange("p (x y) -> p x y", x=8)[:, :, 4:8]
                    ln = gsm[:, 224:256].rearrange("p (x y) -> p x y", x=8)
                    act.wait_ge(sem("m_biased"), 1)
                    link(act.activation(ln, f, ACT.Abs))
                    link(act.activation(ln, ln, ACT.Exp, scale=-1.0))
                    act.activation(ln, ln, ACT.Ln, bias=one).then_inc(sem("m_log"), 1)
                    act.wait_ge(sem("conv2_done"), 4)
                    act.activation(qk[:, 4:8, :], qk[:, 4:8, :], ACT.Silu).then_inc(sem("qk_ready"), 1)
                    evict(("eqa", 1), e_qa[:, 1, :])
                act.wait_ge(sem("heads_squared"), n)
                act.activation(v, v, ACT.Sqrt, bias=eps, scale=1.0 / A_D).then_inc(sem("heads_root"), 1)
            for j in range(4):
                evict(("eob", j), e_ob[:, j, :], n=T)
            G.give(act.copy(e_kT[0:A_D, 1, :], G.take(act, ("ekT", 1))[0:A_D, :]), ("ekT", 1))
            for hp in (1, 3):
                G.give(act.copy(e_qT[0:A_D, 2 * hp:2 * hp + 2, :].rearrange("p a b -> p (a b)"),
                                G.take(act, ("eqT", hp))[0:A_D, :]), ("eqT", hp))

            def gqa_fill(i):
                if i % 2 == 0:
                    mod(22 + i // 2)
                elif i in GQA_FILL:
                    to_raw(4 + GQA_FILL[i])

            attend("gqa", A_H, A_D ** -0.5, e_prob, e_probT, gqa_fill)
            def values(tb):
                b = G.take(act, ("evb", tb))
                G.give(act.copy(v1[:, tb, :].rearrange("p (h c) -> p h c", h=4)[:, :, 1:129],
                                b.rearrange("p (h c) -> p h c", h=4)), ("evb", tb))

            def exps(j):
                for d in range(2):
                    act.wait_ge(sem("m_args"), 2 * j + d + 1)
                    x = m_x[:, 2 * j + d, 0:8 if j else 4]
                    act.activation(x, x, ACT.Exp).then_inc(sem("m_exps"), 1)

            act.wait_ge(sem("v1_set"), 1)
            for tb in (1, 3):
                evict(("ekt", tb), ktm[:, tb, :])
            exps(0)
            values(3)
            exps(1)
            for j in range(4):
                G.read(act, ("eob", j))
            act.wait_ge(sem("conv2_done"), 8)
            act.activation(qk[:, 0:4, 0:T], qk[:, 0:4, 0:T], ACT.Silu).then_inc(sem("qk_ready"), 1)
            act.activation(e_ob, e_ob, ACT.Sigmoid).then_inc(sem("out_gates"), 1)
            values(1)
            mod(30)
            exps(2)
            mod(31)
            for tb in (1, 0):
                act.wait_ge(sem("m_shifted"), 2 - tb)
                act.activation(wm[:, :, :], dmx[tb], ACT.Exp)
                x = gsm[:, 352:368]
                act.activation(x, x, ACT.Exp).then_inc(sem("m_wexp"), 1)
                for i in (32, 33) if tb else (34,):
                    mod(i)
                b = G.take(act, ("eW", tb))
                G.give(act.copy(dm[:, 0:4, :].rearrange("p a b -> p (a b)"), b), ("eW", tb))
                if tb == 0:
                    mod(35)
                act.wait_ge(sem("m_hsq"), 2 - tb)
                act.activation(m_ss[:, 0:4], m_ss[:, 0:4], ACT.Sqrt, bias=eps, scale=1.0 / 128).then_inc(sem("m_hroot"), 1)
            def output(c):
                for j in (1, 3):
                    evict(("out", j), x_tm[:, j // 2, 512:1024])
                for j in range(4):
                    G.read(act, ("out", j))
                act.dma_start(out[0].rearrange("(b p) d -> p b d", p=128), x_tm[:, 0:2, :]).then_inc(sem("out_sent"), 16)
                act.wait_ge(sem("out_sent"), 16)

            def added(layer):
                return lambda k: act.wait_ge(sem("moe_added"), KD * layer + k + 1)

            def experts(layer, c, updated):
                squares(c, xT, updated)
                root(c, then=ACT.Exp)
                shift(c, mc(1 + layer, 3), hT[:, :, 0:T])
                for tb in range(TB):
                    b = G.take(act, ("lg", layer, tb))
                    act.wait_ge(sem("router_max"), 2 * layer + tb + 1)
                    act.activation(aff[:, tb, :], b[:, 0:N_EXP], ACT.Exp, bias=small[:, 32 + tb:33 + tb],
                                   accum_out=small[:, 64 + tb:65 + tb]).then_inc(sem("router_exp"), 1)
                for j in range(4):
                    evict(("ht", layer, j), h_tm[:, j // 2, (j % 2) * 512:(j % 2) * 512 + 512])

                def rows(e):
                    act.wait_ge(sem("rows_selected"), e + (N_EXP * layer + 1))
                    act.copy(xe, bank[0][:, 0:KD * CAP]).then_inc(sem("rows_ready"), 1)

                def between_products(e):
                    act.wait_ge(sem("gate_up_done"), e * 4 + (4 * N_EXP * layer + 4))
                    act.copy(gu, bank[0]).then_inc(sem("gu_copied"), 1)
                    act.wait_ge(done, e * 3 + (base + 1))
                    t = bank[1].rearrange("p (j c) -> p j c", j=4)
                    act.activation(sil.rearrange("p a b -> p (a b)").rearrange("p (j c) -> p j c", j=4), t[:, :, 0:64],
                                   ACT.Silu).then_inc(sem("silu_ready"), 1)
                    act.wait_ge(done, e * 3 + (base + 2))
                    act.copy(dsb[:, 1, :], bank[3]).then_inc(sem("down_copied"), 1)

                act.wait_ge(sem("rows_untransposed"), layer + 1)
                act.copy(row_parts, bank[1]).then_inc(sem("rows_copied"), 1)
                for e2 in range(1, N_EXP // 2, 2):
                    evict(("gT", layer, e2), gates_flat[:, e2 * 512:e2 * 512 + 512])
                base = moe_base[layer]
                with act.Fori(0, N_EXP - 1) as e:
                    between_products(e)
                    rows(e + 1)
                between_products(N_EXP - 1)

            experts(0, 6, lambda k: G.read(act, ("eo", k)))
            squares(7, xT, added(0))
            root(7)
            shift(7, mc(2, 0), hT[:, :, 0:T])
            for tb in range(TB):
                evict(("u", tb, 1), u_tm[:, tb, 512:1024])
            for c in range(1, KD, 2):
                evict(("p", c), pT[:, c, :], n=T)
            experts(1, 8, lambda k: G.read(act, ("y", k)))
            squares(9, xT, added(1))
            root(9)
            output(9)

        @block.vector
        def _(dve):
            count = [0]

            def link(ins):
                ins.then_inc(sem("dve_step"), 1)
                count[0] += 1
                dve.wait_ge(sem("dve_step"), count[0])

            def evict(name, to, n=None):
                b = G.take(dve, name)
                G.give(dve.tensor_copy(to, b[:, 0:n] if n else b), name)

            def mod(i):
                which, jj = i // 12, (i % 12) * 4
                to = modc[:, 96 * which + 2 * jj:96 * which + 2 * jj + 8].rearrange("p (j r) -> p j r", r=2)
                b = G.take(dve, ("mod_t", i))
                G.give(dve.tensor_reduce(to, b.rearrange("p (j q r) -> p j r q", j=4, q=4)[:, :, 0:2, :], AX.X, ALU.add),
                       ("mod_t", i))
                G.read(dve, ("mod_t", i))
                bias = vc("b_ada", jj, 4) if which == 0 else vc("b_mod_2", 48 * (which - 1) + jj, 4)
                link(dve.tensor_tensor(to, to, bias.unsqueeze(2).to_broadcast([128, 4, 2]), ALU.add))

            def set_gain(i, scale, g):
                link(dve.scalar_tensor_tensor(gains(i), scale, 1.0, g, ALU.add, ALU.mult))

            def invert(c):
                G.read(dve, ("ms", c))
                link(dve.reciprocal(rs, rs))

            def norm(c, src, g, dst):
                if c:
                    invert(c)
                for k in range(KD):
                    dve.scalar_tensor_tensor(dst[:, k, :], src[:, k, :], g[:, k:k + 1], rs,
                                             ALU.mult, ALU.mult).then_inc(sem("scaled"), 1)

            def rope(src, dst, tab, tb, tmp, n, q):
                a, size = at[tab]
                t = cst[:, a + tb * size // 2:a + (tb + 1) * size // 2].rearrange("p (c x q) -> p c x q", c=2, x=2)
                s1, s2 = src[:, :, :, 0, :], src[:, :, :, 1, :]
                cos, sin = (t[:, c].unsqueeze(1).to_broadcast([128, n, 2, q]) for c in range(2))
                t1, t2, t3, t4 = (tmp[:, i * n * 2 * q:(i + 1) * n * 2 * q].rearrange("p (n x q) -> p n x q", n=n, x=2)
                                  for i in range(4))
                dve.tensor_tensor(t1, s1, cos, ALU.mult)
                dve.tensor_tensor(t2, s2, sin, ALU.mult)
                dve.tensor_tensor(t3, s2, cos, ALU.mult)
                link(dve.tensor_tensor(t4, s1, sin, ALU.mult))
                dve.tensor_tensor(dst[:, :, :, 0, :], t1, t2, ALU.subtract)
                return dve.tensor_tensor(dst[:, :, :, 1, :], t3, t4, ALU.add)

            dve.memset(eps, EPS)
            dve.memset(nul, 0.0)
            dve.memset(one, 1.0).then_inc(sem("eps_ready"), 1)
            dve.memset(cond[:, :, :, :], 0.0).then_inc(sem("cond_cleared"), 1)
            b = G.take(dve, "vec")
            for t in range(3):
                dve.tensor_copy(vcol[:, 128 * t:128 * t + tiles[t]], b[:, 128 * t:128 * t + tiles[t]])
            G.give(dve.tensor_copy(vcol[:, 384:384 + tiles[3]], b[:, 384:384 + tiles[3]]), "vec")
            G.read(dve, "vec")
            dve.sem_inc(sem("vcol_ready"), 1)
            for k in range(0, KD, 2):
                b = G.take(dve, ("xt", k))
                dve.tensor_copy(xT[:, k, :], b[:, 0:T])
                G.give(dve.tensor_copy(xcT[:, k, :], b[:, T:2 * T]), ("xt", k))
            mod(0)
            for k in range(1, KD, 2):
                G.read(dve, ("xt", k))
            invert(0)
            for i in (1, 2, 3):
                mod(i)
            set_gain(0, mc(0, 1), vc("norm1_g", 0, KD))
            set_gain(1, mc(0, 1, 1), vc("norm1_g", 0, KD))
            norm(0, xT, gains(0), hT[:, :, 0:T])
            norm(1, xcT, gains(1), hT[:, :, T:2 * T])

            def low_rank(tag, tb, to, n, at_, say):
                b = G.take(dve, (tag, tb))
                dve.wait_ge(sem(tag + "_root"), tb + 1)
                r = small[:, at_ + tb:at_ + tb + 1]
                link(dve.reciprocal(r, r))
                link(dve.tensor_scalar(to, b[:, 0:n], r, None, ALU.mult))
                dve.sem_inc(sem(say), 1)
                return b

            for tb in range(4):
                b = low_rank("kvr", tb, kvr[:, tb, 0:KV_LORA], KV_LORA, 8, "kv_norm")
                G.give(dve.tensor_copy(kvr[:, tb, KV_LORA:288], b[:, KV_LORA:288]), ("kvr", tb))
                G.read(dve, ("kvr", tb))
                src = kvr[:, tb, KV_LORA:288]
                if tb == 0:
                    dve.wait_ge(sem("tables_in"), 16)
                if tb < TB:
                    link(rope(src.rearrange("p (n x h q) -> p n x h q", n=1, x=2, h=2),
                              src.rearrange("p (n x h q) -> p n x h q", n=1, x=2, h=2), "rope32", tb, small[:, 128:384], 1, 8))
                dve.tensor_copy(kcat[:, tb, :].rearrange("p (h c) -> p h c", h=MLA_H)[:, :, NOPE:],
                                src.unsqueeze(1).to_broadcast([128, MLA_H, ROPE])).then_inc(sem("k_rope"), 1)
            for tb in range(4):
                b = G.take(dve, ("kv", tb, 0))
                v = b.rearrange("p (h c) -> p h c", h=4)
                dve.tensor_copy(kcat[:, tb, 0:4 * QH].rearrange("p (h c) -> p h c", h=4)[:, :, 0:NOPE], v[:, :, 0:NOPE])
                G.give(dve.tensor_copy(v_tm[:, tb, 0:256].rearrange("p (h c) -> p h c", h=4), v[:, :, NOPE:]), ("kv", tb, 0))
            for tb in range(TB):
                low_rank("qc", tb, qc[:, tb, :], Q_LORA, 12, "q_norm")
                dve.sem_inc(freed[G.bank[("qc", tb)]], 1)
            for h in (0, 2):
                G.give(dve.tensor_copy(kT[0:QH, h, :], G.take(dve, ("kT", h))[0:QH, :]), ("kT", h))
            for tb in range(TB):
                evict(("q", tb, 0), q_tm[:, tb, 0:384], 384)
                G.read(dve, ("q", tb, 0))
                G.read(dve, ("q", tb, 1))
                v = q_tm[:, tb, :].rearrange("p (h c) -> p h c", h=MLA_H)[:, :, NOPE:].rearrange(
                    "p n (x h q) -> p n x h q", x=2, h=2)
                rope(v, v, "rope32", tb, small[:, 128:640], MLA_H, 8).then_inc(sem("q_rope"), 1)
            for h in (4, 6):
                G.give(dve.tensor_copy(kT[0:QH, h, :], G.take(dve, ("kT", h))[0:QH, :]), ("kT", h))
            for hp in (0, 2):
                G.give(dve.tensor_copy(qT[0:QH, 2 * hp:2 * hp + 2, :].rearrange("p a b -> p (a b)"),
                                       G.take(dve, ("qT", hp))[0:QH, :]), ("qT", hp))

            def transposed(tag, i, prT):
                h, qb = i // 2, i % 2
                b = G.take(dve, (tag, "pt", i))
                if h >= 2:
                    dve.wait_ge(done, G.number[(tag, "o", h // 2 - 1)])
                to = prT[:, h % 2, :].rearrange("p (j t) -> p j t", j=4)[:, :, qb * 128:qb * 128 + 128]
                G.give(dve.tensor_copy(to, b.rearrange("p (j t) -> p j t", j=4)), (tag, "pt", i))

            def attend(tag, heads, scale, pr, prT, oT, fill):
                def top(i):
                    b = G.take(dve, (tag, "s", i))
                    link(dve.tensor_reduce(small[:, 96 + i:97 + i], b, AX.X, ALU.max))
                    dve.tensor_scalar(small[:, 32 + i:33 + i], small[:, 96 + i:97 + i], -scale, None,
                                      ALU.mult).then_inc(sem(tag + "_max"), 1)

                top(0)
                for i in range(2 * heads):
                    if i + 1 < 2 * heads:
                        top(i + 1)
                    dve.wait_ge(sem(tag + "_exp"), i + 1)
                    r = small[:, 64 + i:65 + i]
                    G.give(dve.reciprocal(r, r), (tag, "s", i))
                    G.read(dve, (tag, "s", i))
                    dve.tensor_scalar(pr[:, i % 2, :], pr[:, i % 2, :], r, None, ALU.mult).then_inc(sem(tag + "_prob"), 1)
                    if i:
                        fill(i - 1)
                    if i >= 4 and i % 4 == 0:
                        evict((tag, "o", i // 4 - 1), oT[:, i // 4 - 1, :], T)
                    if i % 2 == 0:
                        transposed(tag, i, prT)
                fill(2 * heads - 1)
                evict((tag, "o", heads // 2 - 1), oT[:, heads // 2 - 1, :], T)

            def mla_fill(i):
                if i % 2 == 0 and i:
                    mod(4 + i // 2 - 1)
                elif i in MLA_FILL:
                    tag, tb = MLA_FILL[i]
                    if tb % 2 == 0:
                        evict((tag, tb), (gk if tag == "gk" else gv)[:, tb, :])

            attend("mla", MLA_H, QH ** -0.5, prob, probT, o_mla, mla_fill)
            dve.memset(wdec[0:33, :], 0.0).then_inc(sem("wdec_cleared"), 1)
            b = G.take(dve, ("gq", 0))
            G.give(dve.tensor_scalar(gq[:, 0, :], b, 128 ** -0.5, None, ALU.mult), ("gq", 0))
            mod(11)
            mod(12)
            b = G.take(dve, "low")
            dve.memset(low[32:33, :], 1.0)
            G.give(dve.tensor_copy(low[0:32, :], b[0:32, :]), "low")
            G.read(dve, "low")
            dve.sem_inc(sem("low_ready"), 1)

            def log_gates(half):
                dve.wait_ge(sem("gate_log"), half + 1)
                for tb in (2 * half, 2 * half + 1):
                    for d in range(2):
                        g = gg[:, tb, d * 512:d * 512 + 512]
                        G.give(dve.scalar_tensor_tensor(g, G.take(dve, ("z", tb, d)), 0.0, g, ALU.min, ALU.subtract),
                               ("z", tb, d))

            log_gates(0)
            for j in range(3):
                evict(("gr", j), grT[:, j, :], T)
            log_gates(1)
            evict(("gr", 3), grT[:, 3, :], T)
            for i in (13, 14, 15):
                mod(i)

            def state_keys(tb, d):
                g = gg[:, tb, d * 512:d * 512 + 512]
                G.read(dve, ("aft", tb, d))
                dve.tensor_tensor(g, g, gk[:, tb, :], ALU.mult).then_inc(sem("gla_keys"), 1)

            for tb in range(TB):
                for d in range(2):
                    G.read(dve, ("bc", tb, d))
                    dve.tensor_tensor(gex[:, 0, :], gex[:, 0, :], gq[:, tb, :], ALU.mult).then_inc(sem("gla_scaled"), 1)
                    dve.tensor_tensor(gex[:, 1, :], gex[:, 1, :], gk[:, tb, :], ALU.mult).then_inc(sem("gla_scaled"), 1)
                    b = G.take(dve, ("qe", tb, d))
                    to = qeT[:, d, :].rearrange("p (h t) -> p h t", h=4)[:, :, tb * 128:tb * 128 + 128]
                    G.give(dve.tensor_copy(to, b.rearrange("p (h t) -> p h t", h=4)), ("qe", tb, d))
                    state_keys(tb, d)
            for tb in range(2, 4):
                for d in range(2):
                    state_keys(tb, d)
            decay = small[:, 128:256]
            b = G.take(dve, "dec")
            G.give(dve.tensor_copy(decay, b[:, 0:128]), "dec")
            decay = decay.rearrange("p (h r) -> p h r", h=4)
            masks = cst[:, at["upto64"][0]:at["upto64"][0] + 256]
            dve.wait_ge(sem("gla_keys"), 8)
            for i in range(8):
                b = G.take(dve, ("A", i))
                if i >= 2:
                    dve.wait_ge(sem("gla_masked"), i - 1)
                G.give(dve.tensor_tensor(atM[:, i % 2, :], b[:, 0:256], masks, ALU.mult), ("A", i))
                G.read(dve, ("A", i))
                dve.tensor_tensor(atT[:, i, :], atM[:, i % 2, 0:128], atM[:, i % 2, 128:256],
                                  ALU.add).then_inc(sem("gla_masked"), 1)
            G.read(dve, "dec")
            for s in range(7):
                for d in range(2):
                    pos = (s % 4) if d == 0 else 3 - s % 4
                    row = d * 8 + (4 if s < 4 else 0) + pos
                    b = G.take(dve, ("U", s, d))
                    new, old = st[s % 2][:, d, :], st[(s - 1) % 2][:, d, :]
                    if s >= 6:
                        dve.wait_ge(done, G.number[("I", s - 1, d)])
                    if s == 0:
                        G.give(dve.tensor_copy(new, b), ("U", s, d))
                    else:
                        for h in range(4):
                            r = slice(h * 128, h * 128 + 128)
                            ins = dve.scalar_tensor_tensor(new[:, r], old[:, r], decay[:, h, row:row + 1], b[:, r],
                                                           ALU.mult, ALU.add)
                        G.give(ins, ("U", s, d))
                    G.read(dve, ("U", s, d))
                    dve.sem_inc(sem("gla_state"), 1)
            dve.wait_ge(sem("gr_gated"), 1)
            for hp in range(2):
                G.read(dve, ("gn", hp))
                r = rtg[:, hp, :]
                link(dve.reciprocal(r, r))
                o = o_gla[:, 2 * hp:2 * hp + 2, :].rearrange("p a b -> p (a b)")
                link(dve.scalar_tensor_tensor(o, acc[hp], vc("gla_norm_g"), r, ALU.mult, ALU.mult))
                dve.tensor_tensor(o, o, grT[:, 2 * hp:2 * hp + 2, :].rearrange("p a b -> p (a b)"),
                                  ALU.mult).then_inc(sem("gla_out"), 1)
            for n in range(KD):
                m = merged[:, n, :]
                G.read(dve, ("gm", n))
                G.give(dve.tensor_tensor(m, G.take(dve, ("bm", n))[:, 0:T], sig[:, 2 * (n % 2), :], ALU.mult), ("bm", n))
                G.read(dve, ("gG", n))
                G.give(dve.tensor_tensor(part[:, n % 2, :], G.take(dve, ("bg", n))[:, 0:T], sig[:, 2 * (n % 2) + 1, :],
                                         ALU.mult), ("bg", n))
                G.read(dve, ("bm", n))
                G.read(dve, ("bg", n))
                dve.tensor_tensor(m, m, part[:, n % 2, :], ALU.add).then_inc(sem("merged"), 1)
            gate = mc(0, 2)
            for n in range(KD):
                b = G.take(dve, ("wo", n))
                G.give(dve.scalar_tensor_tensor(xT[:, n, :], b[:, 0:T], gate[:, n:n + 1], xT[:, n, :], ALU.mult, ALU.add),
                       ("wo", n))
            dve.memset(pad[:, :, :], 0.0).then_inc(sem("pad_cleared"), 1)
            set_gain(2, mc(0, 4), vc("norm2_g", 0, KD))
            for n in range(KD):
                G.read(dve, ("wo", n))
            norm(2, xT, gains(2), hT[:, :, 0:T])
            for j in range(KF):
                G.read(dve, ("ug", j))
                if j >= 3:
                    dve.wait_ge(sem("ff_ready"), j - 2)
                grid = pad[:, j % 3, :].rearrange("p (r c) -> p r c", r=ROWS + 2)
                y = gel[:, j % 3, :].rearrange("p (r c) -> p r c", r=ROWS)
                for i in range(9):
                    win = grid[:, i // 3:i // 3 + ROWS, i % 3:i % 3 + GRID_W]
                    if i == 0:
                        link(dve.tensor_scalar(y, win, tap(0, j), vc("conv_b", j), ALU.mult, ALU.add))
                    else:
                        ins = dve.scalar_tensor_tensor(y, win, tap(i, j), y, ALU.mult, ALU.add)
                        if i < 8:
                            link(ins)
                ins.then_inc(sem("conv_done"), 1)
                if j == CTX_NORM:
                    set_gain(4, mc(1, 1, 1), vc("g_norm1_2", 0, KD))
                    norm(3, xc2T, gains(4), hT[:, :, T:2 * T])
                if j % 4 == 3 and j > 3:
                    mod(16 + j // 4 - 1)
            mod(20)
            mod(21)
            gate = mc(0, 5)
            for n in range(KD):
                G.take(dve, ("ff", n // 2))
                dve.scalar_tensor_tensor(xT[:, n, :], acc[n // 2][:, (n % 2) * T:(n % 2) * T + T], gate[:, n:n + 1],
                                         xT[:, n, :], ALU.mult, ALU.add).then_inc(sem("ff_added"), 1)
            dve.wait_ge(sem("ff_added"), KD)
            norm(4, xT, vc("final_g", 0, KD), xT)
            set_gain(3, mc(1, 1), vc("g_norm1_2", 0, KD))
            dve.memset(raw[:, :, :], 0.0).then_inc(sem("raw_cleared"), 1)
            dve.wait_ge(sem("scaled"), KD * 5)
            evict(("ekv", 2), e_kv[:, 2, :], 256)
            norm(5, xT, gains(3), hT[:, :, 0:T])
            dve.wait_ge(sem("heads_in"), 48)

            def input_gates(tb):
                b = G.take(dve, ("egt", tb))
                G.give(dve.tensor_tensor(m_gt[:, tb, :], b[:, 0:16], small[:, 112:128], ALU.add), ("egt", tb))

            for tb in (2, 3):
                input_gates(tb)

            def convolve(i):
                n = (i + 4) % 8
                G.read(dve, ("eq", n))
                s = 2 if n >= 4 else 1
                x = raw[:, i % 3, :].rearrange("p (s t) -> p s t", s=2)[:, 0:s]
                y = qk[:, n, 0:s * T].rearrange("p (s t) -> p s t", s=s)
                link(dve.tensor_scalar(y, x[:, :, 0:T], vc("w_conv_2", n), None, ALU.mult))
                link(dve.scalar_tensor_tensor(y, x[:, :, 1:T + 1], vc("w_conv_2", 8 + n), y, ALU.mult, ALU.add))
                dve.scalar_tensor_tensor(y, x[:, :, 2:T + 2], vc("w_conv_2", 16 + n), y, ALU.mult,
                                         ALU.add).then_inc(sem("conv2_done"), 1)

            for i in range(4):
                convolve(i)
            for tb in (0, 1):
                input_gates(tb)
            evict(("ekv", 0), e_kv[:, 0, :], 256)
            for tb in range(4):
                G.read(dve, ("egt", tb))
            dve.sem_inc(sem("m_biased"), 1)
            tmp = small[:, 128:640]

            def heads(x, n):
                return x.rearrange("p (h c) -> p h c", h=n)

            def halves(x, n):
                return x.rearrange("p (n x h q) -> p n x h q", n=n, x=2, h=2)

            def head_squares(x, n, to):
                link(dve.tensor_tensor(tmp[:, 0:n * A_D], x, x, ALU.mult))
                link(dve.tensor_reduce(to, heads(tmp[:, 0:n * A_D], n), AX.X, ALU.add))

            def head_scale(x, n, r, g):
                v = heads(x, n)
                link(dve.tensor_tensor(v, v, r.unsqueeze(2).to_broadcast([128, n, A_D]), ALU.mult))
                link(dve.tensor_tensor(v, v, g.unsqueeze(1).to_broadcast([128, n, A_D]), ALU.mult))

            for tb in range(4):
                G.read(dve, ("ekv", tb))
            for tb in range(4):
                head_squares(e_kv[:, tb, 0:128], A_KV, small[:, 8 + 2 * tb:10 + 2 * tb])
            dve.sem_inc(sem("heads_squared"), 1)
            dve.wait_ge(sem("heads_root"), 1)
            link(dve.reciprocal(small[:, 8:16], small[:, 8:16]))
            for tb in range(4):
                head_scale(e_kv[:, tb, 0:128], A_KV, small[:, 8 + 2 * tb:10 + 2 * tb], small[:, 704:768])
                if tb < TB:
                    v = halves(e_kv[:, tb, 0:128], A_KV)
                    link(rope(v, v, "rope64", tb, tmp, A_KV, 16))
            dve.sem_inc(sem("heads_ready"), 1)
            evict(("eqa", 0), e_qa[:, 0, :])
            dve.wait_ge(sem("m_log"), 1)
            f = gsm[:, 0:64].rearrange("p (x y) -> p x y", x=8)[:, :, 4:8]
            lf = gsm[:, 64:96].rearrange("p (x y) -> p x y", x=8)
            ln = gsm[:, 224:256].rearrange("p (x y) -> p x y", x=8)
            dve.scalar_tensor_tensor(lf, f, 0.0, ln, ALU.min, ALU.subtract).then_inc(sem("m_gates"), 1)

            for tb in range(TB):
                G.read(dve, ("eqa", tb))
            for tb in range(TB):
                head_squares(e_qa[:, tb, :], A_H, small[:, 16 + 8 * tb:24 + 8 * tb])
            dve.sem_inc(sem("heads_squared"), 1)
            dve.wait_ge(sem("heads_root"), 2)
            link(dve.reciprocal(small[:, 16:32], small[:, 16:32]))
            for tb in range(TB):
                head_scale(e_qa[:, tb, :], A_H, small[:, 16 + 8 * tb:24 + 8 * tb], small[:, 640:704])
                for g in range(2):
                    v = halves(e_qa[:, tb, g * 256:g * 256 + 256], 4)
                    link(rope(v, v, "rope64", tb, tmp, 4, 16))
                dve.sem_inc(sem("heads_ready"), 1)
            G.give(dve.tensor_copy(e_kT[0:A_D, 0, :], G.take(dve, ("ekT", 0))[0:A_D, :]), ("ekT", 0))
            for hp in (0, 2):
                G.give(dve.tensor_copy(e_qT[0:A_D, 2 * hp:2 * hp + 2, :].rearrange("p a b -> p (a b)"),
                                       G.take(dve, ("eqT", hp))[0:A_D, :]), ("eqT", hp))

            def gqa_fill(i):
                if i % 2 == 0:
                    if i:
                        mod(22 + i // 2 - 1)
                    if i - 1 in GQA_FILL:
                        convolve(4 + GQA_FILL[i - 1])

            attend("gqa", A_H, A_D ** -0.5, e_prob, e_probT, e_oT, gqa_fill)
            ends = v1.rearrange("p b (h c) -> p (b h) c", h=4)[:, :, 0:130:129]
            dve.memset(ends, 1.0).then_inc(sem("v1_set"), 1)

            def values(tb):
                b = G.take(dve, ("evb", tb))
                G.give(dve.tensor_copy(v1[:, tb, :].rearrange("p (h c) -> p h c", h=4)[:, :, 1:129],
                                       b.rearrange("p (h c) -> p h c", h=4)), ("evb", tb))

            def pair(v):
                return v.rearrange("p (d h) -> p d h", d=2)

            for tb in range(4):
                b = G.take(dve, ("eb", tb))
                dve.tensor_copy(m_b[:, tb, :], b[:, 0:8])
                G.give(dve.tensor_copy(m_end[:, tb, :], b[:, 8:16]), ("eb", tb))
                G.read(dve, ("eb", tb))
                i_gate = m_gt[:, tb, :].rearrange("p (d y) -> p d y", d=2)[:, :, 0:4]
                dve.tensor_tensor(pair(m_r[:, tb, :]), i_gate, pair(m_b[:, tb, :]), ALU.subtract).then_inc(sem("m_r"), 1)
            for tb in (0, 2):
                evict(("ekt", tb), ktm[:, tb, :])
            def tops(tb):
                for d in range(2):
                    b = G.take(dve, ("eR", tb, d))
                    v = b.rearrange("p (h s) -> p h s", h=4)
                    ins = dve.tensor_reduce(m_top[:, tb, d * 4:d * 4 + 4], v, AX.X, ALU.max)
                    if tb < TB:
                        bar = c_(("bar_later", "bar_earlier")[d]).unsqueeze(1).to_broadcast([128, 4, 128])
                        ins = dve.tensor_tensor(dmx[tb][:, d * 4:d * 4 + 4, :], v, bar, ALU.add)
                    G.give(ins, ("eR", tb, d))
                for d in range(2):
                    G.read(dve, ("eR", tb, d))

            def exponents(j):
                for d in range(2):
                    tb, c = BLOCKS[d][j], slice(4 * d, 4 * d + 4)
                    m, top, x = m_m[:, j, c], m_top[:, tb, c], m_x[:, 2 * j + d, :]
                    mx = top
                    if j:
                        mx = m_mx[:, c]
                        link(dve.tensor_tensor(mx, m, top, ALU.max))
                        dve.tensor_tensor(x[:, 4:8], m, mx, ALU.subtract)
                    dve.tensor_tensor(x[:, 0:4], m_r[:, tb, c], mx, ALU.subtract).then_inc(sem("m_args"), 1)
                    link(dve.tensor_tensor(m_m[:, j + 1, c], m_end[:, tb, c], mx, ALU.add))

            def keys(j):
                for d in range(2):
                    tb, x = BLOCKS[d][j], m_x[:, 2 * j + d, :]
                    dve.wait_ge(sem("m_exps"), 2 * j + d + 1)
                    if j:
                        dve.wait_ge(done, G.number[("eU", j - 1, d, 1)])
                    for h in range(4):
                        ins = dve.tensor_scalar(kw[:, d * 4 + h, :], ktm[:, tb, h * 128:h * 128 + 128], x[:, h:h + 1],
                                                128 ** -0.5, ALU.mult, ALU.mult)
                    ins.then_inc(sem("m_keys"), 1)

            def states(j):
                for d in range(2):
                    to = cn[1 - d] if j == 2 else cn[d]
                    x = m_x[:, 2 * j + d, :]
                    for hp in range(2):
                        b = G.take(dve, ("eU", j, d, hp))
                        for h in (2 * hp, 2 * hp + 1):
                            new, old = to[:, h, 129 * d:129 * d + 129], cn[d][:, h, 129 * d:129 * d + 129]
                            u = b[:, (h % 2) * 129:(h % 2) * 129 + 129]
                            if j:
                                ins = dve.scalar_tensor_tensor(new, old, x[:, 4 + h:5 + h], u, ALU.mult, ALU.add)
                            else:
                                ins = dve.tensor_copy(new, u)
                        G.give(ins, ("eU", j, d, hp))
                        G.read(dve, ("eU", j, d, hp))
                        dve.sem_inc(sem("m_state"), 1)

            for tb in (2, 3, 1):
                tops(tb)
            G.read(dve, ("ekt", 1))
            G.read(dve, ("ekt", 3))
            exponents(0)
            keys(0)
            values(2)
            exponents(1)
            keys(1)
            states(0)
            link(dve.tensor_reduce(m_M, dmx[1], AX.X, ALU.max))
            values(0)
            states(1)
            tops(0)
            exponents(2)
            keys(2)
            mod(29)
            states(2)
            mod(30)
            dve.wait_ge(sem("out_gates"), 1)
            for tb in (1, 0):
                n = 2 - tb
                ms = [m_m[:, 2 + tb, 0:4], m_m[:, 3 - tb, 4:8]]
                if tb == 0:
                    link(dve.tensor_reduce(m_M, dmx[tb], AX.X, ALU.max))
                for d in range(2):
                    c = slice(4 * d, 4 * d + 4)
                    link(dve.tensor_tensor(m_M[:, c], m_M[:, c], ms[d], ALU.max))
                    dve.tensor_tensor(m_in[:, c], ms[d], m_M[:, c], ALU.subtract)
                link(dve.tensor_tensor(m_em, m_b[:, tb, :], m_M, ALU.add))
                link(dve.tensor_scalar(m_em, m_em, -1.0, None, ALU.mult))
                dve.tensor_tensor(dmx[tb], dmx[tb], m_M.unsqueeze(2).to_broadcast([128, 8, 128]),
                                  ALU.subtract).then_inc(sem("m_shifted"), 1)
                for h in range(4):
                    b = G.take(dve, ("eC", tb, h))
                    link(dve.tensor_copy(pair(m_nq)[:, :, h], b[:, 128:130]))
                mod(31 if tb else 33)
                dve.wait_ge(sem("m_wexp"), n)
                b = G.take(dve, ("eS", tb))
                for d in range(2):
                    v = wm[:, 4 * d:4 * d + 4, :].rearrange("p a b -> p (a b)")
                    ins = dve.scalar_tensor_tensor(v, b, 128 ** -0.5, v, ALU.mult, ALU.mult)
                G.give(ins, ("eS", tb))
                G.read(dve, ("eS", tb))
                link(dve.tensor_reduce(m_sum, wm[:, :, :], AX.X, ALU.add))
                link(dve.tensor_tensor(m_nq, m_nq, m_in, ALU.mult))
                link(dve.tensor_tensor(m_den, m_nq, m_sum, ALU.add))
                link(dve.scalar_tensor_tensor(m_den, m_den, -1.0, m_den, ALU.mult, ALU.max))
                link(dve.tensor_tensor(m_den, m_den, m_em, ALU.max))
                link(dve.reciprocal(m_den, m_den))
                dve.tensor_tensor(m_wr, m_in, m_den, ALU.mult)
                link(dve.tensor_tensor(wm[:, :, :], wm[:, :, :], m_den.unsqueeze(2).to_broadcast([128, 8, 128]), ALU.mult))
                link(dve.tensor_tensor(wm[:, 0:4, :], wm[:, 0:4, :], wm[:, 4:8, :], ALU.add))
                dve.sem_inc(sem("m_weights"), 1)
                if tb:
                    mod(32)
                for d in range(2):
                    for h in range(4):
                        b = G.take(dve, ("eC", tb, h))
                        q, r = b[:, 130 * d:130 * d + 128], m_wr[:, 4 * d + h:4 * d + h + 1]
                        if d == 0:
                            ins = dve.tensor_scalar(h_e[:, h, :], q, r, None, ALU.mult)
                            if h == 3:
                                link(ins)
                        else:
                            G.give(dve.scalar_tensor_tensor(h_e[:, h, :], q, r, h_e[:, h, :], ALU.mult, ALU.add),
                                   ("eC", tb, h))
                for h in range(4):
                    G.read(dve, ("eC", tb, h))
                b = G.take(dve, ("eH", tb))
                v = h_e[:, :, :].rearrange("p a b -> p (a b)")
                G.give(dve.tensor_tensor(v, b, v, ALU.add), ("eH", tb))
                G.read(dve, ("eH", tb))
                sqv = wm[:, 4:8, :]
                link(dve.tensor_tensor(sqv, h_e[:, :, :], h_e[:, :, :], ALU.mult))
                dve.tensor_reduce(m_ss[:, 0:4], sqv, AX.X, ALU.add).then_inc(sem("m_hsq"), 1)
                if tb == 0:
                    mod(34)
                dve.wait_ge(sem("m_hroot"), n)
                link(dve.reciprocal(m_ss[:, 0:4], m_ss[:, 0:4]))
                dve.tensor_tensor(h_e[:, :, :], h_e[:, :, :], m_ss[:, 0:4].unsqueeze(2).to_broadcast([128, 4, 128]),
                                  ALU.mult).then_inc(sem("m_out"), 1)
                b = G.take(dve, ("eT", tb))
                for h in range(4):
                    ins = dve.scalar_tensor_tensor(e_mT[:, h, tb * 128:tb * 128 + 128], b[:, h * 128:h * 128 + 128],
                                                   vc("g_hnorm_2", h), e_ob[:, h, tb * 128:tb * 128 + 128], ALU.mult, ALU.mult)
                G.give(ins, ("eT", tb))
                G.read(dve, ("eT", tb))
            mod(35)

            def add_output(tag, gate):
                for n in range(KD):
                    b = G.take(dve, (tag, n))
                    G.give(dve.scalar_tensor_tensor(xT[:, n, :], b[:, 0:T], gate[:, n:n + 1], xT[:, n, :], ALU.mult,
                                                    ALU.add), (tag, n))
                for n in range(KD):
                    G.read(dve, (tag, n))

            add_output("eo", mc(1, 2))

            def output():
                for j in (0, 2):
                    evict(("out", j), x_tm[:, j // 2, 0:512])

            def experts(layer, c):
                set_gain(c - 1 - layer, mc(1 + layer, 4), vc("g_norm2_2", KD * layer, KD))
                norm(c, xT, gains(c - 1 - layer), hT[:, :, 0:T])
                for tb in range(TB):
                    b = G.take(dve, ("lg", layer, tb))
                    dve.tensor_reduce(small[:, 32 + tb:33 + tb], b[:, 0:N_EXP], AX.X, ALU.max,
                                      negate=True).then_inc(sem("router_max"), 1)
                for tb in range(TB):
                    dve.wait_ge(sem("router_exp"), 2 * layer + tb + 1)
                    r = small[:, 64 + tb:65 + tb]
                    G.give(dve.reciprocal(r, r), ("lg", layer, tb))
                    G.read(dve, ("lg", layer, tb))
                    link(dve.tensor_scalar(aff[:, tb, :], aff[:, tb, :], r, None, ALU.mult))
                    dve.sem_inc(sem("affinity"), 1)
                wk = work[0:N_EXP, :]
                b = G.take(dve, ("aT", layer))
                G.give(dve.tensor_copy(wk, b[0:N_EXP, 0:T]), ("aT", layer))
                G.read(dve, ("aT", layer))
                for _ in range(CAP // 8):
                    link(dve.max(top8, wk))
                    link(dve.match_replace(wk, top8, wk, -1.0))
                dve.tensor_scalar(mask_e[0:N_EXP, :], wk, 0.0, None, ALU.is_lt).then_inc(sem("chosen"), 1)
                b = G.take(dve, ("mT", layer))
                G.give(dve.tensor_copy(mask_t.rearrange("p b e -> p (b e)"), b[:, 0:32]), ("mT", layer))
                G.read(dve, ("mT", layer))
                b = G.take(dve, ("cs", layer))
                v = turn_of.rearrange("p b e -> p (b e)")
                G.give(dve.tensor_tensor(v, b[:, 0:32], mask_t.rearrange("p b e -> p (b e)"), ALU.mult), ("cs", layer))
                G.read(dve, ("cs", layer))
                link(dve.tensor_scalar(v, v, -1.0, None, ALU.add))
                hots = [hot[:, tb, :].rearrange("p (e c) -> p e c", e=N_EXP) for tb in range(TB)]
                for lo, hi in ((0, 1), (1, N_EXP)):
                    for tb in range(TB):
                        ins = dve.tensor_tensor(hots[tb][:, lo:hi],
                                                c_("slot_numbers").unsqueeze(1).to_broadcast([128, hi - lo, CAP]),
                                                turn_of[:, tb, lo:hi].unsqueeze(2).to_broadcast([128, hi - lo, CAP]),
                                                ALU.is_equal)
                    link(ins)
                    dve.sem_inc(sem("one_hot"), 1)
                dve.wait_ge(sem("rows_selected"), N_EXP * layer + 1)
                v = bank[0].rearrange("p (m a b c) -> p a m b c", m=4, a=2, b=2)
                to = xe.rearrange("p (a m c) -> p a m c", a=2, m=4)
                link(dve.tensor_copy(to, v[:, :, :, 0]))
                dve.tensor_tensor(to, to, v[:, :, :, 1], ALU.add).then_inc(sem("rows_ready"), 1)
                for tb in range(TB):
                    ins = dve.tensor_tensor(hotg[:, tb, :].rearrange("p (e q c) -> p e q c", e=N_EXP, q=4),
                                            hots[tb].unsqueeze(2).to_broadcast([128, N_EXP, 4, CAP]),
                                            aff[:, tb, :].unsqueeze(2).unsqueeze(3).to_broadcast([128, N_EXP, 4, CAP]),
                                            ALU.mult)
                ins.then_inc(sem("gated_hot"), 1)
                for e2 in range(0, N_EXP // 2, 2):
                    evict(("gT", layer, e2), gates_flat[:, e2 * 512:e2 * 512 + 512])
                base = moe_base[layer]
                with dve.Fori(0, N_EXP) as e:
                    dve.wait_ge(sem("silu_ready"), e + (N_EXP * layer + 1))
                    t = bank[1].rearrange("p (j c) -> p j c", j=4)
                    to = act_t.rearrange("p (h j) c -> p j h c", h=2)
                    dve.tensor_tensor(to, sil.rearrange("p (j h) c -> p j h c", h=2),
                                      t[:, :, 64:128].rearrange("p j (h c) -> p j h c", h=2),
                                      ALU.mult).then_inc(sem("act_ready"), 1)
                    dve.wait_ge(done, e * 3 + (base + 2))
                    dve.tensor_copy(dsb[:, 0, :], bank[2]).then_inc(sem("down_copied"), 1)
                gate = mc(1 + layer, 5)
                for n in range(KD):
                    dve.wait_ge(done, base + 3 * (N_EXP - 1) + 3 + n // 2)
                    dve.scalar_tensor_tensor(xT[:, n, :], acc[n // 2][:, (n % 2) * T:(n % 2) * T + T], gate[:, n:n + 1],
                                             xT[:, n, :], ALU.mult, ALU.add).then_inc(sem("moe_added"), 1)
                dve.wait_ge(sem("moe_added"), KD * (layer + 1))

            experts(0, 6)
            set_gain(6, mc(2, 1), vc("g_norm1_2", KD, KD))
            link(dve.tensor_tensor(gains(0), mc(2, 2), vc("s_pool_2", 0, KD), ALU.mult))
            norm(7, xT, gains(6), hT[:, :, 0:T])
            for tb in range(TB):
                evict(("u", tb, 0), u_tm[:, tb, 0:512])
            for c in range(0, KD, 2):
                evict(("p", c), pT[:, c, :], T)
            add_output("y", gains(0))
            experts(1, 8)
            norm(9, xT, vc("g_final_2", 0, KD), xT)
            output()

        @block.gpsimd
        def _(pool):
            for j in range(KF):
                pool.wait_ge(sem("gelu_done"), j + 1)
                nc.gpsimd.tensor_tensor(ff[:, j, :], ff[:, j, :], gel[:, j % 3, :], ALU.mult).then_inc(sem("ff_ready"), 1)


NAMES = [
    "x", "ctx", "w_ada", "w_in", "w_uq", "w_ukv", "gla_w_decay", "gla_b_decay", "w_br_mla", "w_br_gla", "w_out",
    "w_up", "w_down", "ctx_2", "w_mod_2", "w_in_even_2", "w_out_even_2", "g_qnorm_2", "g_knorm_2", "b_gate_2",
    "w_in_odd_2", "w_pool_grp_2", "w_router_2", "w_exp_gate_2", "w_exp_up_2", "w_exp_down_2",
]


def kernel(**inputs):
    import numpy as _np
    import concourse.bacc as _bacc
    from concourse.bass_utils import run_bass_kernel_spmd as _run

    nc = _bacc.Bacc("TRN2", target_bir_lowering=False, num_devices=1)
    arrays, w = {}, {}
    table, at = shape_tables()
    rows, vat, tiles = vector_rows(inputs)
    laid_out = [("tables", table), ("pool", pool_table()), ("vectors", rows)]
    for name, a in [(n, inputs[n]) for n in NAMES] + laid_out:
        a = _np.ascontiguousarray(a)
        arrays[f"in_{name}_dram"] = a
        w[name] = nc.dram_tensor(f"in_{name}_dram", a.shape, mybir.dt.from_np(a.dtype), kind="ExternalInput").ap()
    out = nc.dram_tensor("out_0_dram", (1, T, D), F32, kind="ExternalOutput").ap()
    build(nc, w, (table, at, vat, tiles), out)
    r = _run(nc, [arrays], core_ids=[0])
    return r.results[0]["out_0_dram"]
```
